# Optimizing a Trainium2 kernel written in Bass

```python
import math
import jax, jax.numpy as jnp
from jax import lax
import numpy as np

D_MODEL = 1024
BATCH = 1
SEQ = 256
DEPTH = 1

NSA_HEADS = 8
NSA_KV_HEADS = 2
NSA_HEAD_DIM = 64
CMP_BLOCK = 32
CMP_STRIDE = 16
CMP_HIDDEN = 256
SEL_BLOCK = 64
SEL_TOPK = 8
WINDOW = 512
Q_BLOCK = 64
FORCE_BONUS = 1e4
GLA_HEADS = 4
GLA_KEY_DIM = 64
GLA_VAL_DIM = 128
GLA_CHUNK = 64
GLA_GATE_RANK = 16
GLA_TAU = 16.0
ROPE_THETA = 500000.0
ROPE_DIM = NSA_HEAD_DIM // 4
N_EXPERTS = 32
TOP_K = 4
D_FF = 1024
SWIGLU_LIMIT = 7.0
SWIGLU_ALPHA = 1.702
EXPERT_BLOCK = 256
EPS = 1e-6
NEG_INF = -1e30

NSA_WIDTH = NSA_HEADS * NSA_HEAD_DIM
NSA_KV_WIDTH = NSA_KV_HEADS * NSA_HEAD_DIM
GLA_KEY_WIDTH = GLA_HEADS * GLA_KEY_DIM
GLA_WIDTH = GLA_HEADS * GLA_VAL_DIM
IN_SIZES = (NSA_WIDTH, NSA_KV_WIDTH, NSA_KV_WIDTH, NSA_KV_WIDTH, NSA_KV_WIDTH, NSA_KV_WIDTH, NSA_KV_WIDTH,
            NSA_HEADS * 3, GLA_KEY_WIDTH, GLA_KEY_WIDTH, GLA_WIDTH, GLA_GATE_RANK, GLA_WIDTH)
IN_WIDTH = sum(IN_SIZES)

kernel_name = 'hybrid_nsa_gla_moe_block'

def rms_norm(t, g):
    tf = t.astype(jnp.float32)
    y = tf * lax.rsqrt(jnp.mean(tf * tf, axis=-1, keepdims=True) + EPS) * g.astype(jnp.float32)
    return y.astype(t.dtype)

def masked_softmax(s, mask):
    s = jnp.where(mask, s.astype(jnp.float32), NEG_INF)
    m = jnp.max(s, axis=-1, keepdims=True)
    p = jnp.exp(s - m) * mask
    den = jnp.sum(p, axis=-1, keepdims=True)
    return p / jnp.where(den > 0, den, 1.0)

def apply_partial_rope(t, positions):
    half = ROPE_DIM // 2
    inv_freq = jnp.exp(-math.log(ROPE_THETA) * jnp.arange(0, ROPE_DIM, 2, dtype=jnp.float32) / ROPE_DIM)
    ang = positions.astype(jnp.float32)[..., None] * inv_freq
    cos = jnp.cos(ang)[:, :, None, :]
    sin = jnp.sin(ang)[:, :, None, :]
    tf = t.astype(jnp.float32)
    x1 = tf[..., :half]
    x2 = tf[..., half:ROPE_DIM]
    out = jnp.concatenate([x1 * cos - x2 * sin, x2 * cos + x1 * sin, tf[..., ROPE_DIM:]], axis=-1)
    return out.astype(t.dtype)

def compress_blocks(t, pos_emb, w1, w2):
    B, S, Hk, dh = t.shape
    n_cmp = (S - CMP_BLOCK) // CMP_STRIDE + 1
    blk_idx = jnp.arange(n_cmp)[:, None] * CMP_STRIDE + jnp.arange(CMP_BLOCK)[None, :]
    tb = t[:, blk_idx] + pos_emb[None, None, :, None, :]
    tb = tb.transpose(0, 1, 3, 2, 4).reshape(B, n_cmp, Hk, CMP_BLOCK * dh)
    return jax.nn.silu(tb @ w1) @ w2

def nsa_mixer(q, k_c, v_c, k_s, v_s, k_w, v_w, gate_logits, positions, q_norm_g, k_norm_g,
              cmp_pos_k, cmp_w1_k, cmp_w2_k, cmp_pos_v, cmp_w1_v, cmp_w2_v):
    B, S = q.shape[0], q.shape[1]
    Hk = NSA_KV_HEADS
    G = NSA_HEADS // Hk
    dh = NSA_HEAD_DIM
    scale = dh ** -0.5
    kv = lambda t: t.reshape(B, S, Hk, dh)
    q = rms_norm(q.reshape(B, S, NSA_HEADS, dh), q_norm_g)
    q_rot = apply_partial_rope(q, positions)
    qg = q.reshape(B, S, Hk, G, dh)
    t_idx = jnp.arange(S)

    kc = rms_norm(compress_blocks(kv(k_c), cmp_pos_k, cmp_w1_k, cmp_w2_k), k_norm_g[0])
    vc = compress_blocks(kv(v_c), cmp_pos_v, cmp_w1_v, cmp_w2_v)
    n_cmp = kc.shape[1]
    cmp_start = jnp.arange(n_cmp) * CMP_STRIDE
    mask_c = (cmp_start + CMP_BLOCK - 1)[None, :] <= t_idx[:, None]
    s_c = jnp.einsum('bskgd,bnkd->bkgsn', qg, kc) * scale
    p_c = masked_softmax(s_c, mask_c)
    o_cmp = jnp.einsum('bkgsn,bnkd->bskgd', p_c.astype(vc.dtype), vc)

    n_sel = S // SEL_BLOCK
    k_sel = min(SEL_TOPK, n_sel)
    j = jnp.arange(n_sel)
    overlap = ((cmp_start[None, :] < (j[:, None] + 1) * SEL_BLOCK) &
               (cmp_start[None, :] + CMP_BLOCK > j[:, None] * SEL_BLOCK)).astype(jnp.float32)
    imp = jnp.einsum('bkgsn,jn->bksj', p_c, overlap)
    cur = t_idx // SEL_BLOCK
    valid = j[None, :] <= cur[:, None]
    forced = (j[None, :] == 0) | (j[None, :] == cur[:, None]) | (j[None, :] == cur[:, None] - 1)
    score = jnp.where(valid, imp + jnp.where(forced, FORCE_BONUS, 0.0), NEG_INF)
    _, sel_idx = lax.top_k(score, k_sel)

    ks = apply_partial_rope(rms_norm(kv(k_s), k_norm_g[1]), positions)
    ks_blocks = ks.reshape(B, n_sel, SEL_BLOCK, Hk, dh).transpose(0, 3, 1, 2, 4)
    vs_blocks = kv(v_s).reshape(B, n_sel, SEL_BLOCK, Hk, dh).transpose(0, 3, 1, 2, 4)
    kw = apply_partial_rope(rms_norm(kv(k_w), k_norm_g[2]), positions).transpose(0, 2, 1, 3)
    vw = kv(v_w).transpose(0, 2, 1, 3)
    pad = ((0, 0), (0, 0), (WINDOW, 0), (0, 0))
    kw_pad = jnp.pad(kw, pad)
    vw_pad = jnp.pad(vw, pad)

    n_qb = S // Q_BLOCK
    q_blocks = q_rot.reshape(B, n_qb, Q_BLOCK, Hk, G, dh).swapaxes(0, 1)
    idx_blocks = sel_idx.reshape(B, Hk, n_qb, Q_BLOCK, k_sel).transpose(2, 0, 1, 3, 4)
    b_ix = jnp.arange(B)[:, None, None, None]
    h_ix = jnp.arange(Hk)[None, :, None, None]

    def block_attn(args):
        c, qb, ib = args
        tq = c * Q_BLOCK + jnp.arange(Q_BLOCK)
        kg = ks_blocks[b_ix, h_ix, ib]
        vg = vs_blocks[b_ix, h_ix, ib]
        s = jnp.einsum('bqkgd,bkqnld->bkgqnl', qb, kg) * scale
        kpos = ib[..., None] * SEL_BLOCK + jnp.arange(SEL_BLOCK)
        m = (kpos <= tq[None, None, :, None, None])[:, :, None]
        shp = s.shape
        p = masked_softmax(s.reshape(shp[:4] + (k_sel * SEL_BLOCK,)),
                           m.reshape(B, Hk, 1, Q_BLOCK, k_sel * SEL_BLOCK)).reshape(shp)
        o_sel = jnp.einsum('bkgqnl,bkqnld->bqkgd', p.astype(vg.dtype), vg)
        kwin = lax.dynamic_slice_in_dim(kw_pad, c * Q_BLOCK, Q_BLOCK + WINDOW, axis=2)
        vwin = lax.dynamic_slice_in_dim(vw_pad, c * Q_BLOCK, Q_BLOCK + WINDOW, axis=2)
        jpos = c * Q_BLOCK - WINDOW + jnp.arange(Q_BLOCK + WINDOW)
        mw = (jpos[None, :] <= tq[:, None]) & (jpos[None, :] > tq[:, None] - WINDOW) & (jpos[None, :] >= 0)
        s_w = jnp.einsum('bqkgd,bkjd->bkgqj', qb, kwin) * scale
        p_w = masked_softmax(s_w, mw)
        o_win = jnp.einsum('bkgqj,bkjd->bqkgd', p_w.astype(vwin.dtype), vwin)
        return o_sel, o_win

    o_sel, o_win = lax.map(block_attn, (jnp.arange(n_qb), q_blocks, idx_blocks))
    o_sel = o_sel.swapaxes(0, 1).reshape(B, S, Hk, G, dh)
    o_win = o_win.swapaxes(0, 1).reshape(B, S, Hk, G, dh)

    gates = jax.nn.sigmoid(gate_logits.astype(jnp.float32)).reshape(B, S, Hk, G, 3).astype(o_cmp.dtype)
    o = gates[..., 0:1] * o_cmp + gates[..., 1:2] * o_sel + gates[..., 2:3] * o_win
    return o.reshape(B, S, NSA_WIDTH)

def gla_mixer(q, k, v, gate_lr, r, w_gate, b_gate, norm_g):
    B, S = q.shape[0], q.shape[1]
    H, dk, dv, C = GLA_HEADS, GLA_KEY_DIM, GLA_VAL_DIM, GLA_CHUNK
    n_ch = S // C
    f32 = jnp.float32
    log_a = jax.nn.log_sigmoid((gate_lr @ w_gate + b_gate).astype(f32)) / GLA_TAU

    def to_chunks(t, d):
        return t.astype(f32).reshape(B, n_ch, C, H, d).transpose(0, 3, 1, 2, 4)

    qf = to_chunks(q, dk) * (dk ** -0.5)
    kf = to_chunks(k, dk)
    vf = to_chunks(v, dv)
    b = jnp.cumsum(to_chunks(log_a, dk), axis=3)
    b_last = b[:, :, :, -1:, :]
    q_dec = qf * jnp.exp(b)
    k_dec = kf * jnp.exp(-b)
    k_state = kf * jnp.exp(b_last - b)
    causal = jnp.tril(jnp.ones((C, C), dtype=bool))
    attn = jnp.where(causal, jnp.einsum('bhncd,bhnsd->bhncs', q_dec, k_dec), 0.0)
    o_intra = jnp.einsum('bhncs,bhnse->bhnce', attn, vf)
    u = jnp.einsum('bhnsd,bhnse->bhnde', k_state, vf)
    decay = jnp.exp(b_last[:, :, :, 0, :])

    def step(state, inp):
        d, u_n = inp
        return d[..., None] * state + u_n, state

    _, s_prev = lax.scan(step, jnp.zeros((B, H, dk, dv), f32),
                         (decay.transpose(2, 0, 1, 3), u.transpose(2, 0, 1, 3, 4)))
    s_prev = s_prev.transpose(1, 2, 0, 3, 4)
    o_inter = jnp.einsum('bhncd,bhnde->bhnce', q_dec, s_prev)
    o = (o_intra + o_inter).transpose(0, 2, 3, 1, 4).reshape(B, S, H, dv)
    o = rms_norm(o, norm_g).reshape(B, S, GLA_WIDTH)
    return (o * jax.nn.silu(r.astype(f32))).astype(q.dtype)

def clamped_swiglu(h):
    x_glu = jnp.minimum(h[..., :D_FF], SWIGLU_LIMIT)
    x_lin = jnp.clip(h[..., D_FF:], -SWIGLU_LIMIT, SWIGLU_LIMIT)
    return x_glu * jax.nn.sigmoid(SWIGLU_ALPHA * x_glu) * (x_lin + 1.0)

def moe_ffn(h, w_router, b_router, w_gate_up, b_gate_up, w_down, b_down):
    B, S, D = h.shape
    xf = h.reshape(-1, D)
    M = xf.shape[0]
    logits = (xf @ w_router + b_router).astype(jnp.float32)
    top_vals, top_idx = lax.top_k(logits, TOP_K)
    gate = jax.nn.softmax(top_vals, axis=-1)
    A = M * TOP_K
    flat_e = top_idx.reshape(-1)
    flat_tok = jnp.arange(A, dtype=jnp.int32) // TOP_K
    order = jnp.argsort(flat_e)
    sorted_e = flat_e[order]
    sorted_tok = flat_tok[order]
    counts = jnp.zeros((N_EXPERTS,), jnp.int32).at[flat_e].add(1)
    padded = (counts + EXPERT_BLOCK - 1) // EXPERT_BLOCK * EXPERT_BLOCK
    start = jnp.cumsum(counts) - counts
    pend = jnp.cumsum(padded)
    pstart = pend - padded
    dest = pstart[sorted_e] + (jnp.arange(A, dtype=jnp.int32) - start[sorted_e])
    n_blocks = -(-(A + N_EXPERTS * (EXPERT_BLOCK - 1)) // EXPERT_BLOCK)
    R = n_blocks * EXPERT_BLOCK
    xs = jnp.zeros((R, D), xf.dtype).at[dest].set(xf[sorted_tok])
    block_e = jnp.minimum(jnp.searchsorted(pend, jnp.arange(n_blocks) * EXPERT_BLOCK, side='right'),
                          N_EXPERTS - 1)

    def expert_block(args):
        xb, e = args
        hgu = xb @ w_gate_up[e] + b_gate_up[e]
        return clamped_swiglu(hgu) @ w_down[e] + b_down[e]

    ys = lax.map(expert_block, (xs.reshape(n_blocks, EXPERT_BLOCK, D), block_e)).reshape(R, D)
    y_sorted = ys[dest] * gate.reshape(-1)[order][:, None].astype(ys.dtype)
    out = jax.ops.segment_sum(y_sorted, sorted_tok, num_segments=M)
    return out.reshape(B, S, D)

def setup_inputs(seed: int = 0) -> dict:
    key = jax.random.key(seed)
    ks = jax.random.split(key, 24)
    f32 = jnp.float32
    L = DEPTH
    dh = NSA_HEAD_DIM

    def nrm(k, shape, scale):
        return jax.random.normal(k, shape, f32) * scale

    x = nrm(ks[0], (BATCH, SEQ, D_MODEL), 1.0)
    offsets = jax.random.randint(ks[1], (BATCH, 1), 0, 1024, dtype=jnp.int32)
    positions = offsets + jnp.arange(SEQ, dtype=jnp.int32)[None, :]
    return {
        'x': x,
        'positions': positions,
        'norm1_g': 1.0 + nrm(ks[2], (L, D_MODEL), 0.02),
        'w_in': nrm(ks[3], (L, D_MODEL, IN_WIDTH), D_MODEL ** -0.5),
        'nsa_q_norm_g': 1.0 + nrm(ks[4], (L, dh), 0.02),
        'nsa_k_norm_g': 1.0 + nrm(ks[5], (L, 3, dh), 0.02),
        'cmp_pos_k': nrm(ks[6], (L, CMP_BLOCK, dh), 0.02),
        'cmp_w1_k': nrm(ks[7], (L, CMP_BLOCK * dh, CMP_HIDDEN), (CMP_BLOCK * dh) ** -0.5),
        'cmp_w2_k': nrm(ks[8], (L, CMP_HIDDEN, dh), CMP_HIDDEN ** -0.5),
        'cmp_pos_v': nrm(ks[9], (L, CMP_BLOCK, dh), 0.02),
        'cmp_w1_v': nrm(ks[10], (L, CMP_BLOCK * dh, CMP_HIDDEN), (CMP_BLOCK * dh) ** -0.5),
        'cmp_w2_v': nrm(ks[11], (L, CMP_HIDDEN, dh), CMP_HIDDEN ** -0.5),
        'gla_w_gate': nrm(ks[12], (L, GLA_GATE_RANK, GLA_KEY_WIDTH), GLA_GATE_RANK ** -0.5),
        'gla_b_gate': nrm(ks[13], (L, GLA_KEY_WIDTH), 0.1),
        'gla_norm_g': 1.0 + nrm(ks[14], (L, GLA_VAL_DIM), 0.02),
        'w_out': nrm(ks[15], (L, NSA_WIDTH + GLA_WIDTH, D_MODEL), (NSA_WIDTH + GLA_WIDTH) ** -0.5),
        'norm2_g': 1.0 + nrm(ks[16], (L, D_MODEL), 0.02),
        'w_router': nrm(ks[17], (L, D_MODEL, N_EXPERTS), D_MODEL ** -0.5),
        'b_router': nrm(ks[18], (L, N_EXPERTS), 0.01),
        'w_gate_up': nrm(ks[19], (L, N_EXPERTS, D_MODEL, 2 * D_FF), D_MODEL ** -0.5),
        'b_gate_up': nrm(ks[20], (L, N_EXPERTS, 2 * D_FF), 0.01),
        'w_down': nrm(ks[21], (L, N_EXPERTS, D_FF, D_MODEL), D_FF ** -0.5),
        'b_down': nrm(ks[22], (L, N_EXPERTS, D_MODEL), 0.01),
    }

def reference(x, positions, norm1_g, w_in, nsa_q_norm_g, nsa_k_norm_g, cmp_pos_k, cmp_w1_k, cmp_w2_k,
              cmp_pos_v, cmp_w1_v, cmp_w2_v, gla_w_gate, gla_b_gate, gla_norm_g, w_out, norm2_g,
              w_router, b_router, w_gate_up, b_gate_up, w_down, b_down):
    split_points = [int(p) for p in np.cumsum(IN_SIZES)[:-1]]
    for l in range(DEPTH):
        h = rms_norm(x, norm1_g[l])
        proj = h @ w_in[l]
        (nq, nkc, nvc, nks, nvs, nkw, nvw, ngate, gq, gk, gv, glr, gr) = jnp.split(proj, split_points, axis=-1)
        nsa_out = nsa_mixer(nq, nkc, nvc, nks, nvs, nkw, nvw, ngate, positions, nsa_q_norm_g[l], nsa_k_norm_g[l],
                            cmp_pos_k[l], cmp_w1_k[l], cmp_w2_k[l], cmp_pos_v[l], cmp_w1_v[l], cmp_w2_v[l])
        gla_out = gla_mixer(gq, gk, gv, glr, gr, gla_w_gate[l], gla_b_gate[l], gla_norm_g[l])
        x = x + jnp.concatenate([nsa_out, gla_out], axis=-1) @ w_out[l]
        h2 = rms_norm(x, norm2_g[l])
        x = x + moe_ffn(h2, w_router[l], b_router[l], w_gate_up[l], b_gate_up[l], w_down[l], b_down[l])
    return x


_drawn_inputs = setup_inputs


def setup_inputs(seed=0):
    import zlib

    import numpy as np

    out = dict(_drawn_inputs(seed))
    spreads = {}
    factors = {'nsa_q_norm_g': 4.544,
     'nsa_k_norm_g': 4.645,
     'cmp_pos_k': 8.0,
     'gla_norm_g': 2.667,
     'b_gate_up': 8.0,
     'b_down': 8.0,
     'cmp_pos_v': 3.745}
    for name, (base, spread) in spreads.items():
        noise = np.random.default_rng([zlib.crc32(name.encode()), seed]).standard_normal(out[name].shape)
        drawn = base * np.exp(spread * noise) if base else spread * noise
        out[name] = __import__('jax').numpy.asarray(drawn.astype(out[name].dtype))
    for name, factor in factors.items():
        out[name] = (out[name] * factor).astype(out[name].dtype)
    return out
```

```python
import math
import numpy as np
import concourse.bass as bass
from concourse import mybir
from contextlib import ExitStack

F32 = mybir.dt.float32
F32R = mybir.dt.float32r
I32 = mybir.dt.int32
ALU = mybir.AluOpType
ACT = mybir.ActivationFunctionType
AX = mybir.AxisListType

P = 128
S, D = 256, 1024
NT = S // P
DK = D // P
DH = 64
HKV, G = 2, 4
HQ = HKV * G
NCMP, CST, CBL = 15, 16, 32
HID = 256
HKO = 32
NCW = HKO + NCMP
GH, DV, CH = 4, 128, 64
GTAU = 16.0
E, TOPK, FF = 32, 4, 1024
CAP = 64
ROUNDS = S // CAP
EPS = 1e-6
NEG = -1e30
SCALE = DH ** -0.5
THETA, RD = 500000.0, 16
LIMIT, ALPHA = 7.0, 1.702

IN_PIECES = [(0, 512), (512, 1024), (1024, 1304), (1304, 1816), (1816, 2328), (2328, 2856)]
NF = len(IN_PIECES) + 4
NSLOT = 6
SLOTW = [max([512] + [b - a for a, b in IN_PIECES[i::NSLOT]]) * DK for i in range(NSLOT)]
PIECES = 6
UP_COLS = [0, FF, 512, FF + 512]
NAT = 2
PAIRS = (DK - NAT) // 2
RING = 6
PROJ = [("q", 0, 512), ("kv", 512, 512), ("w", 1024, 280), ("gqk", 1304, 512), ("gv", 1816, 512),
        ("glr", 2328, 16), ("gr", 2344, 512)]
GROUPS = [(br, ti, h) for br in range(2) for ti in range(NT) for h in range(HKV)]
SC_BANKS = [(3, 4), (5, 6)]
WO_BANKS = (7, 0, 1, 2)
O_BANKS = [(3, 4), (6, 7)]
N_SMALL = 14
N_CONST = 20
FILLER = -3e38
MAGIC = 12582912.0
TWO_PI = (6.28125, 0.0019340515136718750, 2 * math.pi - 6.28125 - 0.0019340515136718750)
PI32 = 3.1415925


def decoder_layer(nc, x, positions, norm1_g, w_in, nsa_q_norm_g, nsa_k_norm_g, cmp_pos_k, cmp_w1_k, cmp_w2_k,
                  cmp_pos_v, cmp_w1_v, cmp_w2_v, gla_w_gate, gla_b_gate, gla_norm_g, w_out, norm2_g,
                  w_router, b_router, w_gate_up, b_gate_up, w_down, b_down, out):
    ctx = ExitStack()
    with ctx:
        place = [(nc.sbuf_base + 31) // 32 * 32]

        def at(name, shape, dt, offset):
            return nc.alloc_sbuf_tensor_at(name, shape, dt, offset=offset)

        def sb(name, shape, dt=F32):
            words = int(np.prod(shape[1:]))
            t = at(name, shape, dt, place[0])
            place[0] += (words * 4 + 31) // 32 * 32
            return t

        stage = [sb(f"stage{i}", [P, SLOTW[i]]) for i in range(NSLOT)]
        ident = sb("ident", [P, P])
        ones = sb("ones", [P, P])
        stack_i = sb("stack_i", [P, CAP])
        iota_i = sb("iota_i", [P, CAP], I32)
        iota_f = sb("iota_f", [P, CAP])
        posm = sb("posm", [P, NT, ROUNDS * E + 2])
        gates4 = sb("gates4", [P, NT, ROUNDS * E + 2])
        bias_t = sb("bias_t", [P, 2 * FF // P, E])
        rounds_f = sb("rounds_f", [P, 4])
        rounds_i = sb("rounds_i", [P, 1], I32)
        token = sb("token", [P, 3])
        shared = place[0]

        wh = sb("wh", [P, RING, 2, 512], F32R)
        wl = sb("wl", [P, RING, 2, 512], F32R)
        xs = sb("xs", [P, DK, 2 * CAP], F32R)
        gu = sb("gu", [P, 2, 512])
        hb = sb("hb", [P, 2, 4, CAP])
        sig = sb("sig", [P, 4, CAP])
        actf = sb("actf", [P, 4, CAP])
        a_hl = sb("a_hl", [P, DK, 2 * CAP], F32R)
        onehot = sb("onehot", [P, NT, CAP], F32R)
        pg = sb("pg", [P, NT, 2, CAP])
        pgt = sb("pgt", [P, S])
        ydn = sb("ydn", [P, D])
        loop_end = place[0]

        place[0] = shared
        xr = sb("xr", [P, NT, D])
        xn_at = place[0]
        xn = sb("xn", [P, NT, D])
        xt_at = place[0]
        xt = sb("xt", [P, DK, S])
        rr = sb("rr", [P, NT, 12, DH])
        kv = sb("kv", [P, NT, 512])
        gt = sb("gt", [P, NT, 24])
        glr = sb("glr", [P, NT, 16])
        gqk = sb("gqk", [P, NT, 512])
        gv_at = place[0]
        gv = sb("gv", [P, NT, 512])
        gr = sb("gr", [P, NT, 512])
        sq_at = place[0]
        sq = sb("sq", [P, NT, 12, DH])
        qt_at = place[0]
        qt = sb("qt", [P, G, S])
        qrt = sb("qrt", [P, G, S])
        kst_at = place[0]
        kst = sb("kst", [P, 2, S])
        hid_at = place[0]
        hid = sb("hid", [NCW, 2, HID])
        hidt = sb("hidt", [P, 2, 2, NCW])
        pt_at = place[0]
        pt = sb("pt", [P, 2, 2 * G * P])
        loga_at = place[0]
        loga = sb("loga", [P, NT, 256])
        eb = sb("eb", [P, NT, 256])
        en_at = place[0]
        en = sb("en", [P, NT, 256])
        es = sb("es", [P, NT, 256])
        qdt = sb("qdt", [P, 2, S])
        kdt = sb("kdt", [P, 2, S])
        ats = sb("ats", [P, 2, NT, 2, P])
        g12 = sb("g12", [P, 12, DH])
        glag = sb("glag", [P, DV])
        wgate = sb("wgate", [17, 256])
        glrt = sb("glrt", [17, S])
        w2 = sb("w2", [P, 2, 2, DH])
        wrt = sb("wrt", [P, DK, E])
        brt = sb("brt", [P, E])
        cmask = sb("cmask", [P, 256])
        mc01 = sb("mc01", [P, NT, NCMP])
        mcneg = sb("mcneg", [P, NT, NCMP])
        tri = sb("tri", [P, P])
        blk = sb("blk", [P, P])
        stri = sb("stri", [P, P])
        poss = sb("poss", [P, NT], I32)
        invf = sb("invf", [P, RD // 2])
        rope = sb("rope", [P, 5, NT, RD // 2])
        posl = sb("posl", [16, 2, P])
        post = sb("post", [P, 2, 16])
        gk0 = sb("gk0", [NCW, DH])
        kcn = sb("kcn", [NCW, DH])
        kcq = sb("kcq", [NCW, DH])
        vcs = sb("vcs", [NCW, DH])
        kct = sb("kct", [P, NCMP])
        dect = sb("dect", [P, 2, 4])
        st = sb("st", [P, 800])
        assert place[0] <= nc.sbuf_usable_end, (place[0], nc.sbuf_usable_end)
        assert loop_end <= loga_at
        g1b = at("g1b", [P, D], F32, sq_at)
        junk = at("junk", [P, D], F32, qt_at)
        kx = at("kx", [P, 2, HKV, P], F32, xt_at)
        tb = at("tb", [P, 2, 16, NCW], F32, xt_at + 2048)
        g2b = at("g2b", [P, D], F32, xt_at)
        bdn = at("bdn", [E, D], F32, xt_at + 4096)
        pb = at("pb", [P, 2, G * S], F32, xn_at)
        ot = at("ot", [P, DK, S], F32, xn_at)
        sta = at("sta", [P, 2, 3, DV], F32, sq_at)
        sgr = at("sgr", [P, NT, 512], F32, en_at)
        gsq = at("gsq", [P, NT, 512], F32, loga_at)
        brow = at("brow", [E, 2 * FF], F32, pt_at)
        h2t = at("h2t", [P, DK, S], F32, qt_at)
        gtt = at("gtt", [E, S], F32, kst_at)
        h2 = at("h2", [P, NT, D], F32, gv_at)
        h2s = at("h2s", [P, NT, 2, D], F32R, loga_at)
        yout = at("yout", [P, NT, D], F32, loga_at)
        pcs = at("pcs", [P, NT, G, DH], F32, sq_at + 4096)
        rtmp = at("rtmp", [P, 4, 12, RD // 2], F32, hid_at)
        otmp = at("otmp", [P, G * DH], F32, sq_at + 3072)
        osum = rr[:, :, 0:HQ, :]
        go = gqk
        qd, kd, kstate = gqk[:, :, 0:256], en, es

        banks = [ctx.enter_context(nc.psum_tensor(f"bank{i}", [P, 512], F32)) for i in range(8)]
        t_bank, x_bank = banks[6], banks[7]

        st_used = [0]

        def stc(*shape):
            n = int(np.prod(shape))
            v = st[:, st_used[0]:st_used[0] + n]
            st_used[0] += n
            if len(shape) == 2:
                v = v.rearrange("p (a b) -> p a b", b=shape[1])
            if len(shape) == 3:
                v = v.rearrange("p (a b c) -> p a b c", b=shape[1], c=shape[2])
            return v

        ms_x, rs_x, nw_x = stc(NT), stc(NT), stc(NT)
        ms_r, rs_r, nw_r = stc(NT, 12), stc(NT, 12), stc(NT, 12)
        ms_k, rs_k, nw_k = stc(1), stc(1), stc(1)
        ms_g, rs_g, nw_g = stc(NT, GH), stc(NT, GH), stc(NT, GH)
        ms_y, rs_y, nw_y = stc(NT), stc(NT), stc(NT)
        gsig = stc(NT, 24)
        cmax, cden = stc(NT, HQ), stc(NT, HQ)
        smax, sden, scoef = stc(8, G), stc(8, G), stc(8, G)
        lg, lgm = stc(NT, E + TOPK), stc(NT, E + TOPK)
        top, msk, gate, lgr = stc(NT, 8), stc(NT, E), stc(NT, E), stc(NT, E)
        gsum, ntop, cnts = stc(NT), stc(NT), stc(E)

        s = {n: ctx.enter_context(nc.semaphore("s_" + n)) for n in (
            "proj_full h_full wo_full x g1 rounds block_full wl yout out const hid g2 pv_full brow small act rope "
            "sin xt_full xt proj kx_full kx post_full post qt_full qt glrt_full glrt z_full absz e1 qr_full qrt "
            "sigh b_full bexp dec esd es ht_full hidt qdt_full qdt kct_full kct u_full sgr csub cexp pct_full pct "
            "pt_full pts nmax pexp ot_full ot h2 h2hi h2t_full h2t bias_full bias ntop gexp gt_full gtt pair_free "
            "wh xfill x_free merged bank_free comb hb sigm actf ahi dve ms_x xn ms_r rn tb qr_ready loga qd "
            "kc_full kcn ms_k at_full ats sta o_full go ms_g glaout cs_full csc pc oc_full osum_c sc_full soft "
            "pv_read osum x1 ms_y h2s rt_full msk gate pos_full t_free loopdve a_hl onehot pg yinit rs_x rs_r "
            "rs_k rs_g rs_y stage0 stage1 stage2 stage3 stage4 stage5 ").split()}

        def split_k(w):
            return w.rearrange("(k p) n -> p k n", p=P)

        def slot(i, width):
            return stage[i % NSLOT][:, 0:DK * width].rearrange("p (k n) -> p k n", k=DK)

        def front_slot(i):
            if i < len(IN_PIECES):
                return slot(i, IN_PIECES[i][1] - IN_PIECES[i][0])
            return slot(i, 512)

        def comp_slot(i):
            return stage[i % NSLOT][:, 0:16 * HID].rearrange("p (k n) -> p k n", k=16)

        def front_arrived(eng, i):
            eng.wait_ge(s[f"stage{i % NSLOT}"], 16 * (i // NSLOT + 1))

        def expert_slot(j):
            return (NF + j) % NSLOT

        def front_loads(j):
            return len(range(expert_slot(j), NF, NSLOT))

        def bc(ap, n):
            return ap.unsqueeze(len(ap.shape)).to_broadcast(list(ap.shape) + [n])

        w_up_v = w_gate_up[0].rearrange("e (k p) n -> p e k n", p=P)
        w_dn_v = w_down[0].rearrange("e (k p) n -> p e k n", p=P)

        def expert_source(e, j):
            if j < 4:
                return w_up_v[:, e, :, UP_COLS[j]:UP_COLS[j] + 512]
            return w_dn_v[:, e, :, 512 * (j - 4):512 * (j - 3)]

        def front_used(eng, i):
            if i < len(IN_PIECES):
                eng.wait_ge(s["proj_full"], NT * (i + 1 + (i == len(IN_PIECES) - 1)))
            elif i < len(IN_PIECES) + 2:
                eng.wait_ge(s["h_full"], i - len(IN_PIECES) + 1)
            else:
                eng.wait_ge(s["wo_full"], NT * (i - len(IN_PIECES) - 1))

        block = ctx.enter_context(nc.Block())

        @block.sync
        def _(sp):
            for ti in range(NT):
                sp.dma_start(xr[:, ti, :], x[0, ti * P:(ti + 1) * P, :]).then_inc(s["x"], 16)
            sp.dma_start(g1b[:], norm1_g[0].partition_broadcast(P)).then_inc(s["g1"], 16)
            for i in range(NF):
                if i >= NSLOT:
                    front_used(sp, i - NSLOT)
                if i < len(IN_PIECES):
                    src, dst = split_k(w_in[0])[:, :, IN_PIECES[i][0]:IN_PIECES[i][1]], front_slot(i)
                elif i < len(IN_PIECES) + 2:
                    src = split_k((cmp_w1_k, cmp_w1_v)[i - len(IN_PIECES)][0])
                    dst = comp_slot(i)
                else:
                    m = i - len(IN_PIECES) - 2
                    src, dst = split_k(w_out[0])[:, :, 512 * m:512 * (m + 1)], front_slot(i)
                sp.dma_start(dst, src).then_inc(s[f"stage{i % NSLOT}"], 16)
            for j in range(PIECES):
                front_used(sp, NF + j - NSLOT)
                sp.dma_start(slot(NF + j, 512), expert_source(0, j)).then_inc(s[f"stage{expert_slot(j)}"], 16)
            sp.wait_ge(s["rounds"], 1)
            last_step = sp.value_load(rounds_i[0:1, 0:1], min_val=E - 1, max_val=ROUNDS * E - 1)
            with sp.Fori(1, last_step + 1) as it:
                expert = sp.snap(it % E, min_val=0, max_val=E - 1)
                for j in range(PIECES):
                    sp.wait_ge(s["block_full"], it * PIECES + (j + 1 - PIECES))
                    sp.dma_start(slot(NF + j, 512), expert_source(expert, j)).then_inc(s[f"stage{expert_slot(j)}"], 16)
            for ti in range(NT):
                sp.wait_ge(s["yout"], 2 * (ti + 1))
                sp.dma_start(out[0, ti * P:(ti + 1) * P, :], yout[:, ti, :]).then_inc(s["out"], 16)
            sp.wait_ge(s["out"], 16 * NT)

        @block.gpsimd
        def _(pool):
            c = [0]

            def step(ins):
                c[0] += 1
                ins.then_inc(s["const"], 1)
                pool.wait_ge(s["const"], c[0])

            def select(t, compare_op, fill, base, pattern, mult):
                step(nc.gpsimd.affine_select(out=t, in_=t, compare_op=compare_op, fill=fill, base=base,
                                             pattern=pattern, channel_multiplier=mult))

            step(nc.gpsimd.memset(ident[:], 0.0))
            select(ident[:], ALU.not_equal, 1.0, 0, [[-1, P]], 1)
            step(nc.gpsimd.memset(glrt[:], 1.0))
            step(nc.gpsimd.memset(ones[:], 1.0))
            step(nc.gpsimd.memset(stack_i[:], 0.0))
            select(stack_i[:], ALU.not_equal, 1.0, 0, [[-1, CAP]], 1)
            select(stack_i[:], ALU.not_equal, 1.0, -CAP, [[-1, CAP]], 1)
            step(nc.gpsimd.memset(cmask[:], 0.0))
            select(cmask[:], ALU.is_ge, NEG, P, [[-1, 2 * P]], 1)
            step(nc.gpsimd.memset(mc01[:], 1.0))
            select(mc01[:], ALU.is_ge, 0.0, 1 - CBL, [[P, NT], [-CST, NCMP]], 1)
            step(nc.gpsimd.memset(tri[:], 1.0))
            select(tri[:], ALU.is_ge, 0.0, 0, [[1, P]], -1)
            step(nc.gpsimd.memset(tri[0:CH, CH:P], 0.0))
            step(nc.gpsimd.memset(blk[:], 0.0))
            step(nc.gpsimd.memset(blk[0:CH, 0:CH], 1.0))
            step(nc.gpsimd.memset(blk[CH:P, CH:P], 1.0))
            step(nc.gpsimd.memset(stri[:], 1.0))
            select(stri[:], ALU.is_gt, 0.0, 0, [[1, P]], -1)
            step(nc.gpsimd.iota(iota_i[:], [[1, CAP]], base=0, channel_multiplier=0))
            assert c[0] == N_CONST, c[0]
            pool.wait_ge(s["hid"], 2)
            pool.dma_start(g2b[:], norm2_g[0].partition_broadcast(P)).then_inc(s["g2"], 16)
            pool.dma_start(bdn[:], b_down[0]).then_inc(s["g2"], 16)
            pool.wait_ge(s["pv_full"], 8)
            pool.dma_start(brow[:], b_gate_up[0]).then_inc(s["brow"], 16)

        @block.scalar
        def _(act):
            small = [
                (poss[:], positions[0].rearrange("(t p) -> p t", p=P)),
                (g12[:, 0:HQ, :], nsa_q_norm_g[0:1, :].partition_broadcast(P).to_broadcast([P, HQ, DH])),
                (g12[:, HQ:HQ + 2, :], nsa_k_norm_g[0, 1:2, :].partition_broadcast(P).to_broadcast([P, 2, DH])),
                (g12[:, HQ + 2:HQ + 4, :], nsa_k_norm_g[0, 2:3, :].partition_broadcast(P).to_broadcast([P, 2, DH])),
                (gk0[:], nsa_k_norm_g[0, 0, :].partition_broadcast(NCW)),
                (glag[:], gla_norm_g[0].partition_broadcast(P)),
                (wgate[0:16, :], gla_w_gate[0]),
                (wgate[16:17, :], gla_b_gate[0:1, :]),
                (posl[:, 0, :], cmp_pos_k[0].rearrange("(c i) d -> c (i d)", i=2)),
                (posl[:, 1, :], cmp_pos_v[0].rearrange("(c i) d -> c (i d)", i=2)),
                (w2[:, 0, :, :], split_k(cmp_w2_k[0])),
                (w2[:, 1, :, :], split_k(cmp_w2_v[0])),
                (wrt[:], split_k(w_router[0])),
                (brt[:], b_router[0].partition_broadcast(P)),
            ]
            for dst, src in small:
                act.dma_start(dst, src, allow_slow_non_contiguous=True).then_inc(s["small"], 16)
            assert len(small) == N_SMALL

            n_act = [0]

            def rstd(what, a, r):
                act.wait_ge(s["ms_" + what], 1)
                link(nc.scalar.activation(r, a, ACT.Ln))
                nc.scalar.activation(r, r, ACT.Exp, scale=-0.5).then_inc(s["rs_" + what], 1)

            def link(ins):
                n_act[0] += 1
                ins.then_inc(s["act"], 1)
                act.wait_ge(s["act"], n_act[0])

            rstd("x", ms_x, rs_x)
            act.wait_ge(s["rope"], 1)
            nc.scalar.activation(rope[:, 2, :, :], rope[:, 0, :, :], ACT.Sin)
            nc.scalar.activation(rope[:, 3, :, :], rope[:, 0, :, :], ACT.Sin, scale=0.5).then_inc(s["sin"], 1)
            for q in range(4):
                act.wait_ge(s["xt_full"], q + 1)
                ti, half = q // 2, q % 2
                nc.scalar.copy(xt[:, 4 * half:4 * half + 4, ti * P:(ti + 1) * P],
                               banks[q][:].rearrange("p (k t) -> p k t", k=4)).then_inc(s["xt"], 1)
            n = 0
            for name, c0, width in PROJ:
                for ti in range(NT):
                    b = banks[4 + n % 4]
                    act.wait_ge(s["proj_full"], n + 1)
                    if name == "q":
                        last = nc.scalar.copy(rr[:, ti, 0:HQ, :].rearrange("p (g h) d -> p h g d", h=HKV),
                                              b[:, 0:512].rearrange("p (h g d) -> p h g d", h=HKV, g=G))
                    elif name == "kv":
                        nc.scalar.copy(kv[:, ti, 0:256], b[:, 0:256])
                        nc.scalar.copy(rr[:, ti, HQ:HQ + 2, :], b[:, 256:384].rearrange("p (h d) -> p h d", h=2))
                        last = nc.scalar.copy(kv[:, ti, 256:384], b[:, 384:512])
                    elif name == "w":
                        nc.scalar.copy(rr[:, ti, HQ + 2:HQ + 4, :], b[:, 0:128].rearrange("p (h d) -> p h d", h=2))
                        nc.scalar.copy(kv[:, ti, 384:512], b[:, 128:256])
                        last = nc.scalar.copy(gt[:, ti, :], b[:, 256:280])
                    else:
                        dst = {"gqk": gqk, "gv": gv, "glr": glr, "gr": gr}[name]
                        last = nc.scalar.copy(dst[:, ti, :], b[:, 0:width])
                    last.then_inc(s["proj"], 1)
                    n += 1
            act.wait_ge(s["kx_full"], 1)
            kvt = banks[0][:].rearrange("p (c t i) -> p c t i", c=2, i=2)
            for i in range(2):
                for h in range(HKV):
                    nc.scalar.copy(kx[i * DH:(i + 1) * DH, :, h, :], kvt[h * DH:(h + 1) * DH, :, :, i])\
                        .then_inc(s["kx"], 1)
            act.wait_ge(s["post_full"], 1)
            nc.scalar.copy(post[:], banks[1][:, 0:32].rearrange("p (c k) -> p c k", c=2)).then_inc(s["post"], 1)
            rstd("r", ms_r, rs_r)
            for ti in range(NT):
                act.wait_ge(s["qt_full"], ti + 1)
                nc.scalar.copy(qt[:, :, ti * P:(ti + 1) * P], banks[2 + ti][:].rearrange("p (g t) -> p g t", g=G))\
                    .then_inc(s["qt"], 1)
            act.wait_ge(s["glrt_full"], 1)
            nc.scalar.copy(glrt[0:16, :], banks[4][0:16, 0:S]).then_inc(s["glrt"], 1)
            act.wait_ge(s["z_full"], 1)
            z = banks[5][:].rearrange("p (t n) -> p t n", t=NT)
            nc.scalar.activation(en[:], z, ACT.Abs).then_inc(s["absz"], 1)
            act.wait_ge(s["absz"], 1)
            link(nc.scalar.activation(en[:], en[:], ACT.Exp, scale=-1.0))
            nc.scalar.activation(en[:], en[:], ACT.Ln, bias=1.0).then_inc(s["e1"], 1)
            for q in range(3):
                act.wait_ge(s["qr_full"], q + 1)
                if q < 2:
                    nc.scalar.copy(qrt[:, :, q * P:(q + 1) * P], banks[6 + q][:].rearrange("p (g t) -> p g t", g=G))\
                        .then_inc(s["qrt"], 1)
                else:
                    nc.scalar.copy(kst[:], banks[0][:].rearrange("p (b t) -> p b t", b=2)).then_inc(s["qrt"], 1)
            for c in range(2):
                act.wait_ge(s["h_full"], c + 1)
                nc.scalar.activation(hid[:, c, :], banks[1 + c][0:NCW, 0:HID], ACT.Sigmoid).then_inc(s["sigh"], 1)
            act.wait_ge(s["proj"], 2 * len(PROJ))
            nc.scalar.activation(gsig, gt[:], ACT.Sigmoid)
            act.wait_ge(s["b_full"], 1)
            b = banks[3][:].rearrange("p (t n) -> p t n", t=NT)
            nc.scalar.activation(eb[:], b, ACT.Exp)
            nc.scalar.activation(en[:], b, ACT.Exp, scale=-1.0).then_inc(s["bexp"], 1)
            nc.scalar.activation(dect[:], banks[5][:, 0:8].rearrange("p (h c) -> p h c", h=2), ACT.Exp)\
                .then_inc(s["dec"], 1)
            act.wait_ge(s["esd"], 1)
            nc.scalar.activation(es[:], es[:], ACT.Exp).then_inc(s["es"], 1)
            act.wait_ge(s["ht_full"], 1)
            nc.scalar.copy(hidt[:], banks[6][:, 0:4 * NCW].rearrange("p (c k n) -> p c k n", c=2, k=2))\
                .then_inc(s["hidt"], 1)
            rstd("k", ms_k[0:NCW, :], rs_k[0:NCW, :])
            for t, b in ((qdt, banks[3]), (kdt, banks[4])):
                act.wait_ge(s["qdt_full"], 1 if t is qdt else 2)
                nc.scalar.copy(t[:], b[:].rearrange("p (h t) -> p h t", h=2)).then_inc(s["qdt"], 1)
            act.wait_ge(s["kct_full"], 1)
            nc.scalar.copy(kct[0:DH, :], banks[5][0:DH, 0:NCMP])
            nc.scalar.copy(kct[DH:P, :], banks[5][0:DH, HKO:NCW]).then_inc(s["kct"], 1)
            act.wait_ge(s["u_full"], 3)
            nc.scalar.activation(sgr[:], gr[:], ACT.Sigmoid).then_inc(s["sgr"], 1)
            rstd("g", ms_g, rs_g)
            act.wait_ge(s["csub"], 1)
            for h in range(HKV):
                v = pcs[:, :, :, h * HKO:h * HKO + NCMP]
                nc.scalar.activation(v, v, ACT.Exp, scale=SCALE).then_inc(s["cexp"], 1)
            for ti in range(NT):
                act.wait_ge(s["pct_full"], ti + 1)
                nc.scalar.copy(pt[0:DH, 0, ti * 512:(ti + 1) * 512], banks[(7, 0)[ti]][0:DH, :]).then_inc(s["pct"], 1)
            def evac_pt(i):
                act.wait_ge(s["pt_full"], i + 1)
                for k in range(GROUPS[i][1] + 1):
                    last = nc.scalar.copy(pt[:, (i + 1) % 2, k * 512:(k + 1) * 512], banks[(7, 0)[k]][:])
                last.then_inc(s["pts"], 1)

            for i, (br, ti, h) in enumerate(GROUPS):
                keys = P * (ti + 1)
                act.wait_ge(s["nmax"], i + 1)
                for g in range(G):
                    v = pb[:, i % 2, g * keys:(g + 1) * keys]
                    nc.scalar.activation(v, v, ACT.Exp, bias=smax[:, i, g:g + 1], scale=SCALE,
                                         accum_out=sden[:, i, g:g + 1]).then_inc(s["pexp"], 1)
                if i:
                    evac_pt(i - 1)
            evac_pt(len(GROUPS) - 1)
            for q in range(4):
                act.wait_ge(s["ot_full"], q + 1)
                nc.scalar.copy(ot[:, 2 * q:2 * q + 2, :], banks[3 + q][:].rearrange("p (k t) -> p k t", k=2))\
                    .then_inc(s["ot"], 1)
            rstd("y", ms_y, rs_y)
            for ti in range(NT):
                act.wait_ge(s["h2"], ti + 1)
                nc.scalar.copy(h2s[:, ti, 0, :], h2[:, ti, :]).then_inc(s["h2hi"], 1)
            for q in range(4):
                act.wait_ge(s["h2t_full"], q + 1)
                nc.scalar.copy(h2t[:, 2 * q:2 * q + 2, :], banks[3 + q][:].rearrange("p (k t) -> p k t", k=2))\
                    .then_inc(s["h2t"], 1)
            act.wait_ge(s["bias_full"], 1)
            nc.scalar.copy(bias_t[:], banks[0][:].rearrange("p (k e) -> p k e", e=E)).then_inc(s["bias"], 1)
            act.wait_ge(s["ntop"], 1)
            nc.scalar.activation(gate, lgr, ACT.Exp).then_inc(s["gexp"], 1)
            act.wait_ge(s["gt_full"], 1)
            nc.scalar.copy(gtt[:], banks[4][0:E, 0:S]).then_inc(s["gtt"], 1)

            def split_high(it, j):
                act.wait_ge(s[f"stage{expert_slot(j)}"], it * 16 + 16 * (front_loads(j) + 1))
                for q in range(PAIRS):
                    n = j * PAIRS + q
                    act.wait_ge(s["pair_free"], it * (PIECES * PAIRS) + n + 1)
                    nc.scalar.copy(wh[:, n % RING, :, :], slot(NF + j, 512)[:, 2 * q:2 * q + 2, :])\
                        .then_inc(s["wh"], 1)

            def gather_evac(fill, half):
                act.wait_ge(s["xfill"], fill)
                nc.scalar.copy(xs[:, 4 * half:4 * half + 4, :], x_bank[:].rearrange("p (k n) -> p k n", k=4))\
                    .then_inc(s["x_free"], 1)

            def up_evac(it, n):
                act.wait_ge(s["block_full"], it * PIECES + n + 1)
                act.wait_ge(s["merged"], it * 4 + n + 1)
                nc.scalar.copy(gu[:, n % 2, :], banks[4 + n % 2][:]).then_inc(s["bank_free"], 1)

            def down_evac(it, m):
                act.wait_ge(s["block_full"], it * PIECES + 5 + m)
                act.wait_ge(s["comb"], it + 1)
                nc.scalar.copy(ydn[:, 512 * m:512 * (m + 1)], banks[4 + m][:]).then_inc(s["bank_free"], 1)

            def act_half(it, hf):
                act.wait_ge(s["hb"], it * 2 + hf + 1)
                nc.scalar.activation(sig[:], hb[:, 0, :, :], ACT.Sigmoid, scale=ALPHA).then_inc(s["sigm"], 1)
                act.wait_ge(s["actf"], it * 2 + hf + 1)
                nc.scalar.copy(a_hl[:, 4 * hf:4 * hf + 4, 0:CAP], actf[:]).then_inc(s["ahi"], 1)

            def body(it, last):
                split_high(it, 2)
                up_evac(it, 0)
                split_high(it, 3)
                up_evac(it, 1)
                split_high(it, 4)
                up_evac(it, 2)
                act_half(it, 0)
                split_high(it, 5)
                up_evac(it, 3)
                if not last:
                    gather_evac(it * 3 + 3, 0)
                act_half(it, 1)
                act.wait_ge(s["xfill"], it * 3 + (3 if last else 4))
                nc.scalar.copy(pgt[:], x_bank[:, 0:S]).then_inc(s["x_free"], 1)
                if not last:
                    gather_evac(it * 3 + 5, 1)
                    split_high(it + 1, 0)
                down_evac(it, 0)
                if not last:
                    split_high(it + 1, 1)
                down_evac(it, 1)

            act.wait_ge(s["rounds"], 1)
            last_step = act.value_load(rounds_i[0:1, 0:1], min_val=E - 1, max_val=ROUNDS * E - 1)
            gather_evac(1, 0)
            gather_evac(2, 1)
            split_high(0, 0)
            split_high(0, 1)
            with act.Fori(0, last_step) as it:
                body(it, False)
            body(last_step, True)

        @block.vector
        def _(dve):
            n_dve = [0]
            V = nc.vector

            def link(ins):
                n_dve[0] += 1
                ins.then_inc(s["dve"], 1)
                dve.wait_ge(s["dve"], n_dve[0])

            def newton(what, a, r, w):
                dve.wait_ge(s["rs_" + what], 1)
                link(V.tensor_tensor(w, r, r, ALU.mult))
                link(V.tensor_tensor(w, w, a, ALU.mult))
                link(V.tensor_scalar(w, w, -0.5, 1.5, ALU.mult, ALU.add))
                link(V.tensor_tensor(r, r, w, ALU.mult))

            dve.wait_ge(s["x"], 16 * NT)
            for ti in range(NT):
                link(V.tensor_tensor_reduce(out=junk[:], in0=xr[:, ti, :], in1=xr[:, ti, :], scale=1.0, scalar=0.0,
                                            op0=ALU.mult, op1=ALU.add, accum_out=ms_x[:, ti:ti + 1]))
            V.tensor_scalar(ms_x, ms_x, 1.0 / D, EPS, ALU.mult, ALU.add).then_inc(s["ms_x"], 1)
            dve.wait_ge(s["ms_x"], 1)
            newton("x", ms_x, rs_x, nw_x)
            dve.wait_ge(s["g1"], 16)
            for ti in range(NT):
                V.scalar_tensor_tensor(out=xn[:, ti, :], in0=xr[:, ti, :], scalar=rs_x[:, ti:ti + 1], in1=g1b[:],
                                       op0=ALU.mult, op1=ALU.mult).then_inc(s["xn"], 1)
            for i in range(RD // 2):
                last = V.memset(invf[:, i:i + 1], float(np.exp(np.float32(-math.log(THETA)) * np.float32(2 * i) / np.float32(RD))))
            link(last)
            dve.wait_ge(s["small"], 16 * N_SMALL)
            posf = rope[:, 4, 0, 0:NT]
            link(V.tensor_copy(posf, poss[:]))
            link(V.tensor_tensor(rope[:, 0, :, :], bc(posf, RD // 2),
                                 invf[:].unsqueeze(1).to_broadcast([P, NT, RD // 2]), ALU.mult))
            link(V.tensor_scalar(rope[:, 1, :, :], rope[:, 0, :, :], 1 / (2 * math.pi), MAGIC, ALU.mult, ALU.add))
            link(V.tensor_scalar(rope[:, 1, :, :], rope[:, 1, :, :], -MAGIC, None, ALU.add))
            for c in TWO_PI:
                link(V.scalar_tensor_tensor(out=rope[:, 0, :, :], in0=rope[:, 1, :, :], scalar=-c,
                                            in1=rope[:, 0, :, :], op0=ALU.mult, op1=ALU.add))
            V.tensor_scalar(rope[:, 0, :, :], rope[:, 0, :, :], PI32, -PI32, ALU.min, ALU.max).then_inc(s["rope"], 1)
            dve.wait_ge(s["const"], N_CONST)
            V.tensor_copy(iota_f[:], iota_i[:])
            link(V.tensor_scalar(mcneg[:], mc01[:], 1.0, -NEG, ALU.subtract, ALU.mult))
            dve.wait_ge(s["proj"], 6)
            dve.wait_ge(s["xn"], NT)
            link(V.tensor_tensor(sq[:], rr[:], rr[:], ALU.mult))
            link(V.tensor_reduce(ms_r, sq[:], AX.X, ALU.add))
            V.tensor_scalar(ms_r, ms_r, 1.0 / DH, EPS, ALU.mult, ALU.add).then_inc(s["ms_r"], 1)
            dve.wait_ge(s["ms_r"], 1)
            dve.wait_ge(s["sin"], 1)
            link(V.tensor_tensor(rope[:, 3, :, :], rope[:, 3, :, :], rope[:, 3, :, :], ALU.mult))
            link(V.tensor_scalar(rope[:, 3, :, :], rope[:, 3, :, :], -2.0, 1.0, ALU.mult, ALU.add))
            newton("r", ms_r, rs_r, nw_r)
            link(V.tensor_tensor(rr[:], rr[:], bc(rs_r, DH), ALU.mult))
            for ti in range(NT):
                V.tensor_tensor(rr[:, ti, :, :], rr[:, ti, :, :], g12[:], ALU.mult).then_inc(s["rn"], 1)
            dve.wait_ge(s["kx"], 4)
            dve.wait_ge(s["post"], 1)
            for c in range(2):
                V.memset(tb[:, c, :, NCMP:HKO], 0.0)
                for h in range(HKV):
                    steps_of = kx[:, c, h, :].rearrange("p (n k) -> p k n", k=8)
                    for half in range(2):
                        k8 = slice(8 * half, 8 * half + 8)
                        V.tensor_tensor(tb[:, c, k8, h * HKO:h * HKO + NCMP], steps_of[:, :, half:half + NCMP],
                                        bc(post[:, c, k8], NCMP), ALU.add).then_inc(s["tb"], 1)
            dve.wait_ge(s["rn"], NT)
            dve.wait_ge(s["qt_full"], NT)
            for ti in range(NT):
                sin = rope[:, 2, ti, :].unsqueeze(1).to_broadcast([P, 12, RD // 2])
                cos = rope[:, 3, ti, :].unsqueeze(1).to_broadcast([P, 12, RD // 2])
                lo, hi = rr[:, ti, :, 0:RD // 2], rr[:, ti, :, RD // 2:RD]
                if ti:
                    dve.wait_ge(s["qr_ready"], 2 * ti)
                V.tensor_tensor(rtmp[:, 0], lo, cos, ALU.mult)
                V.tensor_tensor(rtmp[:, 1], hi, sin, ALU.mult)
                V.tensor_tensor(rtmp[:, 2], hi, cos, ALU.mult)
                link(V.tensor_tensor(rtmp[:, 3], lo, sin, ALU.mult))
                V.tensor_tensor(lo, rtmp[:, 0], rtmp[:, 1], ALU.subtract).then_inc(s["qr_ready"], 1)
                V.tensor_tensor(hi, rtmp[:, 2], rtmp[:, 3], ALU.add).then_inc(s["qr_ready"], 1)
            z = banks[5][:].rearrange("p (t n) -> p t n", t=NT)
            dve.wait_ge(s["absz"], 1)
            link(V.tensor_scalar(loga[:], z, 0.0, None, ALU.min))
            dve.wait_ge(s["e1"], 1)
            link(V.tensor_tensor(loga[:], loga[:], en[:], ALU.subtract))
            V.tensor_scalar(loga[:], loga[:], 1.0 / GTAU, None, ALU.mult).then_inc(s["loga"], 1)
            for c in range(2):
                dve.wait_ge(s["sigh"], c + 1)
                V.tensor_tensor(hid[:, c, :], banks[1 + c][0:NCW, 0:HID], hid[:, c, :], ALU.mult).then_inc(s["hid"], 1)
            dve.wait_ge(s["bexp"], 1)
            link(V.tensor_copy(es[:], banks[4][:].rearrange("p (t n) -> p t n", t=NT)))
            V.tensor_tensor(es[:], es[:], banks[3][:].rearrange("p (t n) -> p t n", t=NT), ALU.subtract)\
                .then_inc(s["esd"], 1)
            V.tensor_tensor(kd[:], gqk[:, :, 256:512], en[:], ALU.mult)
            V.scalar_tensor_tensor(out=qd, in0=qd, scalar=SCALE, in1=eb[:], op0=ALU.mult, op1=ALU.mult)\
                .then_inc(s["qd"], 1)
            dve.wait_ge(s["es"], 1)
            V.tensor_tensor(kstate[:], gqk[:, :, 256:512], es[:], ALU.mult).then_inc(s["qd"], 1)
            dve.wait_ge(s["kc_full"], 1)
            link(V.tensor_copy(kcn[:], banks[7][0:NCW, 0:DH]))
            V.tensor_copy(vcs[:], banks[0][0:NCW, 0:DH]).then_inc(s["kcn"], 1)
            link(V.tensor_tensor(kcq[:], kcn[:], kcn[:], ALU.mult))
            link(V.reduce_sum(ms_k[0:NCW, :], kcq[:], AX.X))
            V.tensor_scalar(ms_k[0:NCW, :], ms_k[0:NCW, :], 1.0 / DH, EPS, ALU.mult, ALU.add).then_inc(s["ms_k"], 1)
            dve.wait_ge(s["ms_k"], 1)
            newton("k", ms_k[0:NCW, :], rs_k[0:NCW, :], nw_k[0:NCW, :])
            V.scalar_tensor_tensor(out=kcn[:], in0=kcn[:], scalar=rs_k[0:NCW, :], in1=gk0[:],
                                   op0=ALU.mult, op1=ALU.mult).then_inc(s["kcn"], 1)
            for par in range(2):
                dve.wait_ge(s["at_full"], par + 1)
                V.tensor_tensor(ats[:, par].rearrange("p t h n -> p (t h) n"),
                                banks[1 + par][:].rearrange("p (a n) -> p a n", a=4),
                                tri[:].unsqueeze(1).to_broadcast([P, 4, P]), ALU.mult).then_inc(s["ats"], 1)
            for ci in range(3):
                dve.wait_ge(s["u_full"], ci + 1)
                if ci == 1:
                    dve.wait_ge(s["dec"], 1)
                for hp in range(2):
                    for par in range(2):
                        u = banks[(6, 7, 0)[ci]][par * 64:par * 64 + 64, hp * 256 + par * DV:hp * 256 + par * DV + DV]
                        dst = sta[par * 64:par * 64 + 64, hp, :, :]
                        if ci == 0:
                            last = V.tensor_copy(dst[:, 0, :], u)
                        else:
                            last = V.scalar_tensor_tensor(out=dst[:, ci, :], in0=dst[:, ci - 1, :],
                                                          scalar=dect[par * 64:par * 64 + 64, hp, ci:ci + 1], in1=u,
                                                          op0=ALU.mult, op1=ALU.add)
                last.then_inc(s["sta"], 1)
                dve.wait_ge(s["sta"], ci + 1)
            dve.wait_ge(s["sgr"], 1)
            link(V.tensor_tensor(gr[:], gr[:], sgr[:], ALU.mult))
            for ti in range(NT):
                for par in range(2):
                    dve.wait_ge(s["o_full"], 2 * ti + par + 1)
                    V.tensor_copy(go[:, ti, :].rearrange("p (h r d) -> p h r d", h=2, r=2)[:, :, par, :],
                                  banks[O_BANKS[ti][par]][:, 0:2 * DV].rearrange("p (h d) -> p h d", h=2))\
                        .then_inc(s["go"], 1)
            dve.wait_ge(s["go"], 2 * NT)
            link(V.tensor_tensor(gsq[:], go[:], go[:], ALU.mult))
            link(V.tensor_reduce(ms_g, gsq[:].rearrange("p t (h d) -> p t h d", h=GH), AX.X, ALU.add))
            V.tensor_scalar(ms_g, ms_g, 1.0 / DV, EPS, ALU.mult, ALU.add).then_inc(s["ms_g"], 1)
            dve.wait_ge(s["ms_g"], 1)
            newton("g", ms_g, rs_g, nw_g)
            go4 = go[:].rearrange("p t (h d) -> p (t h) d", h=GH)
            link(V.tensor_tensor(go4, go4, bc(rs_g.rearrange("p t h -> p (t h)"), DV), ALU.mult))
            link(V.tensor_tensor(go4, go4, glag[:].unsqueeze(1).to_broadcast([P, NT * GH, DV]), ALU.mult))
            V.tensor_tensor(go[:], go[:], gr[:], ALU.mult).then_inc(s["glaout"], 1)
            link(V.memset(pcs[:], 0.0))
            dve.wait_ge(s["cs_full"], 2)
            for h in range(HKV):
                v = pcs[:, :, :, h * HKO:h * HKO + NCMP]
                for ti in range(NT):
                    V.tensor_tensor(v[:, ti], banks[5 + h][:, ti * 64:ti * 64 + G * NCMP]
                                    .rearrange("p (g n) -> p g n", g=G),
                                    mcneg[:, ti, :].unsqueeze(1).to_broadcast([P, G, NCMP]), ALU.add)\
                        .then_inc(s["csc"], 1)
            dve.wait_ge(s["csc"], 4)
            for h in range(HKV):
                v = pcs[:, :, :, h * HKO:h * HKO + NCMP]
                cm = cmax.rearrange("p t (h g) -> p t h g", h=HKV)[:, :, h, :]
                link(V.tensor_reduce(cm, v, AX.X, ALU.max))
                last = V.tensor_tensor(v, v, bc(cm, NCMP), ALU.subtract)
            last.then_inc(s["csub"], 1)
            for h in range(HKV):
                dve.wait_ge(s["cexp"], h + 1)
                v = pcs[:, :, :, h * HKO:h * HKO + NCMP]
                cd = cden.rearrange("p t (h g) -> p t h g", h=HKV)[:, :, h, :]
                for ti in range(NT):
                    last = V.tensor_tensor(v[:, ti], v[:, ti],
                                           mc01[:, ti, :].unsqueeze(1).to_broadcast([P, G, NCMP]), ALU.mult)
                last.then_inc(s["pc"], 1)
                dve.wait_ge(s["pc"], h + 1)
                link(V.tensor_reduce(cd, v, AX.X, ALU.add))
            link(V.tensor_scalar(cden, cden, 0.5, None, ALU.max))
            link(V.reciprocal(cden, cden))
            gates = gsig.rearrange("p t (h b) -> p t h b", b=3)
            link(V.tensor_tensor(cden, cden, gates[:, :, :, 0], ALU.mult))
            for h in range(HKV):
                dve.wait_ge(s["oc_full"], h + 1)
                for ti in range(NT):
                    last = V.tensor_tensor(osum[:, ti, h * G:(h + 1) * G, :],
                                           banks[1 + h][:, ti * 256:(ti + 1) * 256].rearrange("p (g d) -> p g d", g=G),
                                           bc(cden[:, ti, h * G:(h + 1) * G], DH), ALU.mult)
                last.then_inc(s["osum_c"], 1)
            dve.wait_ge(s["osum_c"], 2)

            def soft(i):
                br, ti, h = GROUPS[i]
                keys = P * (ti + 1)
                dve.wait_ge(s["sc_full"], i + 1)
                mask = cmask[:, 2 * P - keys:2 * P] if ti == 0 else cmask[:]
                per = 512 // keys
                for b in range(G // per):
                    V.tensor_tensor(pb[:, i % 2, b * 512:b * 512 + 512].rearrange("p (g k) -> p g k", g=per),
                                    banks[SC_BANKS[i % 2][b]][:].rearrange("p (g k) -> p g k", g=per),
                                    mask.unsqueeze(1).to_broadcast([P, per, keys]), ALU.add).then_inc(s["soft"], 1)
                n_soft[0] += G // per
                dve.wait_ge(s["soft"], n_soft[0])
                link(V.reduce_max(smax[:, i, :], pb[:, i % 2, 0:G * keys].rearrange("p (g k) -> p g k", g=G), AX.X))
                V.tensor_scalar(smax[:, i, :], smax[:, i, :], -SCALE, None, ALU.mult).then_inc(s["nmax"], 1)

            def gather_out(i):
                br, ti, h = GROUPS[i]
                dve.wait_ge(s["pexp"], G * (i + 1))
                link(V.reciprocal(scoef[:, i, :], sden[:, i, :]))
                link(V.tensor_tensor(scoef[:, i, :], scoef[:, i, :], gates[:, ti, h * G:(h + 1) * G, 1 + br], ALU.mult))
                dve.wait_ge(s["pv_full"], i + 1)
                tmp = otmp[:].rearrange("p (g d) -> p g d", g=G)
                V.tensor_tensor(tmp, banks[1 + i % 2][:, 0:256].rearrange("p (g d) -> p g d", g=G),
                                bc(scoef[:, i, :], DH), ALU.mult).then_inc(s["pv_read"], 1)
                dve.wait_ge(s["pv_read"], i + 1)
                o = osum[:, ti, h * G:(h + 1) * G, :]
                V.tensor_tensor(o, o, tmp, ALU.add).then_inc(s["osum"], 1)
                dve.wait_ge(s["osum"], i + 1)

            n_soft = [0]
            for i in range(len(GROUPS)):
                soft(i)
                if i:
                    gather_out(i - 1)
            gather_out(len(GROUPS) - 1)
            for q in range(4):
                m, ti = q // 2, q % 2
                dve.wait_ge(s["wo_full"], q + 1)
                xv = xr[:, ti, 512 * m:512 * (m + 1)]
                V.tensor_tensor(xv, xv, banks[WO_BANKS[q]][:], ALU.add).then_inc(s["x1"], 1)
            dve.wait_ge(s["x1"], 4)
            for ti in range(NT):
                link(V.tensor_tensor_reduce(out=junk[:], in0=xr[:, ti, :], in1=xr[:, ti, :], scale=1.0, scalar=0.0,
                                            op0=ALU.mult, op1=ALU.add, accum_out=ms_y[:, ti:ti + 1]))
            V.tensor_scalar(ms_y, ms_y, 1.0 / D, EPS, ALU.mult, ALU.add).then_inc(s["ms_y"], 1)
            dve.wait_ge(s["ms_y"], 1)
            newton("y", ms_y, rs_y, nw_y)
            dve.wait_ge(s["g2"], 32)
            for ti in range(NT):
                V.scalar_tensor_tensor(out=h2[:, ti, :], in0=xr[:, ti, :], scalar=rs_y[:, ti:ti + 1], in1=g2b[:],
                                       op0=ALU.mult, op1=ALU.mult).then_inc(s["h2"], 1)
            dve.wait_ge(s["h2"], NT)
            for ti in range(NT):
                dve.wait_ge(s["h2hi"], ti + 1)
                V.tensor_tensor(h2s[:, ti, 1, :], h2[:, ti, :], h2s[:, ti, 0, :].bitcast(F32), ALU.subtract)\
                    .then_inc(s["h2s"], 1)
            dve.wait_ge(s["rt_full"], 1)
            V.memset(lg[:, :, E:], FILLER)
            link(V.tensor_tensor(lg[:, :, 0:E], banks[7][:, 0:NT * E].rearrange("p (t e) -> p t e", t=NT),
                                 brt[:].unsqueeze(1).to_broadcast([P, NT, E]), ALU.add))
            for ti in range(NT):
                link(V.max(top[:, ti, :], lg[:, ti, 0:E]))
            link(V.tensor_scalar(ntop, top[:, :, 0], -1.0, None, ALU.mult))
            V.tensor_tensor(lgr, lg[:, :, 0:E], bc(ntop, E), ALU.add).then_inc(s["ntop"], 1)
            link(V.memset(top[:, :, TOPK:8], FILLER))
            for ti in range(NT):
                link(V.match_replace(lgm[:, ti, :], top[:, ti, :], lg[:, ti, :], -FILLER))
            V.tensor_tensor(msk, lgm[:, :, 0:E], lg[:, :, 0:E], ALU.not_equal).then_inc(s["msk"], 1)
            dve.wait_ge(s["msk"], 1)
            dve.wait_ge(s["gexp"], 1)
            link(V.tensor_tensor(gate, gate, msk, ALU.mult))
            link(V.tensor_reduce(gsum, gate, AX.X, ALU.add))
            link(V.reciprocal(gsum, gsum))
            V.tensor_tensor(gate, gate, bc(gsum, E), ALU.mult).then_inc(s["gate"], 1)
            dve.wait_ge(s["gate"], 1)
            V.memset(gates4[:, :, ROUNDS * E:], 0.0)
            for r in range(ROUNDS):
                V.tensor_copy(gates4[:, :, r * E:(r + 1) * E], gate)
            dve.wait_ge(s["pos_full"], 1)
            V.memset(posm[:, :, ROUNDS * E:], -1.0)
            link(V.scalar_tensor_tensor(out=lgr, in0=banks[1][:, 0:NT * E].rearrange("p (t e) -> p t e", t=NT),
                                        scalar=1.0, in1=msk, op0=ALU.add, op1=ALU.mult))
            for r in range(ROUNDS):
                link(V.tensor_scalar(posm[:, :, r * E:(r + 1) * E], lgr, -1.0 - CAP * r, None, ALU.add))
            link(V.reduce_max(rounds_f[:, 0:1], banks[2][:, 0:E], AX.X))
            for r in range(1, ROUNDS):
                link(V.tensor_scalar(rounds_f[:, r:r + 1], rounds_f[:, 0:1], float(CAP * r), float(E), ALU.is_gt, ALU.mult))
            link(V.reduce_sum(rounds_f[:, 0:1], rounds_f[:, 1:ROUNDS], AX.X))
            V.tensor_scalar(rounds_i[:], rounds_f[:, 0:1], float(E - 1), None, ALU.add).then_inc(s["rounds"], 1)

            def split_low(it, j):
                for q in range(PAIRS):
                    n = j * PAIRS + q
                    dve.wait_ge(s["wh"], it * (PIECES * PAIRS) + n + 1)
                    V.tensor_tensor(wl[:, n % RING, :, :], slot(NF + j, 512)[:, 2 * q:2 * q + 2, :],
                                    wh[:, n % RING, :, :].bitcast(F32), ALU.subtract).then_inc(s["wl"], 1)

            def place_of(tensor, it, *shape):
                v = tensor[:, :, bass.ds(it, 1)]
                if len(shape) == 1:
                    return v.to_broadcast([P, NT, CAP])
                return v.unsqueeze(3).to_broadcast([P, NT, 2, CAP])

            def slots_of(n):
                if n == 1:
                    return iota_f[:].unsqueeze(1).to_broadcast([P, NT, CAP])
                return iota_f[:].unsqueeze(1).unsqueeze(1).to_broadcast([P, NT, 2, CAP])

            def swiglu(it, hf):
                dve.wait_ge(s["merged"], it * 4 + 2 * hf + 4)
                bias = bias_t[:].rearrange("p (a b c) e -> p b a c e", a=2, b=2)[:, hf, :, :, bass.ds(it % E, 1)]
                V.tensor_tensor(hb[:], t_bank[:].rearrange("p (a c n) -> p a c n", a=2, c=4),
                                bias.to_broadcast([P, 2, 4, CAP]), ALU.add).then_inc(s["t_free"], 1)
                dve.wait_ge(s["t_free"], it * 2 + hf + 2)
                V.tensor_scalar(hb[:, 0], hb[:, 0], LIMIT, None, ALU.min).then_inc(s["hb"], 1)
                V.tensor_scalar(hb[:, 1], hb[:, 1], LIMIT, -LIMIT, ALU.min, ALU.max).then_inc(s["loopdve"], 1)
                dve.wait_ge(s["hb"], it * 2 + hf + 1)
                dve.wait_ge(s["loopdve"], it * 5 + 2 * hf + 2)
                V.scalar_tensor_tensor(out=hb[:, 1], in0=hb[:, 1], scalar=1.0, in1=hb[:, 0],
                                       op0=ALU.add, op1=ALU.mult).then_inc(s["loopdve"], 1)
                dve.wait_ge(s["loopdve"], it * 5 + 2 * hf + 3)
                dve.wait_ge(s["sigm"], it * 2 + hf + 1)
                V.tensor_tensor(actf[:], hb[:, 1], sig[:], ALU.mult).then_inc(s["actf"], 1)
                dve.wait_ge(s["ahi"], it * 2 + hf + 1)
                V.tensor_tensor(a_hl[:, 4 * hf:4 * hf + 4, CAP:], actf[:],
                                a_hl[:, 4 * hf:4 * hf + 4, 0:CAP].bitcast(F32), ALU.subtract).then_inc(s["a_hl"], 1)

            def one_hot(it):
                V.tensor_tensor(onehot[:], slots_of(1), place_of(posm, it, 1), ALU.is_equal).then_inc(s["onehot"], 1)

            def body(it, last):
                dve.wait_ge(s["xfill"], it * 3 + 2)
                if not last:
                    one_hot(it + 1)
                V.tensor_tensor(pg[:], slots_of(2), place_of(posm, it, 1, 1), ALU.is_equal).then_inc(s["loopdve"], 1)
                dve.wait_ge(s["loopdve"], it * 5 + 1)
                V.tensor_tensor(pg[:], pg[:], place_of(gates4, it, 1, 1), ALU.mult).then_inc(s["pg"], 1)
                split_low(it, 2)
                split_low(it, 3)
                swiglu(it, 0)
                split_low(it, 4)
                swiglu(it, 1)
                split_low(it, 5)
                if not last:
                    split_low(it + 1, 0)
                    split_low(it + 1, 1)

            dve.wait_ge(s["yinit"], 4)
            dve.wait_ge(s["bias"], 1)
            V.memset(pgt[:], 0.0).then_inc(s["merged"], 2)
            V.memset(token[:, 0:1], 0.0).then_inc(s["t_free"], 1)
            V.memset(token[:, 1:2], 0.0).then_inc(s["x_free"], 1)
            V.memset(token[:, 2:3], 0.0).then_inc(s["pair_free"], RING)
            V.memset(ydn[:], 0.0).then_inc(s["bank_free"], 2)
            one_hot(0)
            dve.wait_ge(s["rounds"], 1)
            last_step = dve.value_load(rounds_i[0:1, 0:1], min_val=E - 1, max_val=ROUNDS * E - 1)
            split_low(0, 0)
            split_low(0, 1)
            with dve.Fori(0, last_step) as it:
                body(it, False)
            body(last_step, True)
            dve.wait_ge(s["comb"], last_step + 2)
            for ti in range(NT):
                for m in range(2):
                    V.tensor_copy(yout[:, ti, 512 * m:512 * (m + 1)], banks[2 * ti + m][:]).then_inc(s["yout"], 1)

        @block.tensor
        def _(pe):
            mm, tp = nc.tensor.matmul, nc.tensor.transpose
            pe.wait_ge(s["const"], 2)
            for ti in range(NT):
                pe.wait_ge(s["xn"], ti + 1)
                for half in range(2):
                    for k in range(4):
                        c = 4 * half + k
                        last = tp(banks[2 * ti + half][:, k * P:(k + 1) * P], xn[:, ti, c * P:(c + 1) * P], ident[:])
                    last.then_inc(s["xt_full"], 1)
            pe.wait_ge(s["xt"], 4)
            n = 0
            for name, c0, width in PROJ:
                piece = next(i for i, (a, b) in enumerate(IN_PIECES) if a <= c0 < b)
                front_arrived(pe, piece)
                off = c0 - IN_PIECES[piece][0]
                for ti in range(NT):
                    if n >= 4:
                        pe.wait_ge(s["proj"], n - 3)
                    for k in range(DK):
                        last = mm(banks[4 + n % 4][:, 0:width], xt[:, k, ti * P:(ti + 1) * P],
                                  front_slot(piece)[:, k, off:off + width], start=k == 0, stop=k == DK - 1)
                    last.then_inc(s["proj_full"], 1)
                    n += 1
            pe.wait_ge(s["proj"], n)
            for c in range(2):
                for ti in range(NT):
                    last = tp(banks[0][:, (2 * c + ti) * P:(2 * c + ti + 1) * P], kv[:, ti, c * P:(c + 1) * P], ident[:])
            last.then_inc(s["kx_full"], 1)
            pe.wait_ge(s["small"], 16 * N_SMALL)
            for c in range(2):
                last = tp(banks[1][:, 16 * c:16 * c + 16], posl[:, c, :], ident[0:16, 0:16])
            last.then_inc(s["post_full"], 1)

            def pair(ti, g):
                return rr[:, ti, HKV * g:HKV * (g + 1), :]

            for ti in range(NT):
                pe.wait_ge(s["rn"], ti + 1)
                for g in range(G):
                    last = tp(banks[2 + ti][:, g * P:(g + 1) * P], pair(ti, g), ident[:])
                last.then_inc(s["qt_full"], 1)
            for ti in range(NT):
                last = tp(banks[4][0:16, ti * P:(ti + 1) * P], glr[:, ti, :], ident[:])
            last.then_inc(s["glrt_full"], 1)
            pe.wait_ge(s["glrt"], 1)
            for ti in range(NT):
                last = mm(banks[5][:, ti * 256:(ti + 1) * 256], glrt[:, ti * P:(ti + 1) * P], wgate[:], start=True, stop=True)
            last.then_inc(s["z_full"], 1)
            for ti in range(NT):
                pe.wait_ge(s["qr_ready"], 2 * (ti + 1))
                for g in range(G):
                    last = tp(banks[6 + ti][:, g * P:(g + 1) * P], pair(ti, g), ident[:])
                last.then_inc(s["qr_full"], 1)
            pe.wait_ge(s["kx"], 4)
            for br in range(2):
                for ti in range(NT):
                    last = tp(banks[0][:, (2 * br + ti) * P:(2 * br + ti + 1) * P],
                              rr[:, ti, HQ + 2 * br:HQ + 2 * br + 2, :], ident[:])
            last.then_inc(s["qr_full"], 1)
            pe.wait_ge(s["tb"], 8)
            pe.wait_ge(s["qt"], 2)
            for c in range(2):
                i = len(IN_PIECES) + c
                front_arrived(pe, i)
                for k in range(16):
                    last = mm(banks[1 + c][0:NCW, 0:HID], tb[:, c, k, :], comp_slot(i)[:, k, :], start=k == 0, stop=k == 15)
                last.then_inc(s["h_full"], 1)
            pe.wait_ge(s["loga"], 1)
            pe.wait_ge(s["const"], N_CONST)
            for ti in range(NT):
                mm(banks[3][:, ti * 256:(ti + 1) * 256], tri[:], loga[:, ti, :], start=True, stop=True)
                mm(banks[4][:, ti * 256:(ti + 1) * 256], blk[:], loga[:, ti, :], start=True, stop=True)
                for hp in range(2):
                    last = mm(banks[5][:, hp * 4 + ti * 2:hp * 4 + ti * 2 + 2], loga[:, ti, hp * P:(hp + 1) * P],
                              blk[:, 0:P:CH], start=True, stop=True)
            last.then_inc(s["b_full"], 1)
            pe.wait_ge(s["hid"], 2)
            pe.wait_ge(s["qrt"], 3)
            for c in range(2):
                for k in range(2):
                    last = tp(banks[6][:, (2 * c + k) * NCW:(2 * c + k + 1) * NCW], hid[:, c, k * P:(k + 1) * P],
                              ident[0:NCW, 0:NCW])
            last.then_inc(s["ht_full"], 1)
            pe.wait_ge(s["hidt"], 1)
            for c in range(2):
                for k in range(2):
                    last = mm(banks[(7, 0)[c]][0:NCW, 0:DH], hidt[:, c, k, :], w2[:, c, k, :], start=k == 0, stop=k == 1)
            last.then_inc(s["kc_full"], 1)
            pe.wait_ge(s["qd"], 1)
            for src, b in ((qd, banks[3]), (kd, banks[4])):
                for hp in range(2):
                    for ti in range(NT):
                        last = tp(b[:, hp * S + ti * P:hp * S + (ti + 1) * P], src[:, ti, hp * P:(hp + 1) * P], ident[:])
                last.then_inc(s["qdt_full"], 1)
            pe.wait_ge(s["qdt"], 2)
            for par in range(2):
                for ti in range(NT):
                    for hp in range(2):
                        last = mm(banks[1 + par][:, (2 * ti + hp) * P:(2 * ti + hp + 1) * P],
                                  kdt[par * 64:par * 64 + 64, hp, ti * P:(ti + 1) * P],
                                  qdt[par * 64:par * 64 + 64, hp, ti * P:(ti + 1) * P], start=True, stop=True)
                last.then_inc(s["at_full"], 1)
            pe.wait_ge(s["kcn"], 2)
            pe.wait_ge(s["dec"], 1)
            tp(banks[5][0:DH, 0:NCW], kcn[:], ident[0:NCW, 0:NCW]).then_inc(s["kct_full"], 1)
            pe.wait_ge(s["qd"], 2)
            for ci in range(3):
                ti, r = ci // 2, 64 * (ci % 2)
                for hp in range(2):
                    last = mm(banks[(6, 7, 0)[ci]][:, hp * 256:(hp + 1) * 256], kstate[r:r + 64, ti, hp * P:(hp + 1) * P],
                              gv[r:r + 64, ti, hp * 256:(hp + 1) * 256], start=True, stop=True)
                last.then_inc(s["u_full"], 1)
            pe.wait_ge(s["sta"], 3)
            for ti in range(NT):
                for par in range(2):
                    pe.wait_ge(s["ats"], par + 1)
                    b = banks[O_BANKS[ti][par]]
                    for hp in range(2):
                        h = 2 * hp + par
                        last = mm(b[:, hp * DV:(hp + 1) * DV], ats[:, par, ti, hp, :], gv[:, ti, h * DV:(h + 1) * DV],
                                  start=True, stop=True)
                        for j in range(2):
                            ci = 2 * ti + j
                            if ci:
                                last = mm(b[64 * j:64 * j + 64, hp * DV:(hp + 1) * DV],
                                          qdt[par * 64:par * 64 + 64, hp, ti * P + 64 * j:ti * P + 64 * j + 64],
                                          sta[par * 64:par * 64 + 64, hp, ci - 1, :], start=False, stop=True,
                                          skip_group_check=True)
                    last.then_inc(s["o_full"], 1)
            pe.wait_ge(s["kct"], 1)
            pe.wait_ge(s["go"], 2 * NT)
            for h in range(HKV):
                for ti in range(NT):
                    for g in range(G):
                        last = mm(banks[5 + h][:, ti * 64 + g * NCMP:ti * 64 + (g + 1) * NCMP],
                                  qt[h * DH:(h + 1) * DH, g, ti * P:(ti + 1) * P], kct[h * DH:(h + 1) * DH, :],
                                  start=True, stop=True)
                last.then_inc(s["cs_full"], 1)
            pe.wait_ge(s["pc"], 2)
            for ti in range(NT):
                for g in range(G):
                    last = tp(banks[(7, 0)[ti]][0:DH, g * P:(g + 1) * P], pcs[:, ti, g, :], ident[:])
                last.then_inc(s["pct_full"], 1)
            pe.wait_ge(s["pct"], 2)
            for h in range(HKV):
                for ti in range(NT):
                    for g in range(G):
                        o = ti * 512 + g * P
                        last = mm(banks[1 + h][:, ti * 256 + g * DH:ti * 256 + (g + 1) * DH],
                                  pt[h * HKO:h * HKO + NCMP, 0, o:o + P], vcs[h * HKO:h * HKO + NCMP, :],
                                  start=True, stop=True)
                last.then_inc(s["oc_full"], 1)

            def scores(i):
                br, ti, h = GROUPS[i]
                keys = P * (ti + 1)
                if i >= 2:
                    pe.wait_ge(s["nmax"], i - 1)
                per = 512 // keys
                for g in range(G):
                    last = mm(banks[SC_BANKS[i % 2][g // per]][:, (g % per) * keys:(g % per + 1) * keys],
                              qrt[h * DH:(h + 1) * DH, g, ti * P:(ti + 1) * P],
                              kst[h * DH:(h + 1) * DH, br, 0:keys], start=True, stop=True)
                last.then_inc(s["sc_full"], 1)

            def values(i):
                br, ti, h = GROUPS[i]
                n = ti + 1
                if i:
                    pe.wait_ge(s["pts"], i)
                for g in range(G):
                    pe.wait_ge(s["pexp"], G * i + g + 1)
                    for k in range(n):
                        u = g * n + k
                        last = tp(banks[(7, 0)[u // 4]][:, (u % 4) * P:(u % 4 + 1) * P],
                                  pb[:, i % 2, (g * n + k) * P:(g * n + k + 1) * P], ident[:])
                last.then_inc(s["pt_full"], 1)
                if i >= 2:
                    pe.wait_ge(s["pv_read"], i - 1)
                pe.wait_ge(s["pts"], i + 1)
                for g in range(G):
                    for k in range(n):
                        u = g * n + k
                        last = mm(banks[1 + i % 2][:, g * DH:(g + 1) * DH], pt[:, (i + 1) % 2, u * P:(u + 1) * P],
                                  kv[:, k, 256 + 128 * br + h * DH:256 + 128 * br + (h + 1) * DH],
                                  start=k == 0, stop=k == n - 1)
                last.then_inc(s["pv_full"], 1)

            pe.wait_ge(s["osum_c"], 2)
            scores(0)
            for i in range(len(GROUPS)):
                if i + 1 < len(GROUPS):
                    scores(i + 1)
                values(i)
            pe.wait_ge(s["glaout"], 1)
            pe.wait_ge(s["osum"], 8)
            for q in range(4):
                for kk in range(2):
                    for ti in range(NT):
                        k = 2 * q + kk
                        src = osum[:, ti, 2 * k:2 * k + 2, :] if k < 4 else go[:, ti, (k - 4) * P:(k - 3) * P]
                        last = tp(banks[3 + q][:, kk * S + ti * P:kk * S + (ti + 1) * P], src, ident[:])
                last.then_inc(s["ot_full"], 1)
            pe.wait_ge(s["ot"], 4)
            for q in range(4):
                m, ti = q // 2, q % 2
                i = len(IN_PIECES) + 2 + m
                front_arrived(pe, i)
                for k in range(DK):
                    last = mm(banks[WO_BANKS[q]][:], ot[:, k, ti * P:(ti + 1) * P], front_slot(i)[:, k, :],
                              start=k == 0, stop=k == DK - 1)
                last.then_inc(s["wo_full"], 1)
            pe.wait_ge(s["brow"], 16)
            pe.wait_ge(s["x1"], 4)
            for k in range(2 * FF // P):
                last = tp(banks[0][:, k * E:(k + 1) * E], brow[:, k * P:(k + 1) * P], ident[0:E, 0:E])
            last.then_inc(s["bias_full"], 1)
            pe.wait_ge(s["h2"], NT)
            for q in range(4):
                for kk in range(2):
                    for ti in range(NT):
                        k = 2 * q + kk
                        last = tp(banks[3 + q][:, kk * S + ti * P:kk * S + (ti + 1) * P], h2[:, ti, k * P:(k + 1) * P], ident[:])
                last.then_inc(s["h2t_full"], 1)
            pe.wait_ge(s["h2t"], 4)
            for ti in range(NT):
                for k in range(DK):
                    last = mm(banks[7][:, ti * E:(ti + 1) * E], h2t[:, k, ti * P:(ti + 1) * P], wrt[:, k, :],
                              start=k == 0, stop=k == DK - 1)
            last.then_inc(s["rt_full"], 1)
            pe.wait_ge(s["msk"], 1)
            mm(banks[1][:, 0:E], stri[:], msk[:, 0, :], start=True, stop=True)
            mm(banks[1][:, E:2 * E], stri[:], msk[:, 1, :], start=True, stop=False)
            mm(banks[1][:, E:2 * E], ones[:], msk[:, 0, :], start=False, stop=True)
            mm(banks[2][:, 0:E], ones[:], msk[:, 0, :], start=True, stop=False)
            mm(banks[2][:, 0:E], ones[:], msk[:, 1, :], start=False, stop=True).then_inc(s["pos_full"], 1)
            pe.wait_ge(s["gate"], 1)
            for ti in range(NT):
                last = tp(banks[4][0:E, ti * P:(ti + 1) * P], gate[:, ti, :], ident[:])
            last.then_inc(s["gt_full"], 1)
            pe.wait_ge(s["gtt"], 1)
            pe.wait_ge(s["g2"], 32)
            pe.wait_ge(s["rounds"], 1)
            pe.wait_ge(s["bias"], 1)
            for ti in range(NT):
                for m in range(2):
                    b = banks[2 * ti + m][:]
                    mm(b, ident[:], xr[:, ti, 512 * m:512 * (m + 1)], start=True, stop=False)
                    mm(b, gtt[:, ti * P:(ti + 1) * P], bdn[:, 512 * m:512 * (m + 1)], start=False, stop=True)\
                        .then_inc(s["yinit"], 1)

            def gather(fill, hots, half):
                pe.wait_ge(s["x_free"], fill)
                pe.wait_ge(s["onehot"], hots)
                for c in range(4):
                    k = 4 * half + c
                    for hl in range(2):
                        for ti in range(NT):
                            last = mm(x_bank[:, c * P + hl * CAP:c * P + (hl + 1) * CAP],
                                      h2s[:, ti, hl, k * P:(k + 1) * P], onehot[:, ti, :],
                                      start=ti == 0, stop=ti == NT - 1)
                last.then_inc(s["xfill"], 1)

            def block_products(it, j, lhs):
                bank = banks[4 + j % 2][:]
                pe.wait_ge(s["bank_free"], it * PIECES + j + 1)
                pe.wait_ge(s[f"stage{expert_slot(j)}"], it * 16 + 16 * (front_loads(j) + 1))
                w = slot(NF + j, 512)

                for q in range(PAIRS):
                    n = j * PAIRS + q
                    if lhs is a_hl and q in (0, 2):
                        pe.wait_ge(s["a_hl"], it * 2 + 1 + q // 2)
                    pe.wait_ge(s["wl"], it * (PIECES * PAIRS) + n + 1)
                    for kk in range(2):
                        k = 2 * q + kk
                        mm(bank, lhs[:, k, :], wh[:, n % RING, kk, :], start=k == 0, stop=False)
                        last = mm(bank, lhs[:, k, :], wl[:, n % RING, kk, :], start=False, stop=False)
                    last.then_inc(s["pair_free"], 1)
                for k in range(DK - NAT, DK):
                    last = mm(bank, lhs[:, k, :].bitcast(F32), w[:, k, :], start=False, stop=k == DK - 1)
                last.then_inc(s["block_full"], 1)

            def merge(it, n):
                pe.wait_ge(s["bank_free"], it * PIECES + n + 3)
                if n % 2 == 0:
                    pe.wait_ge(s["t_free"], it * 2 + n // 2 + 1)
                for c in range(4):
                    o = ((n % 2) * 4 + c) * CAP
                    last = mm(t_bank[:, o:o + CAP], gu[:, n % 2, c * P:(c + 1) * P], stack_i[:], start=True, stop=True)
                last.then_inc(s["merged"], 1)

            def combine(it):
                pe.wait_ge(s["bank_free"], it * PIECES + 2)
                for ti in range(NT):
                    for m in range(2):
                        last = mm(banks[2 * ti + m][:], pgt[:, ti * P:(ti + 1) * P], ydn[:, 512 * m:512 * (m + 1)],
                                  start=False, stop=True, skip_group_check=True)
                last.then_inc(s["comb"], 1)

            def body(it, last):
                block_products(it, 0, xs)
                block_products(it, 1, xs)
                merge(it, 0)
                block_products(it, 2, xs)
                merge(it, 1)
                block_products(it, 3, xs)
                merge(it, 2)
                if not last:
                    gather(it * 3 + 3, it + 2, 0)
                merge(it, 3)
                combine(it)
                pe.wait_ge(s["x_free"], it * 3 + (3 if last else 4))
                pe.wait_ge(s["pg"], it + 1)
                for ti in range(NT):
                    tr = tp(x_bank[:, ti * P:(ti + 1) * P], pg[:, ti].rearrange("p a n -> p (a n)"), ident[:])
                tr.then_inc(s["xfill"], 1)
                if not last:
                    gather(it * 3 + 5, it + 2, 1)
                block_products(it, 4, a_hl)
                block_products(it, 5, a_hl)

            last_step = pe.value_load(rounds_i[0:1, 0:1], min_val=E - 1, max_val=ROUNDS * E - 1)
            gather(1, 1, 0)
            gather(2, 1, 1)
            with pe.Fori(0, last_step) as it:
                pe.wait_ge(s["x_free"], it * 3 + 3)
                body(it, False)
            pe.wait_ge(s["x_free"], last_step * 3 + 3)
            body(last_step, True)
            combine(last_step + 1)


def kernel(x, positions, norm1_g, w_in, nsa_q_norm_g, nsa_k_norm_g, cmp_pos_k, cmp_w1_k, cmp_w2_k,
           cmp_pos_v, cmp_w1_v, cmp_w2_v, gla_w_gate, gla_b_gate, gla_norm_g, w_out, norm2_g,
           w_router, b_router, w_gate_up, b_gate_up, w_down, b_down):
    import concourse.bacc as bacc
    from concourse.bass_utils import run_bass_kernel_spmd

    inputs = {
        "x": x, "positions": positions, "norm1_g": norm1_g, "w_in": w_in, "nsa_q_norm_g": nsa_q_norm_g,
        "nsa_k_norm_g": nsa_k_norm_g, "cmp_pos_k": cmp_pos_k, "cmp_w1_k": cmp_w1_k, "cmp_w2_k": cmp_w2_k,
        "cmp_pos_v": cmp_pos_v, "cmp_w1_v": cmp_w1_v, "cmp_w2_v": cmp_w2_v, "gla_w_gate": gla_w_gate,
        "gla_b_gate": gla_b_gate, "gla_norm_g": gla_norm_g, "w_out": w_out, "norm2_g": norm2_g,
        "w_router": w_router, "b_router": b_router, "w_gate_up": w_gate_up, "b_gate_up": b_gate_up,
        "w_down": w_down, "b_down": b_down,
    }
    nc = bacc.Bacc("TRN2", target_bir_lowering=False, num_devices=1)
    arrays = {f"in_{n}": np.ascontiguousarray(a) for n, a in inputs.items()}
    aps = [nc.dram_tensor(n, a.shape, mybir.dt.from_np(a.dtype), kind="ExternalInput").ap() for n, a in arrays.items()]
    y = nc.dram_tensor("y", (1, S, D), F32, kind="ExternalOutput").ap()
    decoder_layer(nc, *aps, y)
    result = run_bass_kernel_spmd(nc, [arrays], core_ids=[0])
    return result.results[0]["y"]
```

```python
import math
import numpy as np
import concourse.bass as bass
from concourse import mybir
from contextlib import ExitStack

F32 = mybir.dt.float32
F32R = mybir.dt.float32r
I32 = mybir.dt.int32
ALU = mybir.AluOpType
ACT = mybir.ActivationFunctionType
AX = mybir.AxisListType

P = 128
S, D = 256, 1024
NT = S // P
DK = D // P
DH = 64
HKV, G = 2, 4
HQ = HKV * G
NCMP, CST, CBL = 15, 16, 32
HID = 256
HKO = 32
NCW = HKO + NCMP
GH, DV, CH = 4, 128, 64
GTAU = 16.0
E, TOPK, FF = 32, 4, 1024
CAP = 64
ROUNDS = S // CAP
EPS = 1e-6
NEG = -1e30
SCALE = DH ** -0.5
THETA, RD = 500000.0, 16
LIMIT, ALPHA = 7.0, 1.702

IN_PIECES = [(0, 512), (512, 1024), (1024, 1304), (1304, 1816), (1816, 2328), (2328, 2856)]
NF = len(IN_PIECES) + 4
NSLOT = 6
SLOTW = [max([512] + [b - a for a, b in IN_PIECES[i::NSLOT]]) * DK for i in range(NSLOT)]
PIECES = 6
UP_COLS = [0, FF, 512, FF + 512]
UNITS = [(0, 1), (2, 3), (4, 5), (6,)]
NU = len(UNITS)
NV = NU - 1
SPLIT = sum(len(u) for u in UNITS)
RING = 2
PROJ = [("q", 0, 512), ("kv", 512, 512), ("w", 1024, 280), ("gqk", 1304, 512), ("gv", 1816, 512),
        ("glr", 2328, 16), ("gr", 2344, 512)]
GROUPS = [(br, ti, h) for br in range(2) for ti in range(NT) for h in range(HKV)]
PROJ_BANKS = [4, 5, 6, 7, 4, 5, 6, 7, 5, 6, 7, 5, 6, 7]
PT_BANKS = (2, 3)
WO_BANKS = (0, 1, 2, 3)
O_BANKS = [(5, 6), (7, 5)]
N_SMALL = 14
N_CONST = 20
FILLER = -3e38
MAGIC = 12582912.0
TWO_PI = (6.28125, 0.0019340515136718750, 2 * math.pi - 6.28125 - 0.0019340515136718750)
PI32 = 3.1415925


def decoder_layer(nc, x, positions, norm1_g, w_in, nsa_q_norm_g, nsa_k_norm_g, cmp_pos_k, cmp_w1_k, cmp_w2_k,
                  cmp_pos_v, cmp_w1_v, cmp_w2_v, gla_w_gate, gla_b_gate, gla_norm_g, w_out, norm2_g,
                  w_router, b_router, w_gate_up, b_gate_up, w_down, b_down, out):
    ctx = ExitStack()
    with ctx:
        place = [(nc.sbuf_base + 31) // 32 * 32]

        def at(name, shape, dt, offset):
            return nc.alloc_sbuf_tensor_at(name, shape, dt, offset=offset)

        def sb(name, shape, dt=F32):
            words = int(np.prod(shape[1:]))
            t = at(name, shape, dt, place[0])
            place[0] += (words * 4 + 31) // 32 * 32
            return t

        stage = [sb(f"stage{i}", [P, SLOTW[i]]) for i in range(NSLOT)]
        ident = sb("ident", [P, P])
        ones = sb("ones", [P, P])
        stack_i = sb("stack_i", [P, CAP])
        iota_i = sb("iota_i", [P, CAP], I32)
        iota_f = sb("iota_f", [P, CAP])
        posm = sb("posm", [P, NT, ROUNDS * E + 2])
        gates4 = sb("gates4", [P, NT, ROUNDS * E + 2])
        bias_t = sb("bias_t", [P, 2 * FF // P, E])
        rounds_f = sb("rounds_f", [P, 4])
        rounds_i = sb("rounds_i", [P, 1], I32)
        token = sb("token", [P, 4])
        shared = place[0]

        wh = sb("wh", [P, RING, SPLIT, 512], F32R)
        wl = sb("wl", [P, RING, SPLIT, 512], F32R)
        xs = sb("xs", [P, DK, 2 * CAP], F32R)
        gu = sb("gu", [P, 2, 512])
        hb = sb("hb", [P, 2, 4, CAP])
        sig = sb("sig", [P, 4, CAP])
        actf = sb("actf", [P, 4, CAP])
        a_hl = sb("a_hl", [P, DK, 2 * CAP], F32R)
        onehot = sb("onehot", [P, NT, CAP], F32R)
        pgr = sb("pgr", [P, NT, 2, CAP])
        pgw = sb("pgw", [P, NT, 2, CAP])
        pgt = sb("pgt", [P, S], F32R)
        gslot = sb("gslot", [P, 1])
        yh = sb("yh", [P, D], F32R)
        yl = sb("yl", [P, D], F32R)
        loop_end = place[0]

        place[0] = shared
        xr = sb("xr", [P, NT, D])
        xn_at = place[0]
        xn = sb("xn", [P, NT, D])
        xt_at = place[0]
        xt = sb("xt", [P, DK, S])
        rr = sb("rr", [P, NT, 12, DH])
        kv = sb("kv", [P, NT, 512])
        gt = sb("gt", [P, NT, 24])
        glr = sb("glr", [P, NT, 16])
        gqk = sb("gqk", [P, NT, 512])
        gv_at = place[0]
        gv = sb("gv", [P, NT, 512])
        gr = sb("gr", [P, NT, 512])
        sq_at = place[0]
        sq = sb("sq", [P, NT, 12, DH])
        qt_at = place[0]
        qt = sb("qt", [P, G, S])
        qrt = sb("qrt", [P, G, S])
        kst_at = place[0]
        kst = sb("kst", [P, 2, S])
        hid_at = place[0]
        hid = sb("hid", [NCW, 2, HID])
        hidt = sb("hidt", [P, 2, 2, NCW])
        pt_at = place[0]
        pt = sb("pt", [P, 2, 2 * G * P])
        g12 = sb("g12", [P, 12, DH])
        glag = sb("glag", [P, DV])
        wgate = sb("wgate", [17, 256])
        glrt = sb("glrt", [17, S])
        w2 = sb("w2", [P, 2, 2, DH])
        wrt = sb("wrt", [P, DK, E])
        brt = sb("brt", [P, E])
        cmask = sb("cmask", [P, 256])
        mc01 = sb("mc01", [P, NT, NCMP])
        mcneg = sb("mcneg", [P, NT, NCMP])
        tri = sb("tri", [P, P])
        blk = sb("blk", [P, P])
        stri = sb("stri", [P, P])
        gk0 = sb("gk0", [NCW, DH])
        kcn = sb("kcn", [NCW, DH])
        kcq = sb("kcq", [NCW, DH])
        vcs = sb("vcs", [NCW, DH])
        loga_at = place[0]
        loga = sb("loga", [P, NT, 256])
        eb = sb("eb", [P, NT, 256])
        en_at = place[0]
        en = sb("en", [P, NT, 256])
        es = sb("es", [P, NT, 256])
        qdt = sb("qdt", [P, 2, S])
        kdt = sb("kdt", [P, 2, S])
        ats = sb("ats", [P, 2, NT, 2, P])
        poss = sb("poss", [P, NT], I32)
        invf = sb("invf", [P, RD // 2])
        rope = sb("rope", [P, 5, NT, RD // 2])
        posl = sb("posl", [16, 2, P])
        post = sb("post", [P, 2, 16])
        kct = sb("kct", [P, NCMP])
        dect = sb("dect", [P, 2, 4])
        st = sb("st", [P, 800])
        assert place[0] <= nc.sbuf_usable_end, (place[0], nc.sbuf_usable_end)
        assert loop_end <= loga_at
        g1b = at("g1b", [P, D], F32, sq_at)
        junk = at("junk", [P, D], F32, qt_at)
        kx = at("kx", [P, 2, HKV, P], F32, xt_at)
        tb = at("tb", [P, 2, 16, NCW], F32, xt_at + 2048)
        g2b = at("g2b", [P, D], F32, xt_at)
        bdn = at("bdn", [E, D], F32, xt_at + 4096)
        pb = at("pb", [P, 2, G * S], F32, xn_at)
        ot = at("ot", [P, DK, S], F32, xn_at)
        sta = at("sta", [P, 2, 3, DV], F32, sq_at)
        sgr = at("sgr", [P, NT, 512], F32, en_at)
        gsq = at("gsq", [P, NT, 512], F32, loga_at)
        brow = at("brow", [E, 2 * FF], F32, pt_at)
        h2t = at("h2t", [P, DK, S], F32, qt_at)
        gtt = at("gtt", [E, S], F32, kst_at)
        h2 = at("h2", [P, NT, D], F32, gv_at)
        h2s = at("h2s", [P, NT, 2, D], F32R, loga_at)
        yout = at("yout", [P, NT, D], F32, loga_at)
        pcs = at("pcs", [P, NT, G, DH], F32, sq_at + 4096)
        rtmp = at("rtmp", [P, 4, 12, RD // 2], F32, hid_at)
        otmp = at("otmp", [P, G * DH], F32, sq_at + 3072)
        otmp2 = at("otmp2", [P, NT, G * DH], F32, en_at)
        osum = rr[:, :, 0:HQ, :]
        go = gqk
        qd, kd, kstate = gqk[:, :, 0:256], en, es

        banks = [ctx.enter_context(nc.psum_tensor(f"bank{i}", [P, 512], F32)) for i in range(8)]
        t_bank, x_bank = banks[6], banks[7]

        st_used = [0]

        def stc(*shape):
            n = int(np.prod(shape))
            v = st[:, st_used[0]:st_used[0] + n]
            st_used[0] += n
            if len(shape) == 2:
                v = v.rearrange("p (a b) -> p a b", b=shape[1])
            if len(shape) == 3:
                v = v.rearrange("p (a b c) -> p a b c", b=shape[1], c=shape[2])
            return v

        ms_x, rs_x, nw_x = stc(NT), stc(NT), stc(NT)
        ms_r, rs_r, nw_r = stc(NT, 12), stc(NT, 12), stc(NT, 12)
        ms_k, rs_k, nw_k = stc(1), stc(1), stc(1)
        ms_g, rs_g, nw_g = stc(NT, GH), stc(NT, GH), stc(NT, GH)
        ms_y, rs_y, nw_y = stc(NT), stc(NT), stc(NT)
        gsig = stc(NT, 24)
        cmax, cden = stc(NT, HQ), stc(NT, HQ)
        smax, sden, scoef = stc(8, G), stc(8, G), stc(8, G)
        lg, lgm = stc(NT, E + TOPK), stc(NT, E + TOPK)
        top, msk, gate, lgr = stc(NT, 8), stc(NT, E), stc(NT, E), stc(NT, E)
        gsum, ntop, cnts = stc(NT), stc(NT), stc(E)

        s = {n: ctx.enter_context(nc.semaphore("s_" + n)) for n in (
            "oc_read dec_full "
            "proj_full h_full wo_full x g1 rounds block_full wl wl_pool yout out const hid g2 pv_full brow small act rope "
            "sin xt_full xt proj kx_full kx post_full post qt_full qt glrt_full glrt z_full absz e1 qr_full qrt "
            "sigh b_full bexp dec esd es ht_full hidt qdt_full qdt kct_full kct u_full sgr csub cexp pct_full pct "
            "pt_full pts nmax pexp ot_full ot h2 h2hi h2t_full h2t bias_full bias ntop gexp gt_full gtt unit_free "
            "wh xfill x_free merged gu comb hb yh yl sigm actf ahi dve ms_x xn ms_r rn tb qr_ready loga qd "
            "kc_full kcn ms_k at_full ats sta o_full go ms_g glaout cs_full csc pc oc_full osum_c sc_full soft "
            "pv_read osum x1 ms_y h2s rt_full msk gate pos_full t_free loopdve a_hl onehot pgr pgw gslot yinit rs_x rs_r "
            "rs_k rs_g rs_y stage0 stage1 stage2 stage3 stage4 stage5 ").split()}

        def split_k(w):
            return w.rearrange("(k p) n -> p k n", p=P)

        def slot(i, width):
            return stage[i % NSLOT][:, 0:DK * width].rearrange("p (k n) -> p k n", k=DK)

        def front_slot(i):
            if i < len(IN_PIECES):
                return slot(i, IN_PIECES[i][1] - IN_PIECES[i][0])
            return slot(i, 512)

        def comp_slot(i):
            return stage[i % NSLOT][:, 0:16 * HID].rearrange("p (k n) -> p k n", k=16)

        def front_arrived(eng, i):
            eng.wait_ge(s[f"stage{i % NSLOT}"], 16 * (i // NSLOT + 1))

        def expert_slot(j):
            return (NF + j) % NSLOT

        def front_loads(j):
            return len(range(expert_slot(j), NF, NSLOT))

        def bc(ap, n):
            return ap.unsqueeze(len(ap.shape)).to_broadcast(list(ap.shape) + [n])

        w_up_v = w_gate_up[0].rearrange("e (k p) n -> p e k n", p=P)
        w_dn_v = w_down[0].rearrange("e (k p) n -> p e k n", p=P)

        def expert_source(e, j):
            if j < 4:
                return w_up_v[:, e, :, UP_COLS[j]:UP_COLS[j] + 512]
            return w_dn_v[:, e, :, 512 * (j - 4):512 * (j - 3)]

        def front_used(eng, i):
            if i < len(IN_PIECES):
                eng.wait_ge(s["proj_full"], NT * (i + 1 + (i == len(IN_PIECES) - 1)))
            elif i < len(IN_PIECES) + 2:
                eng.wait_ge(s["h_full"], i - len(IN_PIECES) + 1)
            else:
                eng.wait_ge(s["wo_full"], NT * (i - len(IN_PIECES) - 1))

        block = ctx.enter_context(nc.Block())

        @block.sync
        def _(sp):
            for ti in range(NT):
                sp.dma_start(xr[:, ti, :], x[0, ti * P:(ti + 1) * P, :]).then_inc(s["x"], 16)
            sp.dma_start(g1b[:], norm1_g[0].partition_broadcast(P)).then_inc(s["g1"], 16)
            for i in range(NF):
                if i == 2:
                    sp.wait_ge(s["small"], 16 * N_SMALL)
                if i >= NSLOT:
                    front_used(sp, i - NSLOT)
                if i < len(IN_PIECES):
                    src, dst = split_k(w_in[0])[:, :, IN_PIECES[i][0]:IN_PIECES[i][1]], front_slot(i)
                elif i < len(IN_PIECES) + 2:
                    src = split_k((cmp_w1_k, cmp_w1_v)[i - len(IN_PIECES)][0])
                    dst = comp_slot(i)
                else:
                    m = i - len(IN_PIECES) - 2
                    src, dst = split_k(w_out[0])[:, :, 512 * m:512 * (m + 1)], front_slot(i)
                sp.dma_start(dst, src).then_inc(s[f"stage{i % NSLOT}"], 16)
            for j in range(PIECES):
                front_used(sp, NF + j - NSLOT)
                sp.dma_start(slot(NF + j, 512), expert_source(0, j)).then_inc(s[f"stage{expert_slot(j)}"], 16)
            sp.wait_ge(s["rounds"], 1)
            last_step = sp.value_load(rounds_i[0:1, 0:1], min_val=E - 1, max_val=ROUNDS * E - 1)
            with sp.Fori(1, last_step + 1) as it:
                expert = sp.snap(it % E, min_val=0, max_val=E - 1)
                for j in range(PIECES):
                    sp.wait_ge(s["block_full"], it * PIECES + (j + 1 - PIECES))
                    sp.dma_start(slot(NF + j, 512), expert_source(expert, j)).then_inc(s[f"stage{expert_slot(j)}"], 16)
            for ti in range(NT):
                sp.wait_ge(s["yout"], 2 * (ti + 1))
                sp.dma_start(out[0, ti * P:(ti + 1) * P, :], yout[:, ti, :]).then_inc(s["out"], 16)
            sp.wait_ge(s["out"], 16 * NT)

        @block.gpsimd
        def _(pool):
            c = [0]

            def step(ins):
                c[0] += 1
                ins.then_inc(s["const"], 1)
                pool.wait_ge(s["const"], c[0])

            def select(t, compare_op, fill, base, pattern, mult):
                step(nc.gpsimd.affine_select(out=t, in_=t, compare_op=compare_op, fill=fill, base=base,
                                             pattern=pattern, channel_multiplier=mult))

            step(nc.gpsimd.memset(ident[:], 0.0))
            select(ident[:], ALU.not_equal, 1.0, 0, [[-1, P]], 1)
            small = [
                (poss[:], positions[0].rearrange("(t p) -> p t", p=P)),
                (g12[:, 0:HQ, :], nsa_q_norm_g[0:1, :].partition_broadcast(P).to_broadcast([P, HQ, DH])),
                (g12[:, HQ:HQ + 2, :], nsa_k_norm_g[0, 1:2, :].partition_broadcast(P).to_broadcast([P, 2, DH])),
                (g12[:, HQ + 2:HQ + 4, :], nsa_k_norm_g[0, 2:3, :].partition_broadcast(P).to_broadcast([P, 2, DH])),
                (gk0[:], nsa_k_norm_g[0, 0, :].partition_broadcast(NCW)),
                (glag[:], gla_norm_g[0].partition_broadcast(P)),
                (wgate[0:16, :], gla_w_gate[0]),
                (wgate[16:17, :], gla_b_gate[0:1, :]),
                (posl[:, 0, :], cmp_pos_k[0].rearrange("(c i) d -> c (i d)", i=2)),
                (posl[:, 1, :], cmp_pos_v[0].rearrange("(c i) d -> c (i d)", i=2)),
                (w2[:, 0, :, :], split_k(cmp_w2_k[0])),
                (w2[:, 1, :, :], split_k(cmp_w2_v[0])),
                (wrt[:], split_k(w_router[0])),
                (brt[:], b_router[0].partition_broadcast(P)),
            ]
            for dst, src in small:
                pool.dma_start(dst, src, allow_slow_non_contiguous=True).then_inc(s["small"], 16)
            assert len(small) == N_SMALL
            step(nc.gpsimd.memset(glrt[:], 1.0))
            step(nc.gpsimd.memset(ones[:], 1.0))
            step(nc.gpsimd.memset(stack_i[:], 0.0))
            select(stack_i[:], ALU.not_equal, 1.0, 0, [[-1, CAP]], 1)
            select(stack_i[:], ALU.not_equal, 1.0, -CAP, [[-1, CAP]], 1)
            step(nc.gpsimd.memset(cmask[:], 0.0))
            select(cmask[:], ALU.is_ge, NEG, P, [[-1, 2 * P]], 1)
            step(nc.gpsimd.memset(mc01[:], 1.0))
            select(mc01[:], ALU.is_ge, 0.0, 1 - CBL, [[P, NT], [-CST, NCMP]], 1)
            step(nc.gpsimd.memset(tri[:], 1.0))
            select(tri[:], ALU.is_ge, 0.0, 0, [[1, P]], -1)
            step(nc.gpsimd.memset(tri[0:CH, CH:P], 0.0))
            step(nc.gpsimd.memset(blk[:], 0.0))
            step(nc.gpsimd.memset(blk[0:CH, 0:CH], 1.0))
            step(nc.gpsimd.memset(blk[CH:P, CH:P], 1.0))
            step(nc.gpsimd.memset(stri[:], 1.0))
            select(stri[:], ALU.is_gt, 0.0, 0, [[1, P]], -1)
            step(nc.gpsimd.iota(iota_i[:], [[1, CAP]], base=0, channel_multiplier=0))
            assert c[0] == N_CONST, c[0]
            pool.wait_ge(s["hid"], 2)
            pool.dma_start(g2b[:], norm2_g[0].partition_broadcast(P)).then_inc(s["g2"], 16)
            pool.dma_start(bdn[:], b_down[0]).then_inc(s["g2"], 16)
            pool.wait_ge(s["oc_full"], 2)
            pool.dma_start(brow[:], b_gate_up[0]).then_inc(s["brow"], 16)

            def split_low(it, j):
                ks = UNITS[-1]
                pool.wait_ge(s["wh"], it * (PIECES * NU) + (j + 1) * NU)
                nc.gpsimd.tensor_tensor(wl[:, j % RING, ks[0]:ks[-1] + 1, :], slot(NF + j, 512)[:, ks[0]:ks[-1] + 1, :],
                                        wh[:, j % RING, ks[0]:ks[-1] + 1, :].bitcast(F32), ALU.subtract)\
                    .then_inc(s["wl_pool"], 1)

            pool.wait_ge(s["rounds"], 1)
            last_step = pool.value_load(rounds_i[0:1, 0:1], min_val=E - 1, max_val=ROUNDS * E - 1)
            with pool.Fori(0, last_step + 1) as it:
                for j in range(PIECES):
                    split_low(it, j)

        @block.scalar
        def _(act):
            n_act = [0]

            def rstd(what, a, r):
                act.wait_ge(s["ms_" + what], 1)
                link(nc.scalar.activation(r, a, ACT.Ln))
                nc.scalar.activation(r, r, ACT.Exp, scale=-0.5).then_inc(s["rs_" + what], 1)

            def link(ins):
                n_act[0] += 1
                ins.then_inc(s["act"], 1)
                act.wait_ge(s["act"], n_act[0])

            rstd("x", ms_x, rs_x)
            for q in range(4):
                act.wait_ge(s["xt_full"], q + 1)
                ti, half = q // 2, q % 2
                nc.scalar.copy(xt[:, 4 * half:4 * half + 4, ti * P:(ti + 1) * P],
                               banks[q][:].rearrange("p (k t) -> p k t", k=4)).then_inc(s["xt"], 1)
            def proj_evac(first, end):
                n = 0
                for name, c0, width in PROJ:
                    for ti in range(NT):
                        if first <= n < end:
                            evac_one(n, name, width, ti)
                        n += 1

            def evac_one(n, name, width, ti):
                b = banks[PROJ_BANKS[n]]
                act.wait_ge(s["proj_full"], n + 1)
                if name == "q":
                    last = nc.scalar.copy(rr[:, ti, 0:HQ, :].rearrange("p (g h) d -> p h g d", h=HKV),
                                          b[:, 0:512].rearrange("p (h g d) -> p h g d", h=HKV, g=G))
                elif name == "kv":
                    nc.scalar.copy(kv[:, ti, 0:256], b[:, 0:256])
                    nc.scalar.copy(rr[:, ti, HQ:HQ + 2, :], b[:, 256:384].rearrange("p (h d) -> p h d", h=2))
                    last = nc.scalar.copy(kv[:, ti, 256:384], b[:, 384:512])
                elif name == "w":
                    nc.scalar.copy(rr[:, ti, HQ + 2:HQ + 4, :], b[:, 0:128].rearrange("p (h d) -> p h d", h=2))
                    nc.scalar.copy(kv[:, ti, 384:512], b[:, 128:256])
                    last = nc.scalar.copy(gt[:, ti, :], b[:, 256:280])
                else:
                    dst = {"gqk": gqk, "gv": gv, "glr": glr, "gr": gr}[name]
                    last = nc.scalar.copy(dst[:, ti, :], b[:, 0:width])
                last.then_inc(s["proj"], 1)

            def evac_pt(i):
                act.wait_ge(s["pt_full"], i + 1)
                for k in range(GROUPS[i][1] + 1):
                    last = nc.scalar.copy(pt[:, (i + 1) % 2, k * 512:(k + 1) * 512], banks[PT_BANKS[k]][:])
                last.then_inc(s["pts"], 1)

            def exps(i):
                br, ti, h = GROUPS[i]
                keys = P * (ti + 1)
                act.wait_ge(s["nmax"], i + 1)
                for g in range(G):
                    v = pb[:, i % 2, g * keys:(g + 1) * keys]
                    nc.scalar.activation(v, v, ACT.Exp, bias=smax[:, i, g:g + 1], scale=SCALE,
                                         accum_out=sden[:, i, g:g + 1]).then_inc(s["pexp"], 1)

            def hidden(c):
                act.wait_ge(s["h_full"], c + 1)
                nc.scalar.activation(hid[:, c, :], banks[6 + c][0:NCW, 0:HID], ACT.Sigmoid).then_inc(s["sigh"], 1)

            proj_evac(0, 4)
            act.wait_ge(s["rope"], 1)
            nc.scalar.activation(rope[:, 2, :, :], rope[:, 0, :, :], ACT.Sin)
            nc.scalar.activation(rope[:, 3, :, :], rope[:, 0, :, :], ACT.Sin, scale=0.5).then_inc(s["sin"], 1)
            proj_evac(4, 6)
            act.wait_ge(s["proj"], 6)
            nc.scalar.activation(gsig, gt[:], ACT.Sigmoid)
            rstd("r", ms_r, rs_r)
            proj_evac(6, 8)
            for ti in range(NT):
                act.wait_ge(s["qt_full"], ti + 1)
                nc.scalar.copy(qt[:, :, ti * P:(ti + 1) * P], banks[2 + ti][:].rearrange("p (g t) -> p g t", g=G))\
                    .then_inc(s["qt"], 1)
            for q in range(3):
                act.wait_ge(s["qr_full"], q + 1)
                if q < 2:
                    nc.scalar.copy(qrt[:, :, q * P:(q + 1) * P], banks[q][:].rearrange("p (g t) -> p g t", g=G))\
                        .then_inc(s["qrt"], 1)
                else:
                    nc.scalar.copy(kst[:], banks[4][:].rearrange("p (b t) -> p b t", b=2)).then_inc(s["qrt"], 1)
            exps(0)
            proj_evac(8, 10)
            evac_pt(0)
            exps(1)
            proj_evac(10, 13)
            evac_pt(1)
            exps(2)
            proj_evac(13, 14)
            act.wait_ge(s["kx_full"], 1)
            kvt = banks[5][:].rearrange("p (c t i) -> p c t i", c=2, i=2)
            for i in range(2):
                for h in range(HKV):
                    nc.scalar.copy(kx[i * DH:(i + 1) * DH, :, h, :], kvt[h * DH:(h + 1) * DH, :, :, i])\
                        .then_inc(s["kx"], 1)
            act.wait_ge(s["post_full"], 1)
            nc.scalar.copy(post[:], banks[6][:, 0:32].rearrange("p (c k) -> p c k", c=2)).then_inc(s["post"], 1)
            evac_pt(2)
            exps(3)
            act.wait_ge(s["glrt_full"], 1)
            nc.scalar.copy(glrt[0:16, :], banks[7][0:16, 0:S]).then_inc(s["glrt"], 1)
            act.wait_ge(s["z_full"], 1)
            z = banks[5][:].rearrange("p (t n) -> p t n", t=NT)
            nc.scalar.activation(en[:], z, ACT.Abs).then_inc(s["absz"], 1)
            act.wait_ge(s["absz"], 1)
            link(nc.scalar.activation(en[:], en[:], ACT.Exp, scale=-1.0))
            nc.scalar.activation(en[:], en[:], ACT.Ln, bias=1.0).then_inc(s["e1"], 1)
            hidden(0)
            evac_pt(3)
            exps(4)
            hidden(1)
            act.wait_ge(s["b_full"], 1)
            b = banks[5][:].rearrange("p (t n) -> p t n", t=NT)
            nc.scalar.activation(eb[:], b, ACT.Exp)
            nc.scalar.activation(en[:], b, ACT.Exp, scale=-1.0).then_inc(s["bexp"], 1)
            evac_pt(4)
            exps(5)
            act.wait_ge(s["esd"], 1)
            nc.scalar.activation(es[:], es[:], ACT.Exp).then_inc(s["es"], 1)
            act.wait_ge(s["dec_full"], 1)
            nc.scalar.activation(dect[:], banks[7][:, 0:8].rearrange("p (h c) -> p h c", h=2), ACT.Exp)\
                .then_inc(s["dec"], 1)
            for t, b in ((qdt, banks[5]), (kdt, banks[6])):
                act.wait_ge(s["qdt_full"], 1 if t is qdt else 2)
                nc.scalar.copy(t[:], b[:].rearrange("p (h t) -> p h t", h=2)).then_inc(s["qdt"], 1)
            act.wait_ge(s["ht_full"], 1)
            nc.scalar.copy(hidt[:], banks[7][:, 0:4 * NCW].rearrange("p (c k n) -> p c k n", c=2, k=2))\
                .then_inc(s["hidt"], 1)
            evac_pt(5)
            exps(6)
            rstd("k", ms_k[0:NCW, :], rs_k[0:NCW, :])
            evac_pt(6)
            exps(7)
            act.wait_ge(s["kct_full"], 1)
            nc.scalar.copy(kct[0:DH, :], banks[7][0:DH, 0:NCMP])
            nc.scalar.copy(kct[DH:P, :], banks[7][0:DH, HKO:NCW]).then_inc(s["kct"], 1)
            evac_pt(7)
            act.wait_ge(s["u_full"], 3)
            nc.scalar.activation(sgr[:], gr[:], ACT.Sigmoid).then_inc(s["sgr"], 1)
            rstd("g", ms_g, rs_g)
            act.wait_ge(s["csub"], 1)
            for h in range(HKV):
                v = pcs[:, :, :, h * HKO:h * HKO + NCMP]
                nc.scalar.activation(v, v, ACT.Exp, scale=SCALE).then_inc(s["cexp"], 1)
            for ti in range(NT):
                act.wait_ge(s["pct_full"], ti + 1)
                nc.scalar.copy(pt[0:DH, 0, ti * 512:(ti + 1) * 512], banks[PT_BANKS[ti]][0:DH, :]).then_inc(s["pct"], 1)
            for q in range(4):
                act.wait_ge(s["ot_full"], q + 1)
                nc.scalar.copy(ot[:, 2 * q:2 * q + 2, :], banks[4 + q][:].rearrange("p (k t) -> p k t", k=2))\
                    .then_inc(s["ot"], 1)
            rstd("y", ms_y, rs_y)
            for ti in range(NT):
                act.wait_ge(s["h2"], ti + 1)
                nc.scalar.copy(h2s[:, ti, 0, :], h2[:, ti, :]).then_inc(s["h2hi"], 1)
            for q in range(4):
                act.wait_ge(s["h2t_full"], q + 1)
                nc.scalar.copy(h2t[:, 2 * q:2 * q + 2, :], banks[4 + q][:].rearrange("p (k t) -> p k t", k=2))\
                    .then_inc(s["h2t"], 1)
            act.wait_ge(s["bias_full"], 1)
            nc.scalar.copy(bias_t[:], banks[0][:].rearrange("p (k e) -> p k e", e=E)).then_inc(s["bias"], 1)
            act.wait_ge(s["ntop"], 1)
            nc.scalar.activation(gate, lgr, ACT.Exp).then_inc(s["gexp"], 1)
            act.wait_ge(s["gt_full"], 1)
            nc.scalar.copy(gtt[:], banks[4][0:E, 0:S]).then_inc(s["gtt"], 1)

            def split_high(it, j):
                act.wait_ge(s[f"stage{expert_slot(j)}"], it * 16 + 16 * (front_loads(j) + 1))
                for q, ks in enumerate(UNITS):
                    act.wait_ge(s["unit_free"], it * (PIECES * NU) + j * NU + q + 1)
                    nc.scalar.copy(wh[:, j % RING, ks[0]:ks[-1] + 1, :], slot(NF + j, 512)[:, ks[0]:ks[-1] + 1, :])\
                        .then_inc(s["wh"], 1)

            def gather_evac(fill, half):
                act.wait_ge(s["xfill"], fill)
                nc.scalar.copy(xs[:, 4 * half:4 * half + 4, :], x_bank[:].rearrange("p (k n) -> p k n", k=4))\
                    .then_inc(s["x_free"], 1)

            def up_evac(it, n):
                act.wait_ge(s["block_full"], it * PIECES + n + 1)
                act.wait_ge(s["merged"], it * 4 + n + 1)
                nc.scalar.copy(gu[:, n % 2, :], banks[4 + n % 2][:]).then_inc(s["gu"], 1)

            def down_high(it, m):
                act.wait_ge(s["block_full"], it * PIECES + 5 + m)
                act.wait_ge(s["comb"], it * NT + NT)
                act.wait_ge(s["gslot"], it + 1)
                nc.scalar.activation(yh[:, 512 * m:512 * (m + 1)], banks[4 + m][:], ACT.Copy, scale=gslot[:])\
                    .then_inc(s["yh"], 1)

            def act_half(it, hf):
                act.wait_ge(s["hb"], it * 2 + hf + 1)
                nc.scalar.activation(sig[:], hb[:, 0, :, :], ACT.Sigmoid, scale=ALPHA).then_inc(s["sigm"], 1)
                act.wait_ge(s["actf"], it * 2 + hf + 1)
                nc.scalar.copy(a_hl[:, 4 * hf:4 * hf + 4, 0:CAP], actf[:]).then_inc(s["ahi"], 1)

            def body(it, last):
                split_high(it, 2)
                up_evac(it, 0)
                split_high(it, 3)
                up_evac(it, 1)
                split_high(it, 4)
                up_evac(it, 2)
                act_half(it, 0)
                split_high(it, 5)
                up_evac(it, 3)
                if not last:
                    gather_evac(it * 3 + 3, 0)
                act_half(it, 1)
                if not last:
                    gather_evac(it * 3 + 4, 1)
                act.wait_ge(s["xfill"], it * 3 + (3 if last else 5))
                act.wait_ge(s["yl"], it * 2 + 2)
                nc.scalar.copy(gslot[:], x_bank[:, S:S + 1]).then_inc(s["gslot"], 1)
                nc.scalar.copy(pgt[:], x_bank[:, 0:S]).then_inc(s["x_free"], 1)
                if not last:
                    split_high(it + 1, 0)
                down_high(it, 0)
                if not last:
                    split_high(it + 1, 1)
                down_high(it, 1)

            act.wait_ge(s["rounds"], 1)
            last_step = act.value_load(rounds_i[0:1, 0:1], min_val=E - 1, max_val=ROUNDS * E - 1)
            gather_evac(1, 0)
            gather_evac(2, 1)
            split_high(0, 0)
            split_high(0, 1)
            with act.Fori(0, last_step) as it:
                body(it, False)
            body(last_step, True)

        @block.vector
        def _(dve):
            n_dve = [0]
            V = nc.vector

            def link(ins):
                n_dve[0] += 1
                ins.then_inc(s["dve"], 1)
                dve.wait_ge(s["dve"], n_dve[0])

            def newton(what, a, r, w):
                dve.wait_ge(s["rs_" + what], 1)
                link(V.tensor_tensor(w, r, r, ALU.mult))
                link(V.tensor_tensor(w, w, a, ALU.mult))
                link(V.tensor_scalar(w, w, -0.5, 1.5, ALU.mult, ALU.add))
                link(V.tensor_tensor(r, r, w, ALU.mult))

            dve.wait_ge(s["x"], 16 * NT)
            for ti in range(NT):
                link(V.tensor_tensor_reduce(out=junk[:], in0=xr[:, ti, :], in1=xr[:, ti, :], scale=1.0, scalar=0.0,
                                            op0=ALU.mult, op1=ALU.add, accum_out=ms_x[:, ti:ti + 1]))
            V.tensor_scalar(ms_x, ms_x, 1.0 / D, EPS, ALU.mult, ALU.add).then_inc(s["ms_x"], 1)
            dve.wait_ge(s["ms_x"], 1)
            newton("x", ms_x, rs_x, nw_x)
            dve.wait_ge(s["g1"], 16)
            for ti in range(NT):
                V.scalar_tensor_tensor(out=xn[:, ti, :], in0=xr[:, ti, :], scalar=rs_x[:, ti:ti + 1], in1=g1b[:],
                                       op0=ALU.mult, op1=ALU.mult).then_inc(s["xn"], 1)
            for i in range(RD // 2):
                last = V.memset(invf[:, i:i + 1], float(np.exp(np.float32(-math.log(THETA)) * np.float32(2 * i) / np.float32(RD))))
            link(last)
            dve.wait_ge(s["small"], 16 * N_SMALL)
            posf = rope[:, 4, 0, 0:NT]
            link(V.tensor_copy(posf, poss[:]))
            link(V.tensor_tensor(rope[:, 0, :, :], bc(posf, RD // 2),
                                 invf[:].unsqueeze(1).to_broadcast([P, NT, RD // 2]), ALU.mult))
            link(V.tensor_scalar(rope[:, 1, :, :], rope[:, 0, :, :], 1 / (2 * math.pi), MAGIC, ALU.mult, ALU.add))
            link(V.tensor_scalar(rope[:, 1, :, :], rope[:, 1, :, :], -MAGIC, None, ALU.add))
            for c in TWO_PI:
                link(V.scalar_tensor_tensor(out=rope[:, 0, :, :], in0=rope[:, 1, :, :], scalar=-c,
                                            in1=rope[:, 0, :, :], op0=ALU.mult, op1=ALU.add))
            V.tensor_scalar(rope[:, 0, :, :], rope[:, 0, :, :], PI32, -PI32, ALU.min, ALU.max).then_inc(s["rope"], 1)
            dve.wait_ge(s["const"], N_CONST)
            V.tensor_copy(iota_f[:], iota_i[:])
            link(V.tensor_scalar(mcneg[:], mc01[:], 1.0, -NEG, ALU.subtract, ALU.mult))
            dve.wait_ge(s["proj"], 6)
            dve.wait_ge(s["xn"], NT)
            link(V.tensor_tensor(sq[:], rr[:], rr[:], ALU.mult))
            link(V.tensor_reduce(ms_r, sq[:], AX.X, ALU.add))
            V.tensor_scalar(ms_r, ms_r, 1.0 / DH, EPS, ALU.mult, ALU.add).then_inc(s["ms_r"], 1)
            dve.wait_ge(s["ms_r"], 1)
            dve.wait_ge(s["sin"], 1)
            link(V.tensor_tensor(rope[:, 3, :, :], rope[:, 3, :, :], rope[:, 3, :, :], ALU.mult))
            link(V.tensor_scalar(rope[:, 3, :, :], rope[:, 3, :, :], -2.0, 1.0, ALU.mult, ALU.add))
            newton("r", ms_r, rs_r, nw_r)
            link(V.tensor_tensor(rr[:], rr[:], bc(rs_r, DH), ALU.mult))
            for ti in range(NT):
                V.tensor_tensor(rr[:, ti, :, :], rr[:, ti, :, :], g12[:], ALU.mult).then_inc(s["rn"], 1)
            dve.wait_ge(s["rn"], NT)
            dve.wait_ge(s["qt_full"], NT)
            for ti in range(NT):
                sin = rope[:, 2, ti, :].unsqueeze(1).to_broadcast([P, 12, RD // 2])
                cos = rope[:, 3, ti, :].unsqueeze(1).to_broadcast([P, 12, RD // 2])
                lo, hi = rr[:, ti, :, 0:RD // 2], rr[:, ti, :, RD // 2:RD]
                if ti:
                    dve.wait_ge(s["qr_ready"], 2 * ti)
                V.tensor_tensor(rtmp[:, 0], lo, cos, ALU.mult)
                V.tensor_tensor(rtmp[:, 1], hi, sin, ALU.mult)
                V.tensor_tensor(rtmp[:, 2], hi, cos, ALU.mult)
                link(V.tensor_tensor(rtmp[:, 3], lo, sin, ALU.mult))
                V.tensor_tensor(lo, rtmp[:, 0], rtmp[:, 1], ALU.subtract).then_inc(s["qr_ready"], 1)
                V.tensor_tensor(hi, rtmp[:, 2], rtmp[:, 3], ALU.add).then_inc(s["qr_ready"], 1)
            def silu_hidden(c):
                dve.wait_ge(s["sigh"], c + 1)
                V.tensor_tensor(hid[:, c, :], banks[6 + c][0:NCW, 0:HID], hid[:, c, :], ALU.mult).then_inc(s["hid"], 1)

            gates = gsig.rearrange("p t (h b) -> p t h b", b=3)
            n_soft = [0]

            def soft(i):
                br, ti, h = GROUPS[i]
                keys = P * (ti + 1)
                dve.wait_ge(s["sc_full"], i + 1)
                mask = cmask[:, 2 * P - keys:2 * P] if ti == 0 else cmask[:]
                per = 512 // keys
                for b in range(G // per):
                    V.tensor_tensor(pb[:, i % 2, b * 512:b * 512 + 512].rearrange("p (g k) -> p g k", g=per),
                                    banks[b][:].rearrange("p (g k) -> p g k", g=per),
                                    mask.unsqueeze(1).to_broadcast([P, per, keys]), ALU.add).then_inc(s["soft"], 1)
                n_soft[0] += G // per
                dve.wait_ge(s["soft"], n_soft[0])
                link(V.reduce_max(smax[:, i, :], pb[:, i % 2, 0:G * keys].rearrange("p (g k) -> p g k", g=G), AX.X))
                V.tensor_scalar(smax[:, i, :], smax[:, i, :], -SCALE, None, ALU.mult).then_inc(s["nmax"], 1)

            def gather_out(i):
                br, ti, h = GROUPS[i]
                dve.wait_ge(s["pexp"], G * (i + 1))
                link(V.reciprocal(scoef[:, i, :], sden[:, i, :]))
                link(V.tensor_tensor(scoef[:, i, :], scoef[:, i, :], gates[:, ti, h * G:(h + 1) * G, 1 + br], ALU.mult))
                dve.wait_ge(s["pv_full"], i + 1)
                o = osum[:, ti, h * G:(h + 1) * G, :]
                pv = banks[4][:, 0:256].rearrange("p (g d) -> p g d", g=G)
                if br == 0:
                    V.tensor_tensor(o, pv, bc(scoef[:, i, :], DH), ALU.mult).then_inc(s["pv_read"], 1)
                else:
                    tmp = otmp[:].rearrange("p (g d) -> p g d", g=G)
                    V.tensor_tensor(tmp, pv, bc(scoef[:, i, :], DH), ALU.mult).then_inc(s["pv_read"], 1)
                    dve.wait_ge(s["pv_read"], i + 1)
                    link(V.tensor_tensor(o, o, tmp, ALU.add))

            soft(0)
            dve.wait_ge(s["qr_full"], 3)
            soft(1)
            gather_out(0)
            soft(2)
            gather_out(1)
            dve.wait_ge(s["kx"], 4)
            dve.wait_ge(s["post"], 1)
            for c in range(2):
                V.memset(tb[:, c, :, NCMP:HKO], 0.0)
                for h in range(HKV):
                    steps_of = kx[:, c, h, :].rearrange("p (n k) -> p k n", k=8)
                    for half in range(2):
                        k8 = slice(8 * half, 8 * half + 8)
                        V.tensor_tensor(tb[:, c, k8, h * HKO:h * HKO + NCMP], steps_of[:, :, half:half + NCMP],
                                        bc(post[:, c, k8], NCMP), ALU.add).then_inc(s["tb"], 1)
            soft(3)
            gather_out(2)
            z = banks[5][:].rearrange("p (t n) -> p t n", t=NT)
            dve.wait_ge(s["absz"], 1)
            link(V.tensor_scalar(loga[:], z, 0.0, None, ALU.min))
            dve.wait_ge(s["e1"], 1)
            link(V.tensor_tensor(loga[:], loga[:], en[:], ALU.subtract))
            V.tensor_scalar(loga[:], loga[:], 1.0 / GTAU, None, ALU.mult).then_inc(s["loga"], 1)
            silu_hidden(0)
            soft(4)
            gather_out(3)
            silu_hidden(1)
            dve.wait_ge(s["bexp"], 1)
            link(V.tensor_copy(es[:], banks[6][:].rearrange("p (t n) -> p t n", t=NT)))
            V.tensor_tensor(es[:], es[:], banks[5][:].rearrange("p (t n) -> p t n", t=NT), ALU.subtract)\
                .then_inc(s["esd"], 1)
            V.tensor_tensor(kd[:], gqk[:, :, 256:512], en[:], ALU.mult)
            V.scalar_tensor_tensor(out=qd, in0=qd, scalar=SCALE, in1=eb[:], op0=ALU.mult, op1=ALU.mult)\
                .then_inc(s["qd"], 1)
            soft(5)
            gather_out(4)
            dve.wait_ge(s["es"], 1)
            V.tensor_tensor(kstate[:], gqk[:, :, 256:512], es[:], ALU.mult).then_inc(s["qd"], 1)
            soft(6)
            gather_out(5)
            for par in range(2):
                dve.wait_ge(s["at_full"], par + 1)
                V.tensor_tensor(ats[:, par].rearrange("p t h n -> p (t h) n"),
                                banks[5 + par][:].rearrange("p (a n) -> p a n", a=4),
                                tri[:].unsqueeze(1).to_broadcast([P, 4, P]), ALU.mult).then_inc(s["ats"], 1)
            dve.wait_ge(s["kc_full"], 1)
            link(V.tensor_copy(kcn[:], banks[7][0:NCW, 0:DH]))
            V.tensor_copy(vcs[:], banks[7][0:NCW, DH:2 * DH]).then_inc(s["kcn"], 1)
            link(V.tensor_tensor(kcq[:], kcn[:], kcn[:], ALU.mult))
            link(V.reduce_sum(ms_k[0:NCW, :], kcq[:], AX.X))
            V.tensor_scalar(ms_k[0:NCW, :], ms_k[0:NCW, :], 1.0 / DH, EPS, ALU.mult, ALU.add).then_inc(s["ms_k"], 1)
            dve.wait_ge(s["ms_k"], 1)
            newton("k", ms_k[0:NCW, :], rs_k[0:NCW, :], nw_k[0:NCW, :])
            V.scalar_tensor_tensor(out=kcn[:], in0=kcn[:], scalar=rs_k[0:NCW, :], in1=gk0[:],
                                   op0=ALU.mult, op1=ALU.mult).then_inc(s["kcn"], 1)
            soft(7)
            gather_out(6)
            for ci in range(3):
                dve.wait_ge(s["u_full"], ci + 1)
                if ci == 1:
                    dve.wait_ge(s["dec"], 1)
                for hp in range(2):
                    for par in range(2):
                        u = banks[5 + ci][par * 64:par * 64 + 64, hp * 256 + par * DV:hp * 256 + par * DV + DV]
                        dst = sta[par * 64:par * 64 + 64, hp, :, :]
                        if ci == 0:
                            last = V.tensor_copy(dst[:, 0, :], u)
                        else:
                            last = V.scalar_tensor_tensor(out=dst[:, ci, :], in0=dst[:, ci - 1, :],
                                                          scalar=dect[par * 64:par * 64 + 64, hp, ci:ci + 1], in1=u,
                                                          op0=ALU.mult, op1=ALU.add)
                last.then_inc(s["sta"], 1)
                dve.wait_ge(s["sta"], ci + 1)
            gather_out(7)
            dve.wait_ge(s["sgr"], 1)
            link(V.tensor_tensor(gr[:], gr[:], sgr[:], ALU.mult))
            for ti in range(NT):
                for par in range(2):
                    dve.wait_ge(s["o_full"], 2 * ti + par + 1)
                    V.tensor_copy(go[:, ti, :].rearrange("p (h r d) -> p h r d", h=2, r=2)[:, :, par, :],
                                  banks[O_BANKS[ti][par]][:, 0:2 * DV].rearrange("p (h d) -> p h d", h=2))\
                        .then_inc(s["go"], 1)
            dve.wait_ge(s["go"], 2 * NT)
            link(V.tensor_tensor(gsq[:], go[:], go[:], ALU.mult))
            link(V.tensor_reduce(ms_g, gsq[:].rearrange("p t (h d) -> p t h d", h=GH), AX.X, ALU.add))
            V.tensor_scalar(ms_g, ms_g, 1.0 / DV, EPS, ALU.mult, ALU.add).then_inc(s["ms_g"], 1)
            dve.wait_ge(s["ms_g"], 1)
            newton("g", ms_g, rs_g, nw_g)
            go4 = go[:].rearrange("p t (h d) -> p (t h) d", h=GH)
            link(V.tensor_tensor(go4, go4, bc(rs_g.rearrange("p t h -> p (t h)"), DV), ALU.mult))
            link(V.tensor_tensor(go4, go4, glag[:].unsqueeze(1).to_broadcast([P, NT * GH, DV]), ALU.mult))
            V.tensor_tensor(go[:], go[:], gr[:], ALU.mult).then_inc(s["glaout"], 1)
            link(V.memset(pcs[:], 0.0))
            dve.wait_ge(s["cs_full"], 2)
            for h in range(HKV):
                v = pcs[:, :, :, h * HKO:h * HKO + NCMP]
                for ti in range(NT):
                    V.tensor_tensor(v[:, ti], banks[6 + h][:, ti * 64:ti * 64 + G * NCMP]
                                    .rearrange("p (g n) -> p g n", g=G),
                                    mcneg[:, ti, :].unsqueeze(1).to_broadcast([P, G, NCMP]), ALU.add)\
                        .then_inc(s["csc"], 1)
            dve.wait_ge(s["csc"], 4)
            for h in range(HKV):
                v = pcs[:, :, :, h * HKO:h * HKO + NCMP]
                cm = cmax.rearrange("p t (h g) -> p t h g", h=HKV)[:, :, h, :]
                link(V.tensor_reduce(cm, v, AX.X, ALU.max))
                last = V.tensor_tensor(v, v, bc(cm, NCMP), ALU.subtract)
            last.then_inc(s["csub"], 1)
            for h in range(HKV):
                dve.wait_ge(s["cexp"], h + 1)
                v = pcs[:, :, :, h * HKO:h * HKO + NCMP]
                cd = cden.rearrange("p t (h g) -> p t h g", h=HKV)[:, :, h, :]
                for ti in range(NT):
                    last = V.tensor_tensor(v[:, ti], v[:, ti],
                                           mc01[:, ti, :].unsqueeze(1).to_broadcast([P, G, NCMP]), ALU.mult)
                last.then_inc(s["pc"], 1)
                dve.wait_ge(s["pc"], h + 1)
                link(V.tensor_reduce(cd, v, AX.X, ALU.add))
            link(V.tensor_scalar(cden, cden, 0.5, None, ALU.max))
            link(V.reciprocal(cden, cden))
            link(V.tensor_tensor(cden, cden, gates[:, :, :, 0], ALU.mult))
            for h in range(HKV):
                dve.wait_ge(s["oc_full"], h + 1)
                if h:
                    dve.wait_ge(s["osum_c"], NT * h)
                for ti in range(NT):
                    V.tensor_tensor(otmp2[:, ti].rearrange("p (g d) -> p g d", g=G),
                                    banks[h][:, ti * 256:(ti + 1) * 256].rearrange("p (g d) -> p g d", g=G),
                                    bc(cden[:, ti, h * G:(h + 1) * G], DH), ALU.mult).then_inc(s["oc_read"], 1)
                dve.wait_ge(s["oc_read"], NT * (h + 1))
                for ti in range(NT):
                    o = osum[:, ti, h * G:(h + 1) * G, :]
                    V.tensor_tensor(o, o, otmp2[:, ti].rearrange("p (g d) -> p g d", g=G), ALU.add)\
                        .then_inc(s["osum_c"], 1)
            for q in range(4):
                m, ti = q // 2, q % 2
                dve.wait_ge(s["wo_full"], q + 1)
                xv = xr[:, ti, 512 * m:512 * (m + 1)]
                V.tensor_tensor(xv, xv, banks[WO_BANKS[q]][:], ALU.add).then_inc(s["x1"], 1)
            dve.wait_ge(s["x1"], 4)
            for ti in range(NT):
                link(V.tensor_tensor_reduce(out=junk[:], in0=xr[:, ti, :], in1=xr[:, ti, :], scale=1.0, scalar=0.0,
                                            op0=ALU.mult, op1=ALU.add, accum_out=ms_y[:, ti:ti + 1]))
            V.tensor_scalar(ms_y, ms_y, 1.0 / D, EPS, ALU.mult, ALU.add).then_inc(s["ms_y"], 1)
            dve.wait_ge(s["ms_y"], 1)
            newton("y", ms_y, rs_y, nw_y)
            dve.wait_ge(s["g2"], 32)
            for ti in range(NT):
                V.scalar_tensor_tensor(out=h2[:, ti, :], in0=xr[:, ti, :], scalar=rs_y[:, ti:ti + 1], in1=g2b[:],
                                       op0=ALU.mult, op1=ALU.mult).then_inc(s["h2"], 1)
            dve.wait_ge(s["h2"], NT)
            for ti in range(NT):
                dve.wait_ge(s["h2hi"], ti + 1)
                V.tensor_tensor(h2s[:, ti, 1, :], h2[:, ti, :], h2s[:, ti, 0, :].bitcast(F32), ALU.subtract)\
                    .then_inc(s["h2s"], 1)
            dve.wait_ge(s["rt_full"], 1)
            V.memset(lg[:, :, E:], FILLER)
            link(V.tensor_tensor(lg[:, :, 0:E], banks[3][:, 0:NT * E].rearrange("p (t e) -> p t e", t=NT),
                                 brt[:].unsqueeze(1).to_broadcast([P, NT, E]), ALU.add))
            for ti in range(NT):
                link(V.max(top[:, ti, :], lg[:, ti, 0:E]))
            link(V.tensor_scalar(ntop, top[:, :, 0], -1.0, None, ALU.mult))
            V.tensor_tensor(lgr, lg[:, :, 0:E], bc(ntop, E), ALU.add).then_inc(s["ntop"], 1)
            link(V.memset(top[:, :, TOPK:8], FILLER))
            for ti in range(NT):
                link(V.match_replace(lgm[:, ti, :], top[:, ti, :], lg[:, ti, :], -FILLER))
            V.tensor_tensor(msk, lgm[:, :, 0:E], lg[:, :, 0:E], ALU.not_equal).then_inc(s["msk"], 1)
            dve.wait_ge(s["msk"], 1)
            dve.wait_ge(s["gexp"], 1)
            link(V.tensor_tensor(gate, gate, msk, ALU.mult))
            link(V.tensor_reduce(gsum, gate, AX.X, ALU.add))
            link(V.reciprocal(gsum, gsum))
            V.tensor_tensor(gate, gate, bc(gsum, E), ALU.mult).then_inc(s["gate"], 1)
            dve.wait_ge(s["gate"], 1)
            V.memset(gates4[:, :, ROUNDS * E:], 0.0)
            for r in range(ROUNDS):
                V.tensor_copy(gates4[:, :, r * E:(r + 1) * E], gate)
            dve.wait_ge(s["pos_full"], 1)
            V.memset(posm[:, :, ROUNDS * E:], -1.0)
            link(V.scalar_tensor_tensor(out=lgr, in0=banks[1][:, 0:NT * E].rearrange("p (t e) -> p t e", t=NT),
                                        scalar=1.0, in1=msk, op0=ALU.add, op1=ALU.mult))
            for r in range(ROUNDS):
                link(V.tensor_scalar(posm[:, :, r * E:(r + 1) * E], lgr, -1.0 - CAP * r, None, ALU.add))
            link(V.reduce_max(rounds_f[:, 0:1], banks[2][:, 0:E], AX.X))
            for r in range(1, ROUNDS):
                link(V.tensor_scalar(rounds_f[:, r:r + 1], rounds_f[:, 0:1], float(CAP * r), float(E), ALU.is_gt, ALU.mult))
            link(V.reduce_sum(rounds_f[:, 0:1], rounds_f[:, 1:ROUNDS], AX.X))
            V.tensor_scalar(rounds_i[:], rounds_f[:, 0:1], float(E - 1), None, ALU.add).then_inc(s["rounds"], 1)

            def split_low(it, j):
                for q, ks in enumerate(UNITS[:NV]):
                    dve.wait_ge(s["wh"], it * (PIECES * NU) + j * NU + q + 1)
                    V.tensor_tensor(wl[:, j % RING, ks[0]:ks[-1] + 1, :], slot(NF + j, 512)[:, ks[0]:ks[-1] + 1, :],
                                    wh[:, j % RING, ks[0]:ks[-1] + 1, :].bitcast(F32), ALU.subtract)\
                        .then_inc(s["wl"], 1)

            def down_low(it, m):
                dve.wait_ge(s["yh"], it * 2 + m + 1)
                V.scalar_tensor_tensor(out=yl[:, 512 * m:512 * (m + 1)], in0=banks[4 + m][:], scalar=gslot[:],
                                       in1=yh[:, 512 * m:512 * (m + 1)].bitcast(F32),
                                       op0=ALU.mult, op1=ALU.subtract).then_inc(s["yl"], 1)

            def place_of(tensor, it, *shape):
                v = tensor[:, :, bass.ds(it, 1)]
                if len(shape) == 1:
                    return v.to_broadcast([P, NT, CAP])
                return v.unsqueeze(3).to_broadcast([P, NT, 2, CAP])

            def slots_of(n):
                if n == 1:
                    return iota_f[:].unsqueeze(1).to_broadcast([P, NT, CAP])
                return iota_f[:].unsqueeze(1).unsqueeze(1).to_broadcast([P, NT, 2, CAP])

            def swiglu(it, hf):
                dve.wait_ge(s["merged"], it * 4 + 2 * hf + 4)
                bias = bias_t[:].rearrange("p (a b c) e -> p b a c e", a=2, b=2)[:, hf, :, :, bass.ds(it % E, 1)]
                V.tensor_tensor(hb[:], t_bank[:].rearrange("p (a c n) -> p a c n", a=2, c=4),
                                bias.to_broadcast([P, 2, 4, CAP]), ALU.add).then_inc(s["t_free"], 1)
                dve.wait_ge(s["t_free"], it * 2 + hf + 2)
                V.tensor_scalar(hb[:, 0], hb[:, 0], LIMIT, None, ALU.min).then_inc(s["hb"], 1)
                V.tensor_scalar(hb[:, 1], hb[:, 1], LIMIT, -LIMIT, ALU.min, ALU.max).then_inc(s["loopdve"], 1)
                dve.wait_ge(s["hb"], it * 2 + hf + 1)
                dve.wait_ge(s["loopdve"], it * 4 + 2 * hf + 1)
                V.scalar_tensor_tensor(out=hb[:, 1], in0=hb[:, 1], scalar=1.0, in1=hb[:, 0],
                                       op0=ALU.add, op1=ALU.mult).then_inc(s["loopdve"], 1)
                dve.wait_ge(s["loopdve"], it * 4 + 2 * hf + 2)
                dve.wait_ge(s["sigm"], it * 2 + hf + 1)
                V.tensor_tensor(actf[:], hb[:, 1], sig[:], ALU.mult).then_inc(s["actf"], 1)
                dve.wait_ge(s["ahi"], it * 2 + hf + 1)
                V.tensor_tensor(a_hl[:, 4 * hf:4 * hf + 4, CAP:], actf[:],
                                a_hl[:, 4 * hf:4 * hf + 4, 0:CAP].bitcast(F32), ALU.subtract).then_inc(s["a_hl"], 1)

            def one_hot(it):
                V.tensor_tensor(onehot[:], slots_of(1), place_of(posm, it, 1), ALU.is_equal).then_inc(s["onehot"], 1)

            def body(it, last):
                dve.wait_ge(s["xfill"], it * 3 + 2)
                if not last:
                    one_hot(it + 1)
                V.tensor_tensor(pgr[:], slots_of(2), place_of(posm, it, 1, 1), ALU.is_equal).then_inc(s["pgr"], 1)
                dve.wait_ge(s["pgr"], it + 1)
                V.tensor_tensor(pgw[:], pgr[:], place_of(gates4, it, 1, 1), ALU.mult).then_inc(s["pgw"], 1)
                split_low(it, 2)
                split_low(it, 3)
                swiglu(it, 0)
                split_low(it, 4)
                swiglu(it, 1)
                split_low(it, 5)
                if not last:
                    split_low(it + 1, 0)
                down_low(it, 0)
                if not last:
                    split_low(it + 1, 1)
                down_low(it, 1)

            dve.wait_ge(s["yinit"], 4)
            dve.wait_ge(s["bias"], 1)
            link(V.memset(gu[:], 0.0))
            V.tensor_copy(pgt[:], gu[:, 0, 0:S])
            V.tensor_copy(yh[:], gu[:].rearrange("p a n -> p (a n)"))
            V.tensor_copy(yl[:], gu[:].rearrange("p a n -> p (a n)")).then_inc(s["yl"], 2)
            V.memset(token[:, 0:1], 0.0).then_inc(s["merged"], 2)
            V.memset(token[:, 1:2], 0.0).then_inc(s["t_free"], 1)
            V.memset(token[:, 2:3], 0.0).then_inc(s["x_free"], 1)
            V.memset(token[:, 3:4], 0.0).then_inc(s["unit_free"], RING * NU)
            one_hot(0)
            dve.wait_ge(s["rounds"], 1)
            last_step = dve.value_load(rounds_i[0:1, 0:1], min_val=E - 1, max_val=ROUNDS * E - 1)
            split_low(0, 0)
            split_low(0, 1)
            with dve.Fori(0, last_step) as it:
                body(it, False)
            body(last_step, True)
            for ti in range(NT):
                dve.wait_ge(s["comb"], last_step * NT + NT + ti + 1)
                for m in range(2):
                    V.tensor_copy(yout[:, ti, 512 * m:512 * (m + 1)], banks[2 * ti + m][:]).then_inc(s["yout"], 1)

        @block.tensor
        def _(pe):
            mm, tp = nc.tensor.matmul, nc.tensor.transpose
            pe.wait_ge(s["const"], 2)
            for ti in range(NT):
                pe.wait_ge(s["xn"], ti + 1)
                for half in range(2):
                    for k in range(4):
                        c = 4 * half + k
                        last = tp(banks[2 * ti + half][:, k * P:(k + 1) * P], xn[:, ti, c * P:(c + 1) * P], ident[:])
                    last.then_inc(s["xt_full"], 1)
            pe.wait_ge(s["xt"], 4)
            def pair(ti, g):
                return rr[:, ti, HKV * g:HKV * (g + 1), :]

            def project(first, end):
                n = 0
                for name, c0, width in PROJ:
                    piece = next(i for i, (a, b) in enumerate(IN_PIECES) if a <= c0 < b)
                    off = c0 - IN_PIECES[piece][0]
                    for ti in range(NT):
                        if first <= n < end:
                            front_arrived(pe, piece)
                            before = [m for m in range(n) if PROJ_BANKS[m] == PROJ_BANKS[n]]
                            if before:
                                pe.wait_ge(s["proj"], before[-1] + 1)
                            for k in range(DK):
                                last = mm(banks[PROJ_BANKS[n]][:, 0:width], xt[:, k, ti * P:(ti + 1) * P],
                                          front_slot(piece)[:, k, off:off + width], start=k == 0, stop=k == DK - 1)
                            last.then_inc(s["proj_full"], 1)
                        n += 1

            def hidden(c):
                i = len(IN_PIECES) + c
                front_arrived(pe, i)
                pe.wait_ge(s["tb"], 4 * (c + 1))
                for k in range(16):
                    last = mm(banks[6 + c][0:NCW, 0:HID], tb[:, c, k, :], comp_slot(i)[:, k, :], start=k == 0, stop=k == 15)
                last.then_inc(s["h_full"], 1)

            def scores(i):
                br, ti, h = GROUPS[i]
                keys = P * (ti + 1)
                if i:
                    pe.wait_ge(s["nmax"], i)
                per = 512 // keys
                for g in range(G):
                    last = mm(banks[g // per][:, (g % per) * keys:(g % per + 1) * keys],
                              qrt[h * DH:(h + 1) * DH, g, ti * P:(ti + 1) * P],
                              kst[h * DH:(h + 1) * DH, br, 0:keys], start=True, stop=True)
                last.then_inc(s["sc_full"], 1)

            def values(i):
                br, ti, h = GROUPS[i]
                n = ti + 1
                if i:
                    pe.wait_ge(s["pts"], i)
                for g in range(G):
                    pe.wait_ge(s["pexp"], G * i + g + 1)
                    for k in range(n):
                        u = g * n + k
                        last = tp(banks[PT_BANKS[u // 4]][:, (u % 4) * P:(u % 4 + 1) * P],
                                  pb[:, i % 2, (g * n + k) * P:(g * n + k + 1) * P], ident[:])
                last.then_inc(s["pt_full"], 1)
                if i:
                    pe.wait_ge(s["pv_read"], i)
                pe.wait_ge(s["pts"], i + 1)
                for g in range(G):
                    for k in range(n):
                        u = g * n + k
                        last = mm(banks[4][:, g * DH:(g + 1) * DH], pt[:, (i + 1) % 2, u * P:(u + 1) * P],
                                  kv[:, k, 256 + 128 * br + h * DH:256 + 128 * br + (h + 1) * DH],
                                  start=k == 0, stop=k == n - 1)
                last.then_inc(s["pv_full"], 1)

            project(0, 8)
            for ti in range(NT):
                pe.wait_ge(s["rn"], ti + 1)
                for g in range(G):
                    last = tp(banks[2 + ti][:, g * P:(g + 1) * P], pair(ti, g), ident[:])
                last.then_inc(s["qt_full"], 1)
            for ti in range(NT):
                pe.wait_ge(s["qr_ready"], 2 * (ti + 1))
                for g in range(G):
                    last = tp(banks[ti][:, g * P:(g + 1) * P], pair(ti, g), ident[:])
                last.then_inc(s["qr_full"], 1)
            pe.wait_ge(s["proj"], 5)
            for br in range(2):
                for ti in range(NT):
                    last = tp(banks[4][:, (2 * br + ti) * P:(2 * br + ti + 1) * P],
                              rr[:, ti, HQ + 2 * br:HQ + 2 * br + 2, :], ident[:])
            last.then_inc(s["qr_full"], 1)
            pe.wait_ge(s["qt"], 2)
            pe.wait_ge(s["qrt"], 3)
            scores(0)
            project(8, 10)
            scores(1)
            values(0)
            project(10, 13)
            scores(2)
            values(1)
            project(13, 14)
            pe.wait_ge(s["proj"], 12)
            for c in range(2):
                for ti in range(NT):
                    last = tp(banks[5][:, (2 * c + ti) * P:(2 * c + ti + 1) * P], kv[:, ti, c * P:(c + 1) * P], ident[:])
            last.then_inc(s["kx_full"], 1)
            pe.wait_ge(s["proj"], 13)
            pe.wait_ge(s["small"], 16 * N_SMALL)
            for c in range(2):
                last = tp(banks[6][:, 16 * c:16 * c + 16], posl[:, c, :], ident[0:16, 0:16])
            last.then_inc(s["post_full"], 1)

            scores(3)
            values(2)
            pe.wait_ge(s["proj"], 14)
            for ti in range(NT):
                last = tp(banks[7][0:16, ti * P:(ti + 1) * P], glr[:, ti, :], ident[:])
            last.then_inc(s["glrt_full"], 1)
            pe.wait_ge(s["glrt"], 1)
            pe.wait_ge(s["kx"], 4)
            for ti in range(NT):
                last = mm(banks[5][:, ti * 256:(ti + 1) * 256], glrt[:, ti * P:(ti + 1) * P], wgate[:], start=True, stop=True)
            last.then_inc(s["z_full"], 1)
            pe.wait_ge(s["post"], 1)
            hidden(0)
            scores(4)
            values(3)
            hidden(1)
            pe.wait_ge(s["loga"], 1)
            pe.wait_ge(s["const"], N_CONST)
            pe.wait_ge(s["hid"], 1)
            for ti in range(NT):
                mm(banks[5][:, ti * 256:(ti + 1) * 256], tri[:], loga[:, ti, :], start=True, stop=True)
                last = mm(banks[6][:, ti * 256:(ti + 1) * 256], blk[:], loga[:, ti, :], start=True, stop=True)
            last.then_inc(s["b_full"], 1)
            scores(5)
            values(4)
            pe.wait_ge(s["hid"], 2)
            for ti in range(NT):
                for hp in range(2):
                    last = mm(banks[7][:, hp * 4 + ti * 2:hp * 4 + ti * 2 + 2], loga[:, ti, hp * P:(hp + 1) * P],
                              blk[:, 0:P:CH], start=True, stop=True)
            last.then_inc(s["dec_full"], 1)
            pe.wait_ge(s["qd"], 1)
            for src, b in ((qd, banks[5]), (kd, banks[6])):
                for hp in range(2):
                    for ti in range(NT):
                        last = tp(b[:, hp * S + ti * P:hp * S + (ti + 1) * P], src[:, ti, hp * P:(hp + 1) * P], ident[:])
                last.then_inc(s["qdt_full"], 1)
            pe.wait_ge(s["hid"], 2)
            pe.wait_ge(s["dec"], 1)
            for c in range(2):
                for k in range(2):
                    last = tp(banks[7][:, (2 * c + k) * NCW:(2 * c + k + 1) * NCW], hid[:, c, k * P:(k + 1) * P],
                              ident[0:NCW, 0:NCW])
            last.then_inc(s["ht_full"], 1)
            scores(6)
            values(5)
            pe.wait_ge(s["qdt"], 2)
            for par in range(2):
                for ti in range(NT):
                    for hp in range(2):
                        last = mm(banks[5 + par][:, (2 * ti + hp) * P:(2 * ti + hp + 1) * P],
                                  kdt[par * 64:par * 64 + 64, hp, ti * P:(ti + 1) * P],
                                  qdt[par * 64:par * 64 + 64, hp, ti * P:(ti + 1) * P], start=True, stop=True)
                last.then_inc(s["at_full"], 1)
            pe.wait_ge(s["hidt"], 1)
            for c in range(2):
                for k in range(2):
                    last = mm(banks[7][0:NCW, c * DH:(c + 1) * DH], hidt[:, c, k, :], w2[:, c, k, :], start=k == 0, stop=k == 1)
            last.then_inc(s["kc_full"], 1)
            scores(7)
            values(6)
            pe.wait_ge(s["kcn"], 2)
            tp(banks[7][0:DH, 0:NCW], kcn[:], ident[0:NCW, 0:NCW]).then_inc(s["kct_full"], 1)
            pe.wait_ge(s["qd"], 2)
            for ci in range(3):
                ti, r = ci // 2, 64 * (ci % 2)
                if ci < 2:
                    pe.wait_ge(s["ats"], ci + 1)
                else:
                    pe.wait_ge(s["kct"], 1)
                for hp in range(2):
                    last = mm(banks[5 + ci][:, hp * 256:(hp + 1) * 256], kstate[r:r + 64, ti, hp * P:(hp + 1) * P],
                              gv[r:r + 64, ti, hp * 256:(hp + 1) * 256], start=True, stop=True)
                last.then_inc(s["u_full"], 1)
            values(7)
            pe.wait_ge(s["sta"], 3)
            for ti in range(NT):
                for par in range(2):
                    pe.wait_ge(s["ats"], par + 1)
                    b = banks[O_BANKS[ti][par]]
                    if ti and par:
                        pe.wait_ge(s["go"], 1)
                    for hp in range(2):
                        h = 2 * hp + par
                        last = mm(b[:, hp * DV:(hp + 1) * DV], ats[:, par, ti, hp, :], gv[:, ti, h * DV:(h + 1) * DV],
                                  start=True, stop=True)
                        for j in range(2):
                            ci = 2 * ti + j
                            if ci:
                                last = mm(b[64 * j:64 * j + 64, hp * DV:(hp + 1) * DV],
                                          qdt[par * 64:par * 64 + 64, hp, ti * P + 64 * j:ti * P + 64 * j + 64],
                                          sta[par * 64:par * 64 + 64, hp, ci - 1, :], start=False, stop=True,
                                          skip_group_check=True)
                    last.then_inc(s["o_full"], 1)
            pe.wait_ge(s["kct"], 1)
            for h in range(HKV):
                pe.wait_ge(s["go"], h + 2)
                for ti in range(NT):
                    for g in range(G):
                        last = mm(banks[6 + h][:, ti * 64 + g * NCMP:ti * 64 + (g + 1) * NCMP],
                                  qt[h * DH:(h + 1) * DH, g, ti * P:(ti + 1) * P], kct[h * DH:(h + 1) * DH, :],
                                  start=True, stop=True)
                last.then_inc(s["cs_full"], 1)
            pe.wait_ge(s["pc"], 2)
            pe.wait_ge(s["pts"], 8)
            for ti in range(NT):
                for g in range(G):
                    last = tp(banks[PT_BANKS[ti]][0:DH, g * P:(g + 1) * P], pcs[:, ti, g, :], ident[:])
                last.then_inc(s["pct_full"], 1)
            pe.wait_ge(s["pct"], 2)
            for h in range(HKV):
                for ti in range(NT):
                    for g in range(G):
                        o = ti * 512 + g * P
                        last = mm(banks[h][:, ti * 256 + g * DH:ti * 256 + (g + 1) * DH],
                                  pt[h * HKO:h * HKO + NCMP, 0, o:o + P], vcs[h * HKO:h * HKO + NCMP, :],
                                  start=True, stop=True)
                last.then_inc(s["oc_full"], 1)

            pe.wait_ge(s["glaout"], 1)
            pe.wait_ge(s["osum_c"], 4)
            for q in range(4):
                for kk in range(2):
                    for ti in range(NT):
                        k = 2 * q + kk
                        src = osum[:, ti, 2 * k:2 * k + 2, :] if k < 4 else go[:, ti, (k - 4) * P:(k - 3) * P]
                        last = tp(banks[4 + q][:, kk * S + ti * P:kk * S + (ti + 1) * P], src, ident[:])
                last.then_inc(s["ot_full"], 1)
            pe.wait_ge(s["ot"], 4)
            for q in range(4):
                m, ti = q // 2, q % 2
                i = len(IN_PIECES) + 2 + m
                front_arrived(pe, i)
                for k in range(DK):
                    last = mm(banks[WO_BANKS[q]][:], ot[:, k, ti * P:(ti + 1) * P], front_slot(i)[:, k, :],
                              start=k == 0, stop=k == DK - 1)
                last.then_inc(s["wo_full"], 1)
            pe.wait_ge(s["brow"], 16)
            pe.wait_ge(s["x1"], 4)
            for k in range(2 * FF // P):
                last = tp(banks[0][:, k * E:(k + 1) * E], brow[:, k * P:(k + 1) * P], ident[0:E, 0:E])
            last.then_inc(s["bias_full"], 1)
            pe.wait_ge(s["h2"], NT)
            for q in range(4):
                for kk in range(2):
                    for ti in range(NT):
                        k = 2 * q + kk
                        last = tp(banks[4 + q][:, kk * S + ti * P:kk * S + (ti + 1) * P], h2[:, ti, k * P:(k + 1) * P], ident[:])
                last.then_inc(s["h2t_full"], 1)
            pe.wait_ge(s["h2t"], 4)
            for ti in range(NT):
                for k in range(DK):
                    last = mm(banks[3][:, ti * E:(ti + 1) * E], h2t[:, k, ti * P:(ti + 1) * P], wrt[:, k, :],
                              start=k == 0, stop=k == DK - 1)
            last.then_inc(s["rt_full"], 1)
            pe.wait_ge(s["msk"], 1)
            mm(banks[1][:, 0:E], stri[:], msk[:, 0, :], start=True, stop=True)
            mm(banks[1][:, E:2 * E], stri[:], msk[:, 1, :], start=True, stop=False)
            mm(banks[1][:, E:2 * E], ones[:], msk[:, 0, :], start=False, stop=True)
            mm(banks[2][:, 0:E], ones[:], msk[:, 0, :], start=True, stop=False)
            mm(banks[2][:, 0:E], ones[:], msk[:, 1, :], start=False, stop=True).then_inc(s["pos_full"], 1)
            pe.wait_ge(s["gate"], 1)
            for ti in range(NT):
                last = tp(banks[4][0:E, ti * P:(ti + 1) * P], gate[:, ti, :], ident[:])
            last.then_inc(s["gt_full"], 1)
            pe.wait_ge(s["gtt"], 1)
            pe.wait_ge(s["g2"], 32)
            pe.wait_ge(s["rounds"], 1)
            pe.wait_ge(s["bias"], 1)
            for ti in range(NT):
                for m in range(2):
                    b = banks[2 * ti + m][:]
                    mm(b, ident[:], xr[:, ti, 512 * m:512 * (m + 1)], start=True, stop=False)
                    mm(b, gtt[:, ti * P:(ti + 1) * P], bdn[:, 512 * m:512 * (m + 1)], start=False, stop=True)\
                        .then_inc(s["yinit"], 1)

            def gather(fill, hots, half):
                pe.wait_ge(s["x_free"], fill)
                pe.wait_ge(s["onehot"], hots)
                for c in range(4):
                    k = 4 * half + c
                    for hl in range(2):
                        for ti in range(NT):
                            last = mm(x_bank[:, c * P + hl * CAP:c * P + (hl + 1) * CAP],
                                      h2s[:, ti, hl, k * P:(k + 1) * P], onehot[:, ti, :],
                                      start=ti == 0, stop=ti == NT - 1)
                last.then_inc(s["xfill"], 1)

            def block_products(it, j, lhs, first=0, end=NU):
                bank = banks[4 + j % 2][:]
                if first:
                    pass
                elif j < 2:
                    pe.wait_ge(s["yl"], it * 2 + j + 1)
                else:
                    pe.wait_ge(s["gu"], it * 4 + j - 1)
                pe.wait_ge(s[f"stage{expert_slot(j)}"], it * 16 + 16 * (front_loads(j) + 1))
                w = slot(NF + j, 512)

                for q, ks in list(enumerate(UNITS))[first:end]:
                    if lhs is a_hl and q in (0, 2):
                        pe.wait_ge(s["a_hl"], it * 2 + 1 + q // 2)
                    if q < NV:
                        pe.wait_ge(s["wl"], it * (PIECES * NV) + j * NV + q + 1)
                    else:
                        pe.wait_ge(s["wl_pool"], it * PIECES + j + 1)
                    for k in ks:
                        mm(bank, lhs[:, k, :], wh[:, j % RING, k, :], start=k == 0, stop=False)
                        last = mm(bank, lhs[:, k, :], wl[:, j % RING, k, :], start=False, stop=False)
                    last.then_inc(s["unit_free"], 1)
                if end < NU:
                    return
                for k in range(SPLIT, DK):
                    last = mm(bank, lhs[:, k, :].bitcast(F32), w[:, k, :], start=False, stop=k == DK - 1)
                last.then_inc(s["block_full"], 1)

            def merge(it, n):
                pe.wait_ge(s["gu"], it * 4 + n + 1)
                if n % 2 == 0:
                    pe.wait_ge(s["t_free"], it * 2 + n // 2 + 1)
                for c in range(4):
                    o = ((n % 2) * 4 + c) * CAP
                    last = mm(t_bank[:, o:o + CAP], gu[:, n % 2, c * P:(c + 1) * P], stack_i[:], start=True, stop=True)
                last.then_inc(s["merged"], 1)

            def combine(it, ti):
                pe.wait_ge(s["yl"], it * 2 + 2)
                for m in range(2):
                    for part in (yh, yl):
                        last = mm(banks[2 * ti + m][:], pgt[:, ti * P:(ti + 1) * P],
                                  part[:, 512 * m:512 * (m + 1)], start=False, stop=True, skip_group_check=True)
                last.then_inc(s["comb"], 1)

            def slots(it, fill):
                pe.wait_ge(s["x_free"], fill)
                pe.wait_ge(s["pgw"], it + 1)
                for ti in range(NT):
                    tp(x_bank[:, ti * P:(ti + 1) * P], pgr[:, ti].rearrange("p a n -> p (a n)"), ident[:])
                for ti in range(NT):
                    last = mm(x_bank[:, S:S + 1], pgw[:, ti].rearrange("p a n -> p (a n)"), ones[:, 0:1],
                              start=ti == 0, stop=ti == NT - 1)
                last.then_inc(s["xfill"], 1)

            def body(it, last):
                block_products(it, 0, xs)
                block_products(it, 1, xs)
                merge(it, 0)
                block_products(it, 2, xs)
                merge(it, 1)
                if not last:
                    gather(it * 3 + 3, it + 2, 0)
                block_products(it, 3, xs, 0, 2)
                merge(it, 2)
                block_products(it, 3, xs, 2)
                combine(it, 0)
                merge(it, 3)
                combine(it, 1)
                block_products(it, 4, a_hl, 0, 2)
                if not last:
                    gather(it * 3 + 4, it + 2, 1)
                block_products(it, 4, a_hl, 2)
                slots(it, it * 3 + (3 if last else 5))
                block_products(it, 5, a_hl)

            last_step = pe.value_load(rounds_i[0:1, 0:1], min_val=E - 1, max_val=ROUNDS * E - 1)
            gather(1, 1, 0)
            gather(2, 1, 1)
            with pe.Fori(0, last_step) as it:
                pe.wait_ge(s["x_free"], it * 3 + 3)
                body(it, False)
            pe.wait_ge(s["x_free"], last_step * 3 + 3)
            body(last_step, True)
            for ti in range(NT):
                combine(last_step + 1, ti)


def kernel(x, positions, norm1_g, w_in, nsa_q_norm_g, nsa_k_norm_g, cmp_pos_k, cmp_w1_k, cmp_w2_k,
           cmp_pos_v, cmp_w1_v, cmp_w2_v, gla_w_gate, gla_b_gate, gla_norm_g, w_out, norm2_g,
           w_router, b_router, w_gate_up, b_gate_up, w_down, b_down):
    import concourse.bacc as bacc
    from concourse.bass_utils import run_bass_kernel_spmd

    inputs = {
        "x": x, "positions": positions, "norm1_g": norm1_g, "w_in": w_in, "nsa_q_norm_g": nsa_q_norm_g,
        "nsa_k_norm_g": nsa_k_norm_g, "cmp_pos_k": cmp_pos_k, "cmp_w1_k": cmp_w1_k, "cmp_w2_k": cmp_w2_k,
        "cmp_pos_v": cmp_pos_v, "cmp_w1_v": cmp_w1_v, "cmp_w2_v": cmp_w2_v, "gla_w_gate": gla_w_gate,
        "gla_b_gate": gla_b_gate, "gla_norm_g": gla_norm_g, "w_out": w_out, "norm2_g": norm2_g,
        "w_router": w_router, "b_router": b_router, "w_gate_up": w_gate_up, "b_gate_up": b_gate_up,
        "w_down": w_down, "b_down": b_down,
    }
    nc = bacc.Bacc("TRN2", target_bir_lowering=False, num_devices=1)
    arrays = {f"in_{n}": np.ascontiguousarray(a) for n, a in inputs.items()}
    aps = [nc.dram_tensor(n, a.shape, mybir.dt.from_np(a.dtype), kind="ExternalInput").ap() for n, a in arrays.items()]
    y = nc.dram_tensor("y", (1, S, D), F32, kind="ExternalOutput").ap()
    decoder_layer(nc, *aps, y)
    result = run_bass_kernel_spmd(nc, [arrays], core_ids=[0])
    return result.results[0]["y"]
```

```python
import math
import numpy as np
import concourse.bass as bass
from concourse import mybir
from contextlib import ExitStack

F32 = mybir.dt.float32
F32R = mybir.dt.float32r
I32 = mybir.dt.int32
ALU = mybir.AluOpType
ACT = mybir.ActivationFunctionType
AX = mybir.AxisListType

P = 128
S, D = 256, 1024
NT = S // P
DK = D // P
DH = 64
HKV, G = 2, 4
HQ = HKV * G
NCMP, CST, CBL = 15, 16, 32
HID = 256
HKO = 32
NCW = HKO + NCMP
GH, DV, CH = 4, 128, 64
GTAU = 16.0
E, TOPK, FF = 32, 4, 1024
CAP = 64
ROUNDS = S // CAP
EPS = 1e-6
NEG = -1e30
SCALE = DH ** -0.5
THETA, RD = 500000.0, 16
LIMIT, ALPHA = 7.0, 1.702

IN_PIECES = [(0, 512), (512, 1024), (1024, 1304), (1304, 1816), (1816, 2328), (2328, 2856)]
NF = len(IN_PIECES) + 4
NSLOT = 6
SLOTW = [max([512] + [b - a for a, b in IN_PIECES[i::NSLOT]]) * DK for i in range(NSLOT)]
PIECES = 6
UP_COLS = [0, FF, 512, FF + 512]
UNITS = [(0, 1), (2, 3), (4, 5), (6,)]
NU = len(UNITS)
NV = NU - 1
SPLIT = sum(len(u) for u in UNITS)
RING = 2
PROJ = [("q", 0, 512), ("kv", 512, 512), ("w", 1024, 280), ("gqk", 1304, 512), ("gv", 1816, 512),
        ("glr", 2328, 16), ("gr", 2344, 512)]
GROUPS = [(br, ti, h) for br in range(2) for ti in range(NT) for h in range(HKV)]
PROJ_BANKS = [4, 5, 6, 7, 4, 5, 6, 7, 5, 6, 7, 5, 6, 7]
PT_BANKS = (2, 3)
O_BANKS = [(5, 6), (7, 5)]
N_SMALL = 14
N_CONST = 20
FILLER = -3e38
MAGIC = 12582912.0
TWO_PI = (6.28125, 0.0019340515136718750, 2 * math.pi - 6.28125 - 0.0019340515136718750)
PI32 = 3.1415925


def decoder_layer(nc, x, positions, norm1_g, w_in, nsa_q_norm_g, nsa_k_norm_g, cmp_pos_k, cmp_w1_k, cmp_w2_k,
                  cmp_pos_v, cmp_w1_v, cmp_w2_v, gla_w_gate, gla_b_gate, gla_norm_g, w_out, norm2_g,
                  w_router, b_router, w_gate_up, b_gate_up, w_down, b_down, out):
    ctx = ExitStack()
    with ctx:
        place = [(nc.sbuf_base + 31) // 32 * 32]

        def at(name, shape, dt, offset):
            return nc.alloc_sbuf_tensor_at(name, shape, dt, offset=offset)

        def sb(name, shape, dt=F32):
            words = int(np.prod(shape[1:]))
            t = at(name, shape, dt, place[0])
            place[0] += (words * 4 + 31) // 32 * 32
            return t

        stage = [sb(f"stage{i}", [P, SLOTW[i]]) for i in range(NSLOT)]
        ident = sb("ident", [P, P])
        ones = sb("ones", [P, P])
        stack_i = sb("stack_i", [P, CAP])
        iota_i = sb("iota_i", [P, CAP], I32)
        iota_f = sb("iota_f", [P, CAP])
        posm = sb("posm", [P, NT, ROUNDS * E + 2])
        gates4 = sb("gates4", [P, NT, ROUNDS * E + 2])
        bias_t = sb("bias_t", [P, 2 * FF // P, E])
        rounds_f = sb("rounds_f", [P, 4])
        rounds_i = sb("rounds_i", [P, 1], I32)
        token = sb("token", [P, 4])
        shared = place[0]

        wh = sb("wh", [P, RING, SPLIT, 512], F32R)
        wl = sb("wl", [P, RING, SPLIT, 512], F32R)
        xs = sb("xs", [P, DK, 2 * CAP], F32R)
        gu = sb("gu", [P, 2, 512])
        hb = sb("hb", [P, 2, 4, CAP])
        sig = sb("sig", [P, 4, CAP])
        actf = sb("actf", [P, 4, CAP])
        a_at = place[0]
        a_hl = sb("a_hl", [P, DK, 2 * CAP], F32R)
        onehot = sb("onehot", [P, NT, CAP], F32R)
        pgr = sb("pgr", [P, NT, 2, CAP])
        pgw = sb("pgw", [P, NT, 2, CAP])
        pgt = sb("pgt", [P, S], F32R)
        gslot = sb("gslot", [P, 1])
        yh = sb("yh", [P, D], F32R)
        yl = sb("yl", [P, D], F32R)
        loop_end = place[0]

        place[0] = shared
        xr = sb("xr", [P, NT, D])
        xn_at = place[0]
        xn = sb("xn", [P, NT, D])
        xt_at = place[0]
        xt = sb("xt", [P, DK, S])
        rr = sb("rr", [P, NT, 12, DH])
        kv = sb("kv", [P, NT, 512])
        gt = sb("gt", [P, NT, 24])
        glr = sb("glr", [P, NT, 16])
        gqk = sb("gqk", [P, NT, 512])
        gv_at = place[0]
        gv = sb("gv", [P, NT, 512])
        gr = sb("gr", [P, NT, 512])
        sq_at = place[0]
        sq = sb("sq", [P, NT, 12, DH])
        qt_at = place[0]
        qt = sb("qt", [P, G, S])
        qrt = sb("qrt", [P, G, S])
        kst_at = place[0]
        kst = sb("kst", [P, 2, S])
        hid_at = place[0]
        hid = sb("hid", [NCW, 2, HID])
        hidt = sb("hidt", [P, 2, 2, NCW])
        pt_at = place[0]
        pt = sb("pt", [P, 2, 2 * G * P])
        g12 = sb("g12", [P, 12, DH])
        glag = sb("glag", [P, DV])
        wgate = sb("wgate", [17, 256])
        glrt = sb("glrt", [17, S])
        w2 = sb("w2", [P, 2, 2, DH])
        wrt = sb("wrt", [P, DK, E])
        brt = sb("brt", [P, E])
        cmask = sb("cmask", [P, 256])
        mc01 = sb("mc01", [P, NT, NCMP])
        mcneg = sb("mcneg", [P, NT, NCMP])
        tri = sb("tri", [P, P])
        blk = sb("blk", [P, P])
        stri = sb("stri", [P, P])
        gk0 = sb("gk0", [NCW, DH])
        kcn = sb("kcn", [NCW, DH])
        kcq = sb("kcq", [NCW, DH])
        vcs = sb("vcs", [NCW, DH])
        loga_at = place[0]
        loga = sb("loga", [P, NT, 256])
        eb = sb("eb", [P, NT, 256])
        en_at = place[0]
        en = sb("en", [P, NT, 256])
        es = sb("es", [P, NT, 256])
        qdt = sb("qdt", [P, 2, S])
        kdt = sb("kdt", [P, 2, S])
        ats = sb("ats", [P, 2, NT, 2, P])
        poss = sb("poss", [P, NT], I32)
        invf = sb("invf", [P, RD // 2])
        rope = sb("rope", [P, 5, NT, RD // 2])
        posl = sb("posl", [16, 2, P])
        post = sb("post", [P, 2, 16])
        kct = sb("kct", [P, NCMP])
        dect = sb("dect", [P, 2, 4])
        st = sb("st", [P, 800])
        assert place[0] <= nc.sbuf_usable_end, (place[0], nc.sbuf_usable_end)
        assert loop_end <= loga_at
        g1b = at("g1b", [P, D], F32, sq_at)
        junk = at("junk", [P, D], F32, qt_at)
        kx = at("kx", [P, 2, HKV, P], F32, xt_at)
        tb = at("tb", [P, 2, 16, NCW], F32, xt_at + 2048)
        g2b = at("g2b", [P, D], F32, xt_at)
        sqx = xr
        bdn = at("bdn", [E, D], F32, a_at)
        pb = at("pb", [P, 2, G * S], F32, xn_at)
        ot = at("ot", [P, DK, S], F32, xn_at)
        sta = at("sta", [P, 2, 3, DV], F32, sq_at)
        sgr = at("sgr", [P, NT, 512], F32, en_at)
        gsq = at("gsq", [P, NT, 512], F32, loga_at)
        brow = at("brow", [E, 2 * FF], F32, pt_at)
        h2t = at("h2t", [P, DK, S], F32, qt_at)
        gtt = at("gtt", [E, S], F32, pt_at)
        h2 = at("h2", [P, NT, D], F32, gv_at)
        h2s = at("h2s", [P, NT, 2, D], F32R, loga_at)
        yout = at("yout", [P, NT, D], F32, loga_at)
        pcs = at("pcs", [P, NT, G, DH], F32, sq_at + 4096)
        rtmp = at("rtmp", [P, 4, 12, RD // 2], F32, hid_at)
        otmp = at("otmp", [P, G * DH], F32, sq_at + 3072)
        otmp2 = at("otmp2", [P, NT, G * DH], F32, en_at)
        osum = rr[:, :, 0:HQ, :]
        go = gqk
        qd, kd, kstate = gqk[:, :, 0:256], en, es

        banks = [ctx.enter_context(nc.psum_tensor(f"bank{i}", [P, 512], F32)) for i in range(8)]
        t_bank, x_bank = banks[6], banks[7]

        st_used = [0]

        def stc(*shape):
            n = int(np.prod(shape))
            v = st[:, st_used[0]:st_used[0] + n]
            st_used[0] += n
            if len(shape) == 2:
                v = v.rearrange("p (a b) -> p a b", b=shape[1])
            if len(shape) == 3:
                v = v.rearrange("p (a b c) -> p a b c", b=shape[1], c=shape[2])
            return v

        ms_x, rs_x, nw_x = stc(NT), stc(NT), stc(NT)
        ms_r, rs_r, nw_r = stc(NT, 12), stc(NT, 12), stc(NT, 12)
        ms_k, rs_k, nw_k = stc(1), stc(1), stc(1)
        ms_g, rs_g, nw_g = stc(NT, GH), stc(NT, GH), stc(NT, GH)
        ms_y, rs_y, nw_y = stc(NT), stc(NT), stc(NT)
        ms2 = stc(NT, 2)
        gsig = stc(NT, 24)
        cmax, cden = stc(NT, HQ), stc(NT, HQ)
        smax, sden, scoef = stc(8, G), stc(8, G), stc(8, G)
        lg, lgm = stc(NT, E + TOPK), stc(NT, E + TOPK)
        top, msk, gate, lgr = stc(NT, 8), stc(NT, E), stc(NT, E), stc(NT, E)
        gsum, ntop, cnts = stc(NT), stc(NT), stc(E)

        s = {n: ctx.enter_context(nc.semaphore("s_" + n)) for n in (
            "oc_read dec_full sqy rs_fine rsx_fine bdn proj_full h_full wo_full x g1 rounds block_full wl "
            "wl_pool yout out const hid g2 pv_full brow small act rope sin xt_full xt proj kx_full kx "
            "post_full post qt_full qt glrt_full glrt z_full absz e1 qr_full qrt sigh b_full bexp dec esd "
            "es ht_full hidt qdt_full qdt kct_full kct u_full sgr csub cexp pct_full pct pt_full pts nmax "
            "pexp ot_full ot h2 h2hi h2t_full h2t bias_full bias ntop gexp gt_full gtt unit_free wh xfill "
            "x_free merged gu comb hb yh yl sigm actf ahi dve ms_x xn ms_r rn tb qr_ready loga qd kc_full "
            "kcn ms_k at_full ats sta o_full go ms_g glaout cs_full csc pc oc_full osum_c sc_full soft "
            "pv_read ms_y h2s rt_full msk gate pos_full t_free loopdve a_hl onehot pgr pgw gslot rs_x "
            "rs_r rs_k rs_g rs_y stage0 stage1 stage2 stage3 stage4 stage5 ").split()}

        def split_k(w):
            return w.rearrange("(k p) n -> p k n", p=P)

        def slot(i, width):
            return stage[i % NSLOT][:, 0:DK * width].rearrange("p (k n) -> p k n", k=DK)

        def front_slot(i):
            if i < len(IN_PIECES):
                return slot(i, IN_PIECES[i][1] - IN_PIECES[i][0])
            return slot(i, 512)

        def comp_slot(i):
            return stage[i % NSLOT][:, 0:16 * HID].rearrange("p (k n) -> p k n", k=16)

        def front_arrived(eng, i):
            eng.wait_ge(s[f"stage{i % NSLOT}"], 16 * (i // NSLOT + 1))

        def expert_slot(j):
            return (NF + j) % NSLOT

        def front_loads(j):
            return len(range(expert_slot(j), NF, NSLOT))

        def bc(ap, n):
            return ap.unsqueeze(len(ap.shape)).to_broadcast(list(ap.shape) + [n])

        w_up_v = w_gate_up[0].rearrange("e (k p) n -> p e k n", p=P)
        w_dn_v = w_down[0].rearrange("e (k p) n -> p e k n", p=P)

        def expert_source(e, j):
            if j < 4:
                return w_up_v[:, e, :, UP_COLS[j]:UP_COLS[j] + 512]
            return w_dn_v[:, e, :, 512 * (j - 4):512 * (j - 3)]

        def front_used(eng, i):
            if i < len(IN_PIECES):
                eng.wait_ge(s["proj_full"], NT * (i + 1 + (i == len(IN_PIECES) - 1)))
            elif i < len(IN_PIECES) + 2:
                eng.wait_ge(s["h_full"], i - len(IN_PIECES) + 1)
            else:
                eng.wait_ge(s["wo_full"], NT * (i - len(IN_PIECES) - 1))

        block = ctx.enter_context(nc.Block())

        @block.sync
        def _(sp):
            for ti in range(NT):
                sp.dma_start(xr[:, ti, :], x[0, ti * P:(ti + 1) * P, :]).then_inc(s["x"], 16)
            sp.dma_start(g1b[:], norm1_g[0].partition_broadcast(P)).then_inc(s["g1"], 16)
            for i in range(NF):
                if i == 2:
                    sp.wait_ge(s["small"], 16 * N_SMALL)
                if i >= NSLOT:
                    front_used(sp, i - NSLOT)
                if i < len(IN_PIECES):
                    src, dst = split_k(w_in[0])[:, :, IN_PIECES[i][0]:IN_PIECES[i][1]], front_slot(i)
                elif i < len(IN_PIECES) + 2:
                    src = split_k((cmp_w1_k, cmp_w1_v)[i - len(IN_PIECES)][0])
                    dst = comp_slot(i)
                else:
                    m = i - len(IN_PIECES) - 2
                    src, dst = split_k(w_out[0])[:, :, 512 * m:512 * (m + 1)], front_slot(i)
                sp.dma_start(dst, src).then_inc(s[f"stage{i % NSLOT}"], 16)
            for j in range(PIECES):
                front_used(sp, NF + j - NSLOT)
                sp.dma_start(slot(NF + j, 512), expert_source(0, j)).then_inc(s[f"stage{expert_slot(j)}"], 16)
            sp.wait_ge(s["rounds"], 1)
            last_step = sp.value_load(rounds_i[0:1, 0:1], min_val=E - 1, max_val=ROUNDS * E - 1)
            with sp.Fori(1, last_step + 1) as it:
                expert = sp.snap(it % E, min_val=0, max_val=E - 1)
                for j in range(PIECES):
                    sp.wait_ge(s["block_full"], it * PIECES + (j + 1 - PIECES))
                    sp.dma_start(slot(NF + j, 512), expert_source(expert, j)).then_inc(s[f"stage{expert_slot(j)}"], 16)
            for ti in range(NT):
                sp.wait_ge(s["yout"], 2 * (ti + 1))
                sp.dma_start(out[0, ti * P:(ti + 1) * P, :], yout[:, ti, :]).then_inc(s["out"], 16)
            sp.wait_ge(s["out"], 16 * NT)

        @block.gpsimd
        def _(pool):
            c = [0]

            def step(ins):
                c[0] += 1
                ins.then_inc(s["const"], 1)
                pool.wait_ge(s["const"], c[0])

            def select(t, compare_op, fill, base, pattern, mult):
                step(nc.gpsimd.affine_select(out=t, in_=t, compare_op=compare_op, fill=fill, base=base,
                                             pattern=pattern, channel_multiplier=mult))

            step(nc.gpsimd.memset(ident[:], 0.0))
            select(ident[:], ALU.not_equal, 1.0, 0, [[-1, P]], 1)
            small = [
                (poss[:], positions[0].rearrange("(t p) -> p t", p=P)),
                (g12[:, 0:HQ, :], nsa_q_norm_g[0:1, :].partition_broadcast(P).to_broadcast([P, HQ, DH])),
                (g12[:, HQ:HQ + 2, :], nsa_k_norm_g[0, 1:2, :].partition_broadcast(P).to_broadcast([P, 2, DH])),
                (g12[:, HQ + 2:HQ + 4, :], nsa_k_norm_g[0, 2:3, :].partition_broadcast(P).to_broadcast([P, 2, DH])),
                (gk0[:], nsa_k_norm_g[0, 0, :].partition_broadcast(NCW)),
                (glag[:], gla_norm_g[0].partition_broadcast(P)),
                (wgate[0:16, :], gla_w_gate[0]),
                (wgate[16:17, :], gla_b_gate[0:1, :]),
                (posl[:, 0, :], cmp_pos_k[0].rearrange("(c i) d -> c (i d)", i=2)),
                (posl[:, 1, :], cmp_pos_v[0].rearrange("(c i) d -> c (i d)", i=2)),
                (w2[:, 0, :, :], split_k(cmp_w2_k[0])),
                (w2[:, 1, :, :], split_k(cmp_w2_v[0])),
                (wrt[:], split_k(w_router[0])),
                (brt[:], b_router[0].partition_broadcast(P)),
            ]
            for dst, src in small:
                pool.dma_start(dst, src, allow_slow_non_contiguous=True).then_inc(s["small"], 16)
            assert len(small) == N_SMALL
            step(nc.gpsimd.memset(glrt[:], 1.0))
            step(nc.gpsimd.memset(ones[:], 1.0))
            step(nc.gpsimd.memset(stack_i[:], 0.0))
            select(stack_i[:], ALU.not_equal, 1.0, 0, [[-1, CAP]], 1)
            select(stack_i[:], ALU.not_equal, 1.0, -CAP, [[-1, CAP]], 1)
            step(nc.gpsimd.memset(cmask[:], 0.0))
            select(cmask[:], ALU.is_ge, NEG, P, [[-1, 2 * P]], 1)
            step(nc.gpsimd.memset(mc01[:], 1.0))
            select(mc01[:], ALU.is_ge, 0.0, 1 - CBL, [[P, NT], [-CST, NCMP]], 1)
            step(nc.gpsimd.memset(tri[:], 1.0))
            select(tri[:], ALU.is_ge, 0.0, 0, [[1, P]], -1)
            step(nc.gpsimd.memset(tri[0:CH, CH:P], 0.0))
            step(nc.gpsimd.memset(blk[:], 0.0))
            step(nc.gpsimd.memset(blk[0:CH, 0:CH], 1.0))
            step(nc.gpsimd.memset(blk[CH:P, CH:P], 1.0))
            step(nc.gpsimd.memset(stri[:], 1.0))
            select(stri[:], ALU.is_gt, 0.0, 0, [[1, P]], -1)
            step(nc.gpsimd.iota(iota_i[:], [[1, CAP]], base=0, channel_multiplier=0))
            assert c[0] == N_CONST, c[0]
            pool.wait_ge(s["hid"], 2)
            pool.dma_start(g2b[:], norm2_g[0].partition_broadcast(P)).then_inc(s["g2"], 16)
            pool.wait_ge(s["oc_full"], 2)
            pool.dma_start(brow[:], b_gate_up[0]).then_inc(s["brow"], 16)
            pool.wait_ge(s["bias_full"], 1)
            pool.dma_start(bdn[:], b_down[0]).then_inc(s["bdn"], 16)

            def split_low(it, j):
                ks = UNITS[-1]
                pool.wait_ge(s["wh"], it * (PIECES * NU) + (j + 1) * NU)
                nc.gpsimd.tensor_tensor(wl[:, j % RING, ks[0]:ks[-1] + 1, :], slot(NF + j, 512)[:, ks[0]:ks[-1] + 1, :],
                                        wh[:, j % RING, ks[0]:ks[-1] + 1, :].bitcast(F32), ALU.subtract)\
                    .then_inc(s["wl_pool"], 1)

            pool.wait_ge(s["rounds"], 1)
            last_step = pool.value_load(rounds_i[0:1, 0:1], min_val=E - 1, max_val=ROUNDS * E - 1)
            with pool.Fori(0, last_step + 1) as it:
                for j in range(PIECES):
                    split_low(it, j)

        @block.scalar
        def _(act):
            n_act = [0]

            def rstd(what, a, r):
                act.wait_ge(s["ms_" + what], 1)
                link(nc.scalar.activation(r, a, ACT.Ln))
                nc.scalar.activation(r, r, ACT.Exp, scale=-0.5).then_inc(s["rs_" + what], 1)

            def link(ins):
                n_act[0] += 1
                ins.then_inc(s["act"], 1)
                act.wait_ge(s["act"], n_act[0])

            for q in range(4):
                act.wait_ge(s["xt_full"], q + 1)
                ti, half = q // 2, q % 2
                nc.scalar.copy(xt[:, 4 * half:4 * half + 4, ti * P:(ti + 1) * P],
                               banks[q][:].rearrange("p (k t) -> p k t", k=4)).then_inc(s["xt"], 1)
            def proj_evac(first, end):
                n = 0
                for name, c0, width in PROJ:
                    for ti in range(NT):
                        if first <= n < end:
                            evac_one(n, name, width, ti)
                        n += 1

            def evac_one(n, name, width, ti):
                b = banks[PROJ_BANKS[n]]

                def scaled(dst, src):
                    return nc.scalar.activation(dst, src, ACT.Copy, scale=rs_x[:, ti:ti + 1])

                act.wait_ge(s["proj_full"], n + 1)
                if name == "q":
                    last = scaled(rr[:, ti, 0:HQ, :].rearrange("p (g h) d -> p h g d", h=HKV),
                                          b[:, 0:512].rearrange("p (h g d) -> p h g d", h=HKV, g=G))
                elif name == "kv":
                    scaled(kv[:, ti, 0:256], b[:, 0:256])
                    scaled(rr[:, ti, HQ:HQ + 2, :], b[:, 256:384].rearrange("p (h d) -> p h d", h=2))
                    last = scaled(kv[:, ti, 256:384], b[:, 384:512])
                elif name == "w":
                    scaled(rr[:, ti, HQ + 2:HQ + 4, :], b[:, 0:128].rearrange("p (h d) -> p h d", h=2))
                    scaled(kv[:, ti, 384:512], b[:, 128:256])
                    last = scaled(gt[:, ti, :], b[:, 256:280])
                else:
                    dst = {"gqk": gqk, "gv": gv, "glr": glr, "gr": gr}[name]
                    last = scaled(dst[:, ti, :], b[:, 0:width])
                last.then_inc(s["proj"], 1)

            def evac_pt(i):
                act.wait_ge(s["pt_full"], i + 1)
                for k in range(GROUPS[i][1] + 1):
                    last = nc.scalar.copy(pt[:, (i + 1) % 2, k * 512:(k + 1) * 512], banks[PT_BANKS[k]][:])
                last.then_inc(s["pts"], 1)

            def exps(i):
                br, ti, h = GROUPS[i]
                keys = P * (ti + 1)
                act.wait_ge(s["nmax"], i + 1)
                for g in range(G):
                    v = pb[:, i % 2, g * keys:(g + 1) * keys]
                    nc.scalar.activation(v, v, ACT.Exp, bias=smax[:, i, g:g + 1], scale=SCALE,
                                         accum_out=sden[:, i, g:g + 1]).then_inc(s["pexp"], 1)

            def hidden(c):
                act.wait_ge(s["h_full"], c + 1)
                nc.scalar.activation(hid[:, c, :], banks[6 + c][0:NCW, 0:HID], ACT.Sigmoid).then_inc(s["sigh"], 1)

            rstd("x", ms_x, rs_x)
            act.wait_ge(s["rsx_fine"], 1)
            proj_evac(0, 4)
            act.wait_ge(s["rope"], 1)
            nc.scalar.activation(rope[:, 2, :, :], rope[:, 0, :, :], ACT.Sin)
            nc.scalar.activation(rope[:, 3, :, :], rope[:, 0, :, :], ACT.Sin, scale=0.5).then_inc(s["sin"], 1)
            proj_evac(4, 6)
            act.wait_ge(s["proj"], 6)
            nc.scalar.activation(gsig, gt[:], ACT.Sigmoid)
            rstd("r", ms_r, rs_r)
            proj_evac(6, 8)
            for ti in range(NT):
                act.wait_ge(s["qt_full"], ti + 1)
                nc.scalar.copy(qt[:, :, ti * P:(ti + 1) * P], banks[2 + ti][:].rearrange("p (g t) -> p g t", g=G))\
                    .then_inc(s["qt"], 1)
            for q in range(3):
                act.wait_ge(s["qr_full"], q + 1)
                if q < 2:
                    nc.scalar.copy(qrt[:, :, q * P:(q + 1) * P], banks[q][:].rearrange("p (g t) -> p g t", g=G))\
                        .then_inc(s["qrt"], 1)
                else:
                    nc.scalar.copy(kst[:], banks[4][:].rearrange("p (b t) -> p b t", b=2)).then_inc(s["qrt"], 1)
            exps(0)
            proj_evac(8, 10)
            evac_pt(0)
            exps(1)
            proj_evac(10, 13)
            evac_pt(1)
            exps(2)
            proj_evac(13, 14)
            act.wait_ge(s["kx_full"], 1)
            kvt = banks[5][:].rearrange("p (c t i) -> p c t i", c=2, i=2)
            for i in range(2):
                for h in range(HKV):
                    nc.scalar.copy(kx[i * DH:(i + 1) * DH, :, h, :], kvt[h * DH:(h + 1) * DH, :, :, i])\
                        .then_inc(s["kx"], 1)
            act.wait_ge(s["post_full"], 1)
            nc.scalar.copy(post[:], banks[6][:, 0:32].rearrange("p (c k) -> p c k", c=2)).then_inc(s["post"], 1)
            evac_pt(2)
            exps(3)
            act.wait_ge(s["glrt_full"], 1)
            nc.scalar.copy(glrt[0:16, :], banks[7][0:16, 0:S]).then_inc(s["glrt"], 1)
            act.wait_ge(s["z_full"], 1)
            z = banks[5][:].rearrange("p (t n) -> p t n", t=NT)
            nc.scalar.activation(en[:], z, ACT.Abs).then_inc(s["absz"], 1)
            act.wait_ge(s["absz"], 1)
            link(nc.scalar.activation(en[:], en[:], ACT.Exp, scale=-1.0))
            nc.scalar.activation(en[:], en[:], ACT.Ln, bias=1.0).then_inc(s["e1"], 1)
            hidden(0)
            evac_pt(3)
            exps(4)
            hidden(1)
            act.wait_ge(s["b_full"], 1)
            b = banks[5][:].rearrange("p (t n) -> p t n", t=NT)
            nc.scalar.activation(eb[:], b, ACT.Exp)
            nc.scalar.activation(en[:], b, ACT.Exp, scale=-1.0).then_inc(s["bexp"], 1)
            evac_pt(4)
            exps(5)
            act.wait_ge(s["esd"], 1)
            nc.scalar.activation(es[:], es[:], ACT.Exp).then_inc(s["es"], 1)
            act.wait_ge(s["dec_full"], 1)
            nc.scalar.activation(dect[:], banks[7][:, 0:8].rearrange("p (h c) -> p h c", h=2), ACT.Exp)\
                .then_inc(s["dec"], 1)
            for t, b in ((qdt, banks[5]), (kdt, banks[6])):
                act.wait_ge(s["qdt_full"], 1 if t is qdt else 2)
                nc.scalar.copy(t[:], b[:].rearrange("p (h t) -> p h t", h=2)).then_inc(s["qdt"], 1)
            act.wait_ge(s["ht_full"], 1)
            nc.scalar.copy(hidt[:], banks[7][:, 0:4 * NCW].rearrange("p (c k n) -> p c k n", c=2, k=2))\
                .then_inc(s["hidt"], 1)
            evac_pt(5)
            exps(6)
            rstd("k", ms_k[0:NCW, :], rs_k[0:NCW, :])
            evac_pt(6)
            exps(7)
            act.wait_ge(s["kct_full"], 1)
            nc.scalar.copy(kct[0:DH, :], banks[7][0:DH, 0:NCMP])
            nc.scalar.copy(kct[DH:P, :], banks[7][0:DH, HKO:NCW]).then_inc(s["kct"], 1)
            evac_pt(7)
            act.wait_ge(s["u_full"], 3)
            nc.scalar.activation(sgr[:], gr[:], ACT.Sigmoid).then_inc(s["sgr"], 1)
            rstd("g", ms_g, rs_g)
            for q in range(2):
                act.wait_ge(s["ot_full"], q + 1)
                nc.scalar.copy(ot[:, 4 + 2 * q:6 + 2 * q, :], banks[4 + q][:].rearrange("p (k t) -> p k t", k=2))\
                    .then_inc(s["ot"], 1)
            act.wait_ge(s["csub"], 1)
            for h in range(HKV):
                v = pcs[:, :, :, h * HKO:h * HKO + NCMP]
                nc.scalar.activation(v, v, ACT.Exp, scale=SCALE).then_inc(s["cexp"], 1)
            for ti in range(NT):
                act.wait_ge(s["pct_full"], ti + 1)
                nc.scalar.copy(pt[0:DH, 0, ti * 512:(ti + 1) * 512], banks[6 + ti][0:DH, :]).then_inc(s["pct"], 1)
            for q in range(2):
                act.wait_ge(s["ot_full"], q + 3)
                nc.scalar.copy(ot[:, 2 * q:2 * q + 2, :], banks[6 + q][:].rearrange("p (k t) -> p k t", k=2))\
                    .then_inc(s["ot"], 1)

            def square(q):
                m, ti = q // 2, q % 2
                act.wait_ge(s["wo_full"], q + 1)
                nc.scalar.activation(sqx[:, ti, 512 * m:512 * (m + 1)], banks[2 * ti + m][:], ACT.Square,
                                     accum_out=ms2[:, ti, m:m + 1]).then_inc(s["sqy"], 1)

            def h2t_evac(q):
                m, ti = q // 2, q % 2
                act.wait_ge(s["h2t_full"], q + 1)
                nc.scalar.copy(h2t[:, 4 * m:4 * m + 4, ti * P:(ti + 1) * P],
                               banks[4 + q][:].rearrange("p (k t) -> p k t", k=4)).then_inc(s["h2t"], 1)

            square(0)
            square(1)
            h2t_evac(0)
            square(2)
            h2t_evac(1)
            square(3)
            h2t_evac(2)
            rstd("y", ms_y, rs_y)
            h2t_evac(3)
            act.wait_ge(s["rs_fine"], 1)
            for ti in range(NT):
                nc.scalar.activation(h2s[:, ti, 0, :], h2[:, ti, :], ACT.Copy, scale=rs_y[:, ti:ti + 1])\
                    .then_inc(s["h2hi"], 1)
            act.wait_ge(s["ntop"], 1)
            nc.scalar.activation(gate, lgr, ACT.Exp).then_inc(s["gexp"], 1)
            act.wait_ge(s["bias_full"], 1)
            nc.scalar.copy(bias_t[:], banks[4][:].rearrange("p (k e) -> p k e", e=E)).then_inc(s["bias"], 1)
            def split_high(it, j, first=0, end=NU):
                act.wait_ge(s[f"stage{expert_slot(j)}"], it * 16 + 16 * (front_loads(j) + 1))
                for q, ks in list(enumerate(UNITS))[first:end]:
                    act.wait_ge(s["unit_free"], it * (PIECES * NU) + j * NU + q + 1)
                    nc.scalar.copy(wh[:, j % RING, ks[0]:ks[-1] + 1, :], slot(NF + j, 512)[:, ks[0]:ks[-1] + 1, :])\
                        .then_inc(s["wh"], 1)

            def gather_evac(fill, half, bank=x_bank):
                act.wait_ge(s["xfill"], fill)
                nc.scalar.copy(xs[:, 4 * half:4 * half + 4, :], bank[:].rearrange("p (k n) -> p k n", k=4))\
                    .then_inc(s["x_free"], 1)

            def up_evac(it, n):
                act.wait_ge(s["block_full"], it * PIECES + n + 1)
                act.wait_ge(s["merged"], it * 4 + n + 1)
                nc.scalar.copy(gu[:, n % 2, :], banks[4 + n % 2][:]).then_inc(s["gu"], 1)

            def down_high(it, m):
                act.wait_ge(s["block_full"], it * PIECES + 5 + m)
                act.wait_ge(s["comb"], it * NT + NT)
                act.wait_ge(s["gslot"], it + 1)
                nc.scalar.activation(yh[:, 512 * m:512 * (m + 1)], banks[4 + m][:], ACT.Copy, scale=gslot[:])\
                    .then_inc(s["yh"], 1)

            def act_half(it, hf):
                act.wait_ge(s["hb"], it * 2 + hf + 1)
                nc.scalar.activation(sig[:], hb[:, 0, :, :], ACT.Sigmoid, scale=ALPHA).then_inc(s["sigm"], 1)
                act.wait_ge(s["actf"], it * 2 + hf + 1)
                nc.scalar.copy(a_hl[:, 4 * hf:4 * hf + 4, 0:CAP], actf[:]).then_inc(s["ahi"], 1)

            def body(it, last):
                split_high(it, 2)
                up_evac(it, 0)
                split_high(it, 3)
                up_evac(it, 1)
                split_high(it, 4)
                up_evac(it, 2)
                act_half(it, 0)
                split_high(it, 5, 0, 2)
                up_evac(it, 3)
                if not last:
                    gather_evac(it * 3 + 3, 0)
                split_high(it, 5, 2)
                act_half(it, 1)
                if not last:
                    split_high(it + 1, 0, 0, 2)
                    gather_evac(it * 3 + 4, 1)
                act.wait_ge(s["xfill"], it * 3 + (3 if last else 5))
                act.wait_ge(s["yl"], it * 2 + 2)
                nc.scalar.copy(gslot[:], x_bank[:, S:S + 1]).then_inc(s["gslot"], 1)
                nc.scalar.copy(pgt[:], x_bank[:, 0:S]).then_inc(s["x_free"], 1)
                down_high(it, 0)
                if not last:
                    split_high(it + 1, 0, 2)
                    split_high(it + 1, 1)
                down_high(it, 1)

            split_high(0, 0)
            gather_evac(1, 0, x_bank)
            gather_evac(2, 1, t_bank)
            act.wait_ge(s["gt_full"], 1)
            nc.scalar.copy(gtt[:], banks[5][0:E, 256:256 + S]).then_inc(s["gtt"], 1)
            split_high(0, 1)
            act.wait_ge(s["rounds"], 1)
            last_step = act.value_load(rounds_i[0:1, 0:1], min_val=E - 1, max_val=ROUNDS * E - 1)
            with act.Fori(0, last_step) as it:
                body(it, False)
            body(last_step, True)

        @block.vector
        def _(dve):
            n_dve = [0]
            V = nc.vector

            def link(ins):
                n_dve[0] += 1
                ins.then_inc(s["dve"], 1)
                dve.wait_ge(s["dve"], n_dve[0])

            def newton(what, a, r, w, done=None):
                dve.wait_ge(s["rs_" + what], 1)
                link(V.tensor_tensor(w, r, r, ALU.mult))
                link(V.tensor_tensor(w, w, a, ALU.mult))
                link(V.tensor_scalar(w, w, -0.5, 1.5, ALU.mult, ALU.add))
                if done is None:
                    link(V.tensor_tensor(r, r, w, ALU.mult))
                else:
                    V.tensor_tensor(r, r, w, ALU.mult).then_inc(done, 1)
                    dve.wait_ge(done, 1)

            def place_of(tensor, it, *shape):
                v = tensor[:, :, bass.ds(it, 1)]
                if len(shape) == 1:
                    return v.to_broadcast([P, NT, CAP])
                return v.unsqueeze(3).to_broadcast([P, NT, 2, CAP])

            def slots_of(n):
                if n == 1:
                    return iota_f[:].unsqueeze(1).to_broadcast([P, NT, CAP])
                return iota_f[:].unsqueeze(1).unsqueeze(1).to_broadcast([P, NT, 2, CAP])

            def one_hot(it):
                V.tensor_tensor(onehot[:], slots_of(1), place_of(posm, it, 1), ALU.is_equal).then_inc(s["onehot"], 1)

            dve.wait_ge(s["x"], 16 * NT)
            dve.wait_ge(s["g1"], 16)
            for ti in range(NT):
                V.tensor_tensor(xn[:, ti, :], xr[:, ti, :], g1b[:], ALU.mult).then_inc(s["xn"], 1)
            for ti in range(NT):
                link(V.tensor_tensor_reduce(out=junk[:], in0=xr[:, ti, :], in1=xr[:, ti, :], scale=1.0, scalar=0.0,
                                            op0=ALU.mult, op1=ALU.add, accum_out=ms_x[:, ti:ti + 1]))
            V.tensor_scalar(ms_x, ms_x, 1.0 / D, EPS, ALU.mult, ALU.add).then_inc(s["ms_x"], 1)
            dve.wait_ge(s["ms_x"], 1)
            newton("x", ms_x, rs_x, nw_x, s["rsx_fine"])
            for i in range(RD // 2):
                last = V.memset(invf[:, i:i + 1], float(np.exp(np.float32(-math.log(THETA)) * np.float32(2 * i) / np.float32(RD))))
            link(last)
            dve.wait_ge(s["small"], 16 * N_SMALL)
            posf = rope[:, 4, 0, 0:NT]
            link(V.tensor_copy(posf, poss[:]))
            link(V.tensor_tensor(rope[:, 0, :, :], bc(posf, RD // 2),
                                 invf[:].unsqueeze(1).to_broadcast([P, NT, RD // 2]), ALU.mult))
            link(V.tensor_scalar(rope[:, 1, :, :], rope[:, 0, :, :], 1 / (2 * math.pi), MAGIC, ALU.mult, ALU.add))
            link(V.tensor_scalar(rope[:, 1, :, :], rope[:, 1, :, :], -MAGIC, None, ALU.add))
            for c in TWO_PI:
                link(V.scalar_tensor_tensor(out=rope[:, 0, :, :], in0=rope[:, 1, :, :], scalar=-c,
                                            in1=rope[:, 0, :, :], op0=ALU.mult, op1=ALU.add))
            V.tensor_scalar(rope[:, 0, :, :], rope[:, 0, :, :], PI32, -PI32, ALU.min, ALU.max).then_inc(s["rope"], 1)
            dve.wait_ge(s["const"], N_CONST)
            V.tensor_copy(iota_f[:], iota_i[:])
            link(V.tensor_scalar(mcneg[:], mc01[:], 1.0, -NEG, ALU.subtract, ALU.mult))
            dve.wait_ge(s["proj"], 6)
            dve.wait_ge(s["xn"], NT)
            link(V.tensor_tensor(sq[:], rr[:], rr[:], ALU.mult))
            link(V.tensor_reduce(ms_r, sq[:], AX.X, ALU.add))
            V.tensor_scalar(ms_r, ms_r, 1.0 / DH, EPS, ALU.mult, ALU.add).then_inc(s["ms_r"], 1)
            dve.wait_ge(s["ms_r"], 1)
            dve.wait_ge(s["sin"], 1)
            link(V.tensor_tensor(rope[:, 3, :, :], rope[:, 3, :, :], rope[:, 3, :, :], ALU.mult))
            link(V.tensor_scalar(rope[:, 3, :, :], rope[:, 3, :, :], -2.0, 1.0, ALU.mult, ALU.add))
            newton("r", ms_r, rs_r, nw_r)
            link(V.tensor_tensor(rr[:], rr[:], bc(rs_r, DH), ALU.mult))
            for ti in range(NT):
                V.tensor_tensor(rr[:, ti, :, :], rr[:, ti, :, :], g12[:], ALU.mult).then_inc(s["rn"], 1)
            dve.wait_ge(s["rn"], NT)
            dve.wait_ge(s["qt_full"], NT)
            for ti in range(NT):
                sin = rope[:, 2, ti, :].unsqueeze(1).to_broadcast([P, 12, RD // 2])
                cos = rope[:, 3, ti, :].unsqueeze(1).to_broadcast([P, 12, RD // 2])
                lo, hi = rr[:, ti, :, 0:RD // 2], rr[:, ti, :, RD // 2:RD]
                if ti:
                    dve.wait_ge(s["qr_ready"], 2 * ti)
                V.tensor_tensor(rtmp[:, 0], lo, cos, ALU.mult)
                V.tensor_tensor(rtmp[:, 1], hi, sin, ALU.mult)
                V.tensor_tensor(rtmp[:, 2], hi, cos, ALU.mult)
                link(V.tensor_tensor(rtmp[:, 3], lo, sin, ALU.mult))
                V.tensor_tensor(lo, rtmp[:, 0], rtmp[:, 1], ALU.subtract).then_inc(s["qr_ready"], 1)
                V.tensor_tensor(hi, rtmp[:, 2], rtmp[:, 3], ALU.add).then_inc(s["qr_ready"], 1)
            def silu_hidden(c):
                dve.wait_ge(s["sigh"], c + 1)
                V.tensor_tensor(hid[:, c, :], banks[6 + c][0:NCW, 0:HID], hid[:, c, :], ALU.mult).then_inc(s["hid"], 1)

            gates = gsig.rearrange("p t (h b) -> p t h b", b=3)
            n_soft = [0]

            def soft(i):
                br, ti, h = GROUPS[i]
                keys = P * (ti + 1)
                dve.wait_ge(s["sc_full"], i + 1)
                mask = cmask[:, 2 * P - keys:2 * P] if ti == 0 else cmask[:]
                per = 512 // keys
                for b in range(G // per):
                    V.tensor_tensor(pb[:, i % 2, b * 512:b * 512 + 512].rearrange("p (g k) -> p g k", g=per),
                                    banks[b][:].rearrange("p (g k) -> p g k", g=per),
                                    mask.unsqueeze(1).to_broadcast([P, per, keys]), ALU.add).then_inc(s["soft"], 1)
                n_soft[0] += G // per
                dve.wait_ge(s["soft"], n_soft[0])
                link(V.reduce_max(smax[:, i, :], pb[:, i % 2, 0:G * keys].rearrange("p (g k) -> p g k", g=G), AX.X))
                V.tensor_scalar(smax[:, i, :], smax[:, i, :], -SCALE, None, ALU.mult).then_inc(s["nmax"], 1)

            def gather_out(i):
                br, ti, h = GROUPS[i]
                dve.wait_ge(s["pexp"], G * (i + 1))
                link(V.reciprocal(scoef[:, i, :], sden[:, i, :]))
                link(V.tensor_tensor(scoef[:, i, :], scoef[:, i, :], gates[:, ti, h * G:(h + 1) * G, 1 + br], ALU.mult))
                dve.wait_ge(s["pv_full"], i + 1)
                o = osum[:, ti, h * G:(h + 1) * G, :]
                pv = banks[4][:, 0:256].rearrange("p (g d) -> p g d", g=G)
                if br == 0:
                    V.tensor_tensor(o, pv, bc(scoef[:, i, :], DH), ALU.mult).then_inc(s["pv_read"], 1)
                else:
                    tmp = otmp[:].rearrange("p (g d) -> p g d", g=G)
                    V.tensor_tensor(tmp, pv, bc(scoef[:, i, :], DH), ALU.mult).then_inc(s["pv_read"], 1)
                    dve.wait_ge(s["pv_read"], i + 1)
                    link(V.tensor_tensor(o, o, tmp, ALU.add))

            soft(0)
            dve.wait_ge(s["qr_full"], 3)
            soft(1)
            gather_out(0)
            soft(2)
            gather_out(1)
            dve.wait_ge(s["kx"], 4)
            dve.wait_ge(s["post"], 1)
            for c in range(2):
                V.memset(tb[:, c, :, NCMP:HKO], 0.0)
                for h in range(HKV):
                    steps_of = kx[:, c, h, :].rearrange("p (n k) -> p k n", k=8)
                    for half in range(2):
                        k8 = slice(8 * half, 8 * half + 8)
                        V.tensor_tensor(tb[:, c, k8, h * HKO:h * HKO + NCMP], steps_of[:, :, half:half + NCMP],
                                        bc(post[:, c, k8], NCMP), ALU.add).then_inc(s["tb"], 1)
            soft(3)
            gather_out(2)
            z = banks[5][:].rearrange("p (t n) -> p t n", t=NT)
            dve.wait_ge(s["absz"], 1)
            link(V.tensor_scalar(loga[:], z, 0.0, None, ALU.min))
            dve.wait_ge(s["e1"], 1)
            link(V.tensor_tensor(loga[:], loga[:], en[:], ALU.subtract))
            V.tensor_scalar(loga[:], loga[:], 1.0 / GTAU, None, ALU.mult).then_inc(s["loga"], 1)
            silu_hidden(0)
            soft(4)
            gather_out(3)
            silu_hidden(1)
            dve.wait_ge(s["bexp"], 1)
            link(V.tensor_copy(es[:], banks[6][:].rearrange("p (t n) -> p t n", t=NT)))
            V.tensor_tensor(es[:], es[:], banks[5][:].rearrange("p (t n) -> p t n", t=NT), ALU.subtract)\
                .then_inc(s["esd"], 1)
            V.tensor_tensor(kd[:], gqk[:, :, 256:512], en[:], ALU.mult)
            V.scalar_tensor_tensor(out=qd, in0=qd, scalar=SCALE, in1=eb[:], op0=ALU.mult, op1=ALU.mult)\
                .then_inc(s["qd"], 1)
            soft(5)
            gather_out(4)
            dve.wait_ge(s["es"], 1)
            V.tensor_tensor(kstate[:], gqk[:, :, 256:512], es[:], ALU.mult).then_inc(s["qd"], 1)
            soft(6)
            gather_out(5)
            for par in range(2):
                dve.wait_ge(s["at_full"], par + 1)
                V.tensor_tensor(ats[:, par].rearrange("p t h n -> p (t h) n"),
                                banks[5 + par][:].rearrange("p (a n) -> p a n", a=4),
                                tri[:].unsqueeze(1).to_broadcast([P, 4, P]), ALU.mult).then_inc(s["ats"], 1)
            dve.wait_ge(s["kc_full"], 1)
            link(V.tensor_copy(kcn[:], banks[7][0:NCW, 0:DH]))
            V.tensor_copy(vcs[:], banks[7][0:NCW, DH:2 * DH]).then_inc(s["kcn"], 1)
            link(V.tensor_tensor(kcq[:], kcn[:], kcn[:], ALU.mult))
            link(V.reduce_sum(ms_k[0:NCW, :], kcq[:], AX.X))
            V.tensor_scalar(ms_k[0:NCW, :], ms_k[0:NCW, :], 1.0 / DH, EPS, ALU.mult, ALU.add).then_inc(s["ms_k"], 1)
            dve.wait_ge(s["ms_k"], 1)
            newton("k", ms_k[0:NCW, :], rs_k[0:NCW, :], nw_k[0:NCW, :])
            V.scalar_tensor_tensor(out=kcn[:], in0=kcn[:], scalar=rs_k[0:NCW, :], in1=gk0[:],
                                   op0=ALU.mult, op1=ALU.mult).then_inc(s["kcn"], 1)
            soft(7)
            gather_out(6)
            for ci in range(3):
                dve.wait_ge(s["u_full"], ci + 1)
                if ci == 1:
                    dve.wait_ge(s["dec"], 1)
                for hp in range(2):
                    for par in range(2):
                        u = banks[5 + ci][par * 64:par * 64 + 64, hp * 256 + par * DV:hp * 256 + par * DV + DV]
                        dst = sta[par * 64:par * 64 + 64, hp, :, :]
                        if ci == 0:
                            last = V.tensor_copy(dst[:, 0, :], u)
                        else:
                            last = V.scalar_tensor_tensor(out=dst[:, ci, :], in0=dst[:, ci - 1, :],
                                                          scalar=dect[par * 64:par * 64 + 64, hp, ci:ci + 1], in1=u,
                                                          op0=ALU.mult, op1=ALU.add)
                last.then_inc(s["sta"], 1)
                dve.wait_ge(s["sta"], ci + 1)
            gather_out(7)
            dve.wait_ge(s["sgr"], 1)
            link(V.tensor_tensor(gr[:], gr[:], sgr[:], ALU.mult))
            for ti in range(NT):
                for par in range(2):
                    dve.wait_ge(s["o_full"], 2 * ti + par + 1)
                    V.tensor_copy(go[:, ti, :].rearrange("p (h r d) -> p h r d", h=2, r=2)[:, :, par, :],
                                  banks[O_BANKS[ti][par]][:, 0:2 * DV].rearrange("p (h d) -> p h d", h=2))\
                        .then_inc(s["go"], 1)
            dve.wait_ge(s["go"], 2 * NT)
            link(V.tensor_tensor(gsq[:], go[:], go[:], ALU.mult))
            link(V.tensor_reduce(ms_g, gsq[:].rearrange("p t (h d) -> p t h d", h=GH), AX.X, ALU.add))
            V.tensor_scalar(ms_g, ms_g, 1.0 / DV, EPS, ALU.mult, ALU.add).then_inc(s["ms_g"], 1)
            dve.wait_ge(s["ms_g"], 1)
            newton("g", ms_g, rs_g, nw_g)
            go4 = go[:].rearrange("p t (h d) -> p (t h) d", h=GH)
            link(V.tensor_tensor(go4, go4, bc(rs_g.rearrange("p t h -> p (t h)"), DV), ALU.mult))
            link(V.tensor_tensor(go4, go4, glag[:].unsqueeze(1).to_broadcast([P, NT * GH, DV]), ALU.mult))
            V.tensor_tensor(go[:], go[:], gr[:], ALU.mult).then_inc(s["glaout"], 1)
            link(V.memset(pcs[:], 0.0))
            dve.wait_ge(s["cs_full"], 2)
            for h in range(HKV):
                v = pcs[:, :, :, h * HKO:h * HKO + NCMP]
                for ti in range(NT):
                    V.tensor_tensor(v[:, ti], banks[6 + h][:, ti * 64:ti * 64 + G * NCMP]
                                    .rearrange("p (g n) -> p g n", g=G),
                                    mcneg[:, ti, :].unsqueeze(1).to_broadcast([P, G, NCMP]), ALU.add)\
                        .then_inc(s["csc"], 1)
            dve.wait_ge(s["csc"], 4)
            for h in range(HKV):
                v = pcs[:, :, :, h * HKO:h * HKO + NCMP]
                cm = cmax.rearrange("p t (h g) -> p t h g", h=HKV)[:, :, h, :]
                link(V.tensor_reduce(cm, v, AX.X, ALU.max))
                last = V.tensor_tensor(v, v, bc(cm, NCMP), ALU.subtract)
            last.then_inc(s["csub"], 1)
            for h in range(HKV):
                dve.wait_ge(s["cexp"], h + 1)
                v = pcs[:, :, :, h * HKO:h * HKO + NCMP]
                cd = cden.rearrange("p t (h g) -> p t h g", h=HKV)[:, :, h, :]
                for ti in range(NT):
                    last = V.tensor_tensor(v[:, ti], v[:, ti],
                                           mc01[:, ti, :].unsqueeze(1).to_broadcast([P, G, NCMP]), ALU.mult)
                last.then_inc(s["pc"], 1)
                dve.wait_ge(s["pc"], h + 1)
                link(V.tensor_reduce(cd, v, AX.X, ALU.add))
            link(V.tensor_scalar(cden, cden, 0.5, None, ALU.max))
            link(V.reciprocal(cden, cden))
            link(V.tensor_tensor(cden, cden, gates[:, :, :, 0], ALU.mult))
            for h in range(HKV):
                dve.wait_ge(s["oc_full"], h + 1)
                if h:
                    dve.wait_ge(s["osum_c"], NT * h)
                for ti in range(NT):
                    V.tensor_tensor(otmp2[:, ti].rearrange("p (g d) -> p g d", g=G),
                                    banks[4 + h][:, ti * 256:(ti + 1) * 256].rearrange("p (g d) -> p g d", g=G),
                                    bc(cden[:, ti, h * G:(h + 1) * G], DH), ALU.mult).then_inc(s["oc_read"], 1)
                dve.wait_ge(s["oc_read"], NT * (h + 1))
                for ti in range(NT):
                    o = osum[:, ti, h * G:(h + 1) * G, :]
                    V.tensor_tensor(o, o, otmp2[:, ti].rearrange("p (g d) -> p g d", g=G), ALU.add)\
                        .then_inc(s["osum_c"], 1)
            dve.wait_ge(s["g2"], 16)
            for q in range(4):
                m, ti = q // 2, q % 2
                dve.wait_ge(s["sqy"], q + 1)
                cols = slice(512 * m, 512 * (m + 1))
                V.tensor_tensor(h2[:, ti, cols], banks[2 * ti + m][:], g2b[:, cols], ALU.mult).then_inc(s["h2"], 1)
            link(V.tensor_tensor(ms_y, ms2[:, :, 0], ms2[:, :, 1], ALU.add))
            V.tensor_scalar(ms_y, ms_y, 1.0 / D, EPS, ALU.mult, ALU.add).then_inc(s["ms_y"], 1)
            dve.wait_ge(s["ms_y"], 1)
            dve.wait_ge(s["h2"], 4)
            V.memset(token[:, 3:4], 0.0).then_inc(s["unit_free"], RING * NU)
            newton("y", ms_y, rs_y, nw_y, s["rs_fine"])

            def rows_low(ti):
                dve.wait_ge(s["h2hi"], ti + 1)
                V.scalar_tensor_tensor(out=h2s[:, ti, 1, :], in0=h2[:, ti, :], scalar=rs_y[:, ti:ti + 1],
                                       in1=h2s[:, ti, 0, :].bitcast(F32), op0=ALU.mult, op1=ALU.subtract)\
                    .then_inc(s["h2s"], 1)

            rows_low(0)
            dve.wait_ge(s["rt_full"], 1)
            V.memset(lg[:, :, E:], FILLER)
            for ti in range(NT):
                last = V.scalar_tensor_tensor(out=lg[:, ti, 0:E], in0=banks[5][:, ti * E:(ti + 1) * E],
                                              scalar=rs_y[:, ti:ti + 1], in1=brt[:], op0=ALU.mult, op1=ALU.add)
            link(last)
            for ti in range(NT):
                link(V.max(top[:, ti, :], lg[:, ti, 0:E]))
            link(V.tensor_scalar(ntop, top[:, :, 0], -1.0, None, ALU.mult))
            V.tensor_tensor(lgr, lg[:, :, 0:E], bc(ntop, E), ALU.add).then_inc(s["ntop"], 1)
            link(V.memset(top[:, :, TOPK:8], FILLER))
            for ti in range(NT):
                link(V.match_replace(lgm[:, ti, :], top[:, ti, :], lg[:, ti, :], -FILLER))
            V.tensor_tensor(msk, lgm[:, :, 0:E], lg[:, :, 0:E], ALU.not_equal).then_inc(s["msk"], 1)
            dve.wait_ge(s["msk"], 1)
            dve.wait_ge(s["gexp"], 1)
            link(V.tensor_tensor(gate, gate, msk, ALU.mult))
            link(V.tensor_reduce(gsum, gate, AX.X, ALU.add))
            link(V.reciprocal(gsum, gsum))
            V.tensor_tensor(gate, gate, bc(gsum, E), ALU.mult).then_inc(s["gate"], 1)
            dve.wait_ge(s["gate"], 1)
            V.memset(gates4[:, :, ROUNDS * E:], 0.0)
            for r in range(ROUNDS):
                V.tensor_copy(gates4[:, :, r * E:(r + 1) * E], gate)
            rows_low(1)
            dve.wait_ge(s["pos_full"], 1)
            V.memset(posm[:, :, ROUNDS * E:], -1.0)
            link(V.scalar_tensor_tensor(out=lgr, in0=banks[6][:, 0:NT * E].rearrange("p (t e) -> p t e", t=NT),
                                        scalar=1.0, in1=msk, op0=ALU.add, op1=ALU.mult))
            link(V.tensor_scalar(posm[:, :, 0:E], lgr, -1.0, None, ALU.add))
            link(V.reduce_max(rounds_f[:, 0:1], banks[7][:, 0:E], AX.X))
            dve.wait_ge(s["bias"], 1)
            V.memset(token[:, 2:3], 0.0).then_inc(s["x_free"], 1)
            one_hot(0)
            for r in range(1, ROUNDS):
                link(V.tensor_scalar(posm[:, :, r * E:(r + 1) * E], lgr, -1.0 - CAP * r, None, ALU.add))
            for r in range(1, ROUNDS):
                link(V.tensor_scalar(rounds_f[:, r:r + 1], rounds_f[:, 0:1], float(CAP * r), float(E), ALU.is_gt, ALU.mult))
            link(V.reduce_sum(rounds_f[:, 0:1], rounds_f[:, 1:ROUNDS], AX.X))
            V.tensor_scalar(rounds_i[:], rounds_f[:, 0:1], float(E - 1), None, ALU.add).then_inc(s["rounds"], 1)

            def split_low(it, j, first=0, end=NV):
                for q, ks in list(enumerate(UNITS))[first:end]:
                    dve.wait_ge(s["wh"], it * (PIECES * NU) + j * NU + q + 1)
                    V.tensor_tensor(wl[:, j % RING, ks[0]:ks[-1] + 1, :], slot(NF + j, 512)[:, ks[0]:ks[-1] + 1, :],
                                    wh[:, j % RING, ks[0]:ks[-1] + 1, :].bitcast(F32), ALU.subtract)\
                        .then_inc(s["wl"], 1)

            def down_low(it, m):
                dve.wait_ge(s["yh"], it * 2 + m + 1)
                V.scalar_tensor_tensor(out=yl[:, 512 * m:512 * (m + 1)], in0=banks[4 + m][:], scalar=gslot[:],
                                       in1=yh[:, 512 * m:512 * (m + 1)].bitcast(F32),
                                       op0=ALU.mult, op1=ALU.subtract).then_inc(s["yl"], 1)

            def swiglu(it, hf):
                dve.wait_ge(s["merged"], it * 4 + 2 * hf + 4)
                bias = bias_t[:].rearrange("p (a b c) e -> p b a c e", a=2, b=2)[:, hf, :, :, bass.ds(it % E, 1)]
                V.tensor_tensor(hb[:], t_bank[:].rearrange("p (a c n) -> p a c n", a=2, c=4),
                                bias.to_broadcast([P, 2, 4, CAP]), ALU.add).then_inc(s["t_free"], 1)
                dve.wait_ge(s["t_free"], it * 2 + hf + 2)
                V.tensor_scalar(hb[:, 0], hb[:, 0], LIMIT, None, ALU.min).then_inc(s["hb"], 1)
                V.tensor_scalar(hb[:, 1], hb[:, 1], LIMIT, -LIMIT, ALU.min, ALU.max).then_inc(s["loopdve"], 1)
                dve.wait_ge(s["hb"], it * 2 + hf + 1)
                dve.wait_ge(s["loopdve"], it * 4 + 2 * hf + 1)
                V.scalar_tensor_tensor(out=hb[:, 1], in0=hb[:, 1], scalar=1.0, in1=hb[:, 0],
                                       op0=ALU.add, op1=ALU.mult).then_inc(s["loopdve"], 1)
                dve.wait_ge(s["loopdve"], it * 4 + 2 * hf + 2)
                dve.wait_ge(s["sigm"], it * 2 + hf + 1)
                V.tensor_tensor(actf[:], hb[:, 1], sig[:], ALU.mult).then_inc(s["actf"], 1)
                dve.wait_ge(s["ahi"], it * 2 + hf + 1)
                V.tensor_tensor(a_hl[:, 4 * hf:4 * hf + 4, CAP:], actf[:],
                                a_hl[:, 4 * hf:4 * hf + 4, 0:CAP].bitcast(F32), ALU.subtract).then_inc(s["a_hl"], 1)

            def body(it, last):
                dve.wait_ge(s["xfill"], it * 3 + 2)
                if not last:
                    one_hot(it + 1)
                V.tensor_tensor(pgr[:], slots_of(2), place_of(posm, it, 1, 1), ALU.is_equal).then_inc(s["pgr"], 1)
                dve.wait_ge(s["pgr"], it + 1)
                V.tensor_tensor(pgw[:], pgr[:], place_of(gates4, it, 1, 1), ALU.mult).then_inc(s["pgw"], 1)
                split_low(it, 2)
                split_low(it, 3)
                swiglu(it, 0)
                split_low(it, 4)
                swiglu(it, 1)
                split_low(it, 5)
                if not last:
                    split_low(it + 1, 0, 0, 2)
                down_low(it, 0)
                if not last:
                    split_low(it + 1, 0, 2)
                    split_low(it + 1, 1)
                down_low(it, 1)

            V.memset(token[:, 0:1], 0.0).then_inc(s["merged"], 2)
            V.memset(token[:, 1:2], 0.0).then_inc(s["t_free"], 1)
            dve.wait_ge(s["h2s"], NT)
            split_low(0, 0)
            V.tensor_scalar(pgt[:], ones[:].unsqueeze(1).to_broadcast([P, NT, P]), 0.0, None, ALU.mult)
            V.tensor_scalar(yh[:], ones[:].unsqueeze(1).to_broadcast([P, DK, P]), 0.0, None, ALU.mult)
            V.tensor_scalar(yl[:], ones[:].unsqueeze(1).to_broadcast([P, DK, P]), 0.0, None, ALU.mult)\
                .then_inc(s["yl"], 2)
            split_low(0, 1)
            dve.wait_ge(s["rounds"], 1)
            last_step = dve.value_load(rounds_i[0:1, 0:1], min_val=E - 1, max_val=ROUNDS * E - 1)
            with dve.Fori(0, last_step) as it:
                body(it, False)
            body(last_step, True)
            for ti in range(NT):
                dve.wait_ge(s["comb"], last_step * NT + NT + ti + 1)
                for m in range(2):
                    V.tensor_copy(yout[:, ti, 512 * m:512 * (m + 1)], banks[2 * ti + m][:]).then_inc(s["yout"], 1)

        @block.tensor
        def _(pe):
            mm, tp = nc.tensor.matmul, nc.tensor.transpose
            pe.wait_ge(s["const"], 2)
            for ti in range(NT):
                pe.wait_ge(s["xn"], ti + 1)
                for half in range(2):
                    for k in range(4):
                        c = 4 * half + k
                        last = tp(banks[2 * ti + half][:, k * P:(k + 1) * P], xn[:, ti, c * P:(c + 1) * P], ident[:])
                    last.then_inc(s["xt_full"], 1)
            pe.wait_ge(s["xt"], 4)
            def pair(ti, g):
                return rr[:, ti, HKV * g:HKV * (g + 1), :]

            def project(first, end):
                n = 0
                for name, c0, width in PROJ:
                    piece = next(i for i, (a, b) in enumerate(IN_PIECES) if a <= c0 < b)
                    off = c0 - IN_PIECES[piece][0]
                    for ti in range(NT):
                        if first <= n < end:
                            front_arrived(pe, piece)
                            before = [m for m in range(n) if PROJ_BANKS[m] == PROJ_BANKS[n]]
                            if before:
                                pe.wait_ge(s["proj"], before[-1] + 1)
                            for k in range(DK):
                                last = mm(banks[PROJ_BANKS[n]][:, 0:width], xt[:, k, ti * P:(ti + 1) * P],
                                          front_slot(piece)[:, k, off:off + width], start=k == 0, stop=k == DK - 1)
                            last.then_inc(s["proj_full"], 1)
                        n += 1

            def hidden(c):
                i = len(IN_PIECES) + c
                front_arrived(pe, i)
                pe.wait_ge(s["tb"], 4 * (c + 1))
                for k in range(16):
                    last = mm(banks[6 + c][0:NCW, 0:HID], tb[:, c, k, :], comp_slot(i)[:, k, :], start=k == 0, stop=k == 15)
                last.then_inc(s["h_full"], 1)

            def scores(i):
                br, ti, h = GROUPS[i]
                keys = P * (ti + 1)
                if i:
                    pe.wait_ge(s["nmax"], i)
                per = 512 // keys
                for g in range(G):
                    last = mm(banks[g // per][:, (g % per) * keys:(g % per + 1) * keys],
                              qrt[h * DH:(h + 1) * DH, g, ti * P:(ti + 1) * P],
                              kst[h * DH:(h + 1) * DH, br, 0:keys], start=True, stop=True)
                last.then_inc(s["sc_full"], 1)

            def values(i):
                br, ti, h = GROUPS[i]
                n = ti + 1
                if i:
                    pe.wait_ge(s["pts"], i)
                for g in range(G):
                    pe.wait_ge(s["pexp"], G * i + g + 1)
                    for k in range(n):
                        u = g * n + k
                        last = tp(banks[PT_BANKS[u // 4]][:, (u % 4) * P:(u % 4 + 1) * P],
                                  pb[:, i % 2, (g * n + k) * P:(g * n + k + 1) * P], ident[:])
                last.then_inc(s["pt_full"], 1)
                if i:
                    pe.wait_ge(s["pv_read"], i)
                pe.wait_ge(s["pts"], i + 1)
                for g in range(G):
                    for k in range(n):
                        u = g * n + k
                        last = mm(banks[4][:, g * DH:(g + 1) * DH], pt[:, (i + 1) % 2, u * P:(u + 1) * P],
                                  kv[:, k, 256 + 128 * br + h * DH:256 + 128 * br + (h + 1) * DH],
                                  start=k == 0, stop=k == n - 1)
                last.then_inc(s["pv_full"], 1)

            project(0, 8)
            for ti in range(NT):
                pe.wait_ge(s["rn"], ti + 1)
                for g in range(G):
                    last = tp(banks[2 + ti][:, g * P:(g + 1) * P], pair(ti, g), ident[:])
                last.then_inc(s["qt_full"], 1)
            for ti in range(NT):
                pe.wait_ge(s["qr_ready"], 2 * (ti + 1))
                for g in range(G):
                    last = tp(banks[ti][:, g * P:(g + 1) * P], pair(ti, g), ident[:])
                last.then_inc(s["qr_full"], 1)
            pe.wait_ge(s["proj"], 5)
            for br in range(2):
                for ti in range(NT):
                    last = tp(banks[4][:, (2 * br + ti) * P:(2 * br + ti + 1) * P],
                              rr[:, ti, HQ + 2 * br:HQ + 2 * br + 2, :], ident[:])
            last.then_inc(s["qr_full"], 1)
            pe.wait_ge(s["qt"], 2)
            pe.wait_ge(s["qrt"], 3)
            scores(0)
            project(8, 10)
            scores(1)
            values(0)
            project(10, 13)
            scores(2)
            values(1)
            project(13, 14)
            pe.wait_ge(s["proj"], 12)
            for c in range(2):
                for ti in range(NT):
                    last = tp(banks[5][:, (2 * c + ti) * P:(2 * c + ti + 1) * P], kv[:, ti, c * P:(c + 1) * P], ident[:])
            last.then_inc(s["kx_full"], 1)
            pe.wait_ge(s["proj"], 13)
            pe.wait_ge(s["small"], 16 * N_SMALL)
            for c in range(2):
                last = tp(banks[6][:, 16 * c:16 * c + 16], posl[:, c, :], ident[0:16, 0:16])
            last.then_inc(s["post_full"], 1)

            scores(3)
            values(2)
            pe.wait_ge(s["proj"], 14)
            for ti in range(NT):
                last = tp(banks[7][0:16, ti * P:(ti + 1) * P], glr[:, ti, :], ident[:])
            last.then_inc(s["glrt_full"], 1)
            pe.wait_ge(s["glrt"], 1)
            pe.wait_ge(s["kx"], 4)
            for ti in range(NT):
                last = mm(banks[5][:, ti * 256:(ti + 1) * 256], glrt[:, ti * P:(ti + 1) * P], wgate[:], start=True, stop=True)
            last.then_inc(s["z_full"], 1)
            pe.wait_ge(s["post"], 1)
            hidden(0)
            scores(4)
            values(3)
            hidden(1)
            pe.wait_ge(s["loga"], 1)
            pe.wait_ge(s["const"], N_CONST)
            pe.wait_ge(s["hid"], 1)
            for ti in range(NT):
                mm(banks[5][:, ti * 256:(ti + 1) * 256], tri[:], loga[:, ti, :], start=True, stop=True)
                last = mm(banks[6][:, ti * 256:(ti + 1) * 256], blk[:], loga[:, ti, :], start=True, stop=True)
            last.then_inc(s["b_full"], 1)
            scores(5)
            values(4)
            pe.wait_ge(s["hid"], 2)
            for ti in range(NT):
                for hp in range(2):
                    last = mm(banks[7][:, hp * 4 + ti * 2:hp * 4 + ti * 2 + 2], loga[:, ti, hp * P:(hp + 1) * P],
                              blk[:, 0:P:CH], start=True, stop=True)
            last.then_inc(s["dec_full"], 1)
            pe.wait_ge(s["qd"], 1)
            for src, b in ((qd, banks[5]), (kd, banks[6])):
                for hp in range(2):
                    for ti in range(NT):
                        last = tp(b[:, hp * S + ti * P:hp * S + (ti + 1) * P], src[:, ti, hp * P:(hp + 1) * P], ident[:])
                last.then_inc(s["qdt_full"], 1)
            pe.wait_ge(s["hid"], 2)
            pe.wait_ge(s["dec"], 1)
            for c in range(2):
                for k in range(2):
                    last = tp(banks[7][:, (2 * c + k) * NCW:(2 * c + k + 1) * NCW], hid[:, c, k * P:(k + 1) * P],
                              ident[0:NCW, 0:NCW])
            last.then_inc(s["ht_full"], 1)
            scores(6)
            values(5)
            pe.wait_ge(s["qdt"], 2)
            for par in range(2):
                for ti in range(NT):
                    for hp in range(2):
                        last = mm(banks[5 + par][:, (2 * ti + hp) * P:(2 * ti + hp + 1) * P],
                                  kdt[par * 64:par * 64 + 64, hp, ti * P:(ti + 1) * P],
                                  qdt[par * 64:par * 64 + 64, hp, ti * P:(ti + 1) * P], start=True, stop=True)
                last.then_inc(s["at_full"], 1)
            pe.wait_ge(s["hidt"], 1)
            for c in range(2):
                for k in range(2):
                    last = mm(banks[7][0:NCW, c * DH:(c + 1) * DH], hidt[:, c, k, :], w2[:, c, k, :], start=k == 0, stop=k == 1)
            last.then_inc(s["kc_full"], 1)
            scores(7)
            values(6)
            pe.wait_ge(s["kcn"], 2)
            tp(banks[7][0:DH, 0:NCW], kcn[:], ident[0:NCW, 0:NCW]).then_inc(s["kct_full"], 1)
            pe.wait_ge(s["qd"], 2)
            for ci in range(3):
                ti, r = ci // 2, 64 * (ci % 2)
                if ci < 2:
                    pe.wait_ge(s["ats"], ci + 1)
                else:
                    pe.wait_ge(s["kct"], 1)
                for hp in range(2):
                    last = mm(banks[5 + ci][:, hp * 256:(hp + 1) * 256], kstate[r:r + 64, ti, hp * P:(hp + 1) * P],
                              gv[r:r + 64, ti, hp * 256:(hp + 1) * 256], start=True, stop=True)
                last.then_inc(s["u_full"], 1)
            values(7)
            pe.wait_ge(s["sta"], 3)
            for ti in range(NT):
                for par in range(2):
                    pe.wait_ge(s["ats"], par + 1)
                    b = banks[O_BANKS[ti][par]]
                    if ti and par:
                        pe.wait_ge(s["go"], 1)
                    for hp in range(2):
                        h = 2 * hp + par
                        last = mm(b[:, hp * DV:(hp + 1) * DV], ats[:, par, ti, hp, :], gv[:, ti, h * DV:(h + 1) * DV],
                                  start=True, stop=True)
                        for j in range(2):
                            ci = 2 * ti + j
                            if ci:
                                last = mm(b[64 * j:64 * j + 64, hp * DV:(hp + 1) * DV],
                                          qdt[par * 64:par * 64 + 64, hp, ti * P + 64 * j:ti * P + 64 * j + 64],
                                          sta[par * 64:par * 64 + 64, hp, ci - 1, :], start=False, stop=True,
                                          skip_group_check=True)
                    last.then_inc(s["o_full"], 1)
            pe.wait_ge(s["kct"], 1)
            for h in range(HKV):
                pe.wait_ge(s["go"], h + 2)
                for ti in range(NT):
                    for g in range(G):
                        last = mm(banks[6 + h][:, ti * 64 + g * NCMP:ti * 64 + (g + 1) * NCMP],
                                  qt[h * DH:(h + 1) * DH, g, ti * P:(ti + 1) * P], kct[h * DH:(h + 1) * DH, :],
                                  start=True, stop=True)
                last.then_inc(s["cs_full"], 1)
            pe.wait_ge(s["nmax"], 8)
            pe.wait_ge(s["pts"], 8)
            for ti in range(NT):
                for m in range(2):
                    mm(banks[2 * ti + m][:], ident[:], xr[:, ti, 512 * m:512 * (m + 1)], start=True, stop=True)

            def to_project(q, count):
                for kk in range(2):
                    for ti in range(NT):
                        k = 2 * q + kk
                        src = osum[:, ti, 2 * k:2 * k + 2, :] if k < 4 else go[:, ti, (k - 4) * P:(k - 3) * P]
                        last = tp(banks[4 + count][:, kk * S + ti * P:kk * S + (ti + 1) * P], src, ident[:])
                last.then_inc(s["ot_full"], 1)

            def project_out(q, first, end):
                m, ti = q // 2, q % 2
                i = len(IN_PIECES) + 2 + m
                front_arrived(pe, i)
                for k in range(first, end):
                    last = mm(banks[2 * ti + m][:], ot[:, k, ti * P:(ti + 1) * P], front_slot(i)[:, k, :],
                              start=False, stop=True, skip_group_check=True)
                if first == 0:
                    last.then_inc(s["wo_full"], 1)

            pe.wait_ge(s["glaout"], 1)
            pe.wait_ge(s["pv_read"], 8)
            to_project(2, 0)
            to_project(3, 1)
            pe.wait_ge(s["ot"], 2)
            project_out(0, 4, DK)
            pe.wait_ge(s["pc"], 2)
            for ti in range(NT):
                for g in range(G):
                    last = tp(banks[6 + ti][0:DH, g * P:(g + 1) * P], pcs[:, ti, g, :], ident[:])
                last.then_inc(s["pct_full"], 1)
            project_out(1, 4, DK)
            pe.wait_ge(s["pct"], 2)
            for h in range(HKV):
                for ti in range(NT):
                    for g in range(G):
                        o = ti * 512 + g * P
                        last = mm(banks[4 + h][:, ti * 256 + g * DH:ti * 256 + (g + 1) * DH],
                                  pt[h * HKO:h * HKO + NCMP, 0, o:o + P], vcs[h * HKO:h * HKO + NCMP, :],
                                  start=True, stop=True)
                last.then_inc(s["oc_full"], 1)
            project_out(2, 4, DK)
            project_out(3, 4, DK)
            pe.wait_ge(s["osum_c"], 4)
            to_project(0, 2)
            to_project(1, 3)
            pe.wait_ge(s["ot"], 4)

            def h2_transposed(q):
                m, ti = q // 2, q % 2
                pe.wait_ge(s["h2"], q + 1)
                for c in range(4):
                    last = tp(banks[4 + q][:, c * P:(c + 1) * P], h2[:, ti, 512 * m + c * P:512 * m + (c + 1) * P],
                              ident[:])
                last.then_inc(s["h2t_full"], 1)

            project_out(0, 0, 4)
            project_out(1, 0, 4)
            h2_transposed(0)
            project_out(2, 0, 4)
            h2_transposed(1)
            project_out(3, 0, 4)
            h2_transposed(2)
            pe.wait_ge(s["brow"], 16)
            pe.wait_ge(s["h2t"], 1)
            for k in range(2 * FF // P):
                last = tp(banks[4][:, k * E:(k + 1) * E], brow[:, k * P:(k + 1) * P], ident[0:E, 0:E])
            last.then_inc(s["bias_full"], 1)
            h2_transposed(3)
            for ti in range(NT):
                pe.wait_ge(s["h2t"], 3 + ti)
                for k in range(DK):
                    last = mm(banks[5][:, ti * E:(ti + 1) * E], h2t[:, k, ti * P:(ti + 1) * P], wrt[:, k, :],
                              start=k == 0, stop=k == DK - 1)
            last.then_inc(s["rt_full"], 1)
            pe.wait_ge(s["msk"], 1)
            mm(banks[6][:, 0:E], stri[:], msk[:, 0, :], start=True, stop=True)
            mm(banks[6][:, E:2 * E], stri[:], msk[:, 1, :], start=True, stop=False)
            mm(banks[6][:, E:2 * E], ones[:], msk[:, 0, :], start=False, stop=True)
            mm(banks[7][:, 0:E], ones[:], msk[:, 0, :], start=True, stop=False)
            mm(banks[7][:, 0:E], ones[:], msk[:, 1, :], start=False, stop=True).then_inc(s["pos_full"], 1)
            def gated_bias(ti):
                for m in range(2):
                    mm(banks[2 * ti + m][:], gtt[:, ti * P:(ti + 1) * P], bdn[:, 512 * m:512 * (m + 1)],
                       start=False, stop=True, skip_group_check=True)

            def gather(fill, hots, half, bank=x_bank):
                if bank is x_bank:
                    pe.wait_ge(s["x_free"], fill)
                pe.wait_ge(s["onehot"], hots)
                for c in range(4):
                    k = 4 * half + c
                    for hl in range(2):
                        for ti in range(NT):
                            last = mm(bank[:, c * P + hl * CAP:c * P + (hl + 1) * CAP],
                                      h2s[:, ti, hl, k * P:(k + 1) * P], onehot[:, ti, :],
                                      start=ti == 0, stop=ti == NT - 1)
                last.then_inc(s["xfill"], 1)

            def block_products(it, j, lhs, first=0, end=NU):
                bank = banks[4 + j % 2][:]
                if j < 2:
                    pe.wait_ge(s["yl"], it * 2 + j + 1)
                elif first == 0:
                    pe.wait_ge(s["gu"], it * 4 + j - 1)
                pe.wait_ge(s[f"stage{expert_slot(j)}"], it * 16 + 16 * (front_loads(j) + 1))
                w = slot(NF + j, 512)

                for q, ks in list(enumerate(UNITS))[first:end]:
                    if lhs is a_hl and q in (0, 2):
                        pe.wait_ge(s["a_hl"], it * 2 + 1 + q // 2)
                    if q < NV:
                        pe.wait_ge(s["wl"], it * (PIECES * NV) + j * NV + q + 1)
                    else:
                        pe.wait_ge(s["wl_pool"], it * PIECES + j + 1)
                    for k in ks:
                        mm(bank, lhs[:, k, :], wh[:, j % RING, k, :], start=k == 0, stop=False)
                        last = mm(bank, lhs[:, k, :], wl[:, j % RING, k, :], start=False, stop=False)
                    last.then_inc(s["unit_free"], 1)
                if end < NU:
                    return
                for k in range(SPLIT, DK):
                    last = mm(bank, lhs[:, k, :].bitcast(F32), w[:, k, :], start=False, stop=k == DK - 1)
                last.then_inc(s["block_full"], 1)

            def merge(it, n):
                pe.wait_ge(s["gu"], it * 4 + n + 1)
                if n % 2 == 0:
                    pe.wait_ge(s["t_free"], it * 2 + n // 2 + 1)
                for c in range(4):
                    o = ((n % 2) * 4 + c) * CAP
                    last = mm(t_bank[:, o:o + CAP], gu[:, n % 2, c * P:(c + 1) * P], stack_i[:], start=True, stop=True)
                last.then_inc(s["merged"], 1)

            def combine(it, ti):
                pe.wait_ge(s["yl"], it * 2 + 2)
                for m in range(2):
                    for part in (yh, yl):
                        last = mm(banks[2 * ti + m][:], pgt[:, ti * P:(ti + 1) * P],
                                  part[:, 512 * m:512 * (m + 1)], start=False, stop=True, skip_group_check=True)
                last.then_inc(s["comb"], 1)

            def slots(it, fill):
                pe.wait_ge(s["x_free"], fill)
                pe.wait_ge(s["pgw"], it + 1)
                for ti in range(NT):
                    tp(x_bank[:, ti * P:(ti + 1) * P], pgr[:, ti].rearrange("p a n -> p (a n)"), ident[:])
                for ti in range(NT):
                    last = mm(x_bank[:, S:S + 1], pgw[:, ti].rearrange("p a n -> p (a n)"), ones[:, 0:1],
                              start=ti == 0, stop=ti == NT - 1)
                last.then_inc(s["xfill"], 1)

            def body(it, last):
                block_products(it, 1, xs)
                merge(it, 0)
                block_products(it, 2, xs)
                merge(it, 1)
                if not last:
                    gather(it * 3 + 3, it + 2, 0)
                block_products(it, 3, xs, 0, 2)
                merge(it, 2)
                block_products(it, 3, xs, 2)
                combine(it, 0)
                merge(it, 3)
                combine(it, 1)
                block_products(it, 4, a_hl, 0, 2)
                if not last:
                    gather(it * 3 + 4, it + 2, 1)
                block_products(it, 4, a_hl, 2)
                slots(it, it * 3 + (3 if last else 5))
                block_products(it, 5, a_hl)
                if not last:
                    pe.wait_ge(s["x_free"], it * 3 + 6)
                    block_products(it + 1, 0, xs)

            gather(1, 1, 0)
            gather(2, 1, 1, t_bank)
            pe.wait_ge(s["gate"], 1)
            for ti in range(NT):
                last = tp(banks[5][0:E, 256 + ti * P:256 + (ti + 1) * P], gate[:, ti, :], ident[:])
            last.then_inc(s["gt_full"], 1)
            pe.wait_ge(s["bias"], 1)
            pe.wait_ge(s["x_free"], 3)
            block_products(0, 0, xs)
            pe.wait_ge(s["gtt"], 1)
            pe.wait_ge(s["bdn"], 16)
            pe.wait_ge(s["h2"], 4)
            pe.wait_ge(s["sqy"], 4)
            gated_bias(0)
            gated_bias(1)
            pe.wait_ge(s["rounds"], 1)
            last_step = pe.value_load(rounds_i[0:1, 0:1], min_val=E - 1, max_val=ROUNDS * E - 1)
            with pe.Fori(0, last_step) as it:
                body(it, False)
            body(last_step, True)
            for ti in range(NT):
                combine(last_step + 1, ti)


def kernel(x, positions, norm1_g, w_in, nsa_q_norm_g, nsa_k_norm_g, cmp_pos_k, cmp_w1_k, cmp_w2_k,
           cmp_pos_v, cmp_w1_v, cmp_w2_v, gla_w_gate, gla_b_gate, gla_norm_g, w_out, norm2_g,
           w_router, b_router, w_gate_up, b_gate_up, w_down, b_down):
    import concourse.bacc as bacc
    from concourse.bass_utils import run_bass_kernel_spmd

    inputs = {
        "x": x, "positions": positions, "norm1_g": norm1_g, "w_in": w_in, "nsa_q_norm_g": nsa_q_norm_g,
        "nsa_k_norm_g": nsa_k_norm_g, "cmp_pos_k": cmp_pos_k, "cmp_w1_k": cmp_w1_k, "cmp_w2_k": cmp_w2_k,
        "cmp_pos_v": cmp_pos_v, "cmp_w1_v": cmp_w1_v, "cmp_w2_v": cmp_w2_v, "gla_w_gate": gla_w_gate,
        "gla_b_gate": gla_b_gate, "gla_norm_g": gla_norm_g, "w_out": w_out, "norm2_g": norm2_g,
        "w_router": w_router, "b_router": b_router, "w_gate_up": w_gate_up, "b_gate_up": b_gate_up,
        "w_down": w_down, "b_down": b_down,
    }
    nc = bacc.Bacc("TRN2", target_bir_lowering=False, num_devices=1)
    arrays = {f"in_{n}": np.ascontiguousarray(a) for n, a in inputs.items()}
    aps = [nc.dram_tensor(n, a.shape, mybir.dt.from_np(a.dtype), kind="ExternalInput").ap() for n, a in arrays.items()]
    y = nc.dram_tensor("y", (1, S, D), F32, kind="ExternalOutput").ap()
    decoder_layer(nc, *aps, y)
    result = run_bass_kernel_spmd(nc, [arrays], core_ids=[0])
    return result.results[0]["y"]
```
